# Optimizing a Trainium2 kernel written in Bass

```python
import jax, jax.numpy as jnp
from jax import lax
import numpy as np

D_MODEL = 1024
BATCH = 1
SEQ = 1024
DEPTH = 1

CHUNK = 64
Q_BLOCK = 128
PLE_DIM = 256
DEEPNORM_ALPHA = (2 * DEPTH) ** 0.25
DEEPNORM_BETA = (8 * DEPTH) ** -0.25
LN_EPS = 1e-5
RMS_EPS = 1e-6

MIX_WIDTH = D_MODEL
HEAD_DIM = 64
POOL_WIDTH = MIX_WIDTH // 4
POOL_GROUPS = 4
POOL_GROUP_DIM = POOL_WIDTH // POOL_GROUPS
POOL_WINDOWS = (2, 4, 8, 16)
SSD_WIDTH = 3 * MIX_WIDTH // 8
SSD_HEADS = SSD_WIDTH // HEAD_DIM
SSD_GROUPS = 2
SSD_STATE = 128
SSD_CONV = 4
SSD_XBC_WIDTH = SSD_WIDTH + 2 * SSD_GROUPS * SSD_STATE
SB_WIDTH = MIX_WIDTH - POOL_WIDTH - SSD_WIDTH
SB_HEADS = SB_WIDTH // HEAD_DIM

COL_POOL = 0
COL_Z = COL_POOL + POOL_WIDTH
COL_XBC = COL_Z + SSD_WIDTH
COL_DT = COL_XBC + SSD_XBC_WIDTH
COL_Q = COL_DT + SSD_HEADS
COL_K = COL_Q + SB_WIDTH
COL_V = COL_K + SB_WIDTH
IN_COLS = COL_V + SB_WIDTH

D_FF = ((8 * D_MODEL // 3 + 255) // 256) * 256
FFN_CONV = 3

kernel_name = 'hybrid_pool_ssd_stickbreak_deepnorm_trunk'

def layer_norm(x, g, b):
    xf = x.astype(jnp.float32)
    mu = jnp.mean(xf, axis=-1, keepdims=True)
    var = jnp.mean(jnp.square(xf - mu), axis=-1, keepdims=True)
    y = (xf - mu) * lax.rsqrt(var + LN_EPS)
    return (y * g + b).astype(x.dtype)

def causal_depthwise_conv(x, w, b):
    k = w.shape[0]
    s_ = x.shape[1]
    xp = jnp.pad(x, ((0, 0), (k - 1, 0), (0, 0)))
    out = b
    for j in range(k):
        out = out + xp[:, j:j + s_] * w[j]
    return out

def multiscale_pool(u, w_pool, scale):
    b_, s_, _ = u.shape
    ug = u.reshape(b_, s_, POOL_GROUPS, POOL_GROUP_DIM).astype(jnp.float32)
    cs = jnp.concatenate([jnp.zeros_like(ug[:, :1]), jnp.cumsum(ug, axis=1)], axis=1)
    t = jnp.arange(s_)[:, None]
    win = jnp.array(POOL_WINDOWS, dtype=jnp.int32)[None, :]
    lo = jnp.maximum(t + 1 - win, 0)
    lower = cs[:, lo, jnp.arange(POOL_GROUPS)[None, :]]
    count = (t + 1 - lo).astype(jnp.float32)
    pooled = (cs[:, 1:] - lower) / count[..., None] - ug
    mixed = jnp.einsum('bsgc,gcd->bsgd', pooled.astype(u.dtype), w_pool)
    return mixed.reshape(b_, s_, POOL_WIDTH) * scale

def ssd_chunked_scan(xs, dt, a, bm, cm):
    b_, s_, h_, p_ = xs.shape
    c_ = s_ // CHUNK
    r_ = h_ // SSD_GROUPS
    xdt = (xs.astype(jnp.float32) * dt[..., None]).reshape(b_, c_, CHUNK, SSD_GROUPS, r_, p_)
    adt = (dt * a).reshape(b_, c_, CHUNK, SSD_GROUPS, r_)
    a_cum = jnp.cumsum(jnp.moveaxis(adt, 2, -1), axis=-1)
    bc = bm.astype(jnp.float32).reshape(b_, c_, CHUNK, SSD_GROUPS, SSD_STATE)
    cc = cm.astype(jnp.float32).reshape(b_, c_, CHUNK, SSD_GROUPS, SSD_STATE)
    causal = jnp.tril(jnp.ones((CHUNK, CHUNK), dtype=bool))
    seg = a_cum[..., :, None] - a_cum[..., None, :]
    decay = jnp.where(causal, jnp.exp(jnp.where(causal, seg, 0.0)), 0.0)
    cb = jnp.einsum('bclgn,bcsgn->bcgls', cc, bc)
    y_diag = jnp.einsum('bcgrls,bcsgrp->bclgrp', cb[:, :, :, None] * decay, xdt)
    decay_to_end = jnp.exp(a_cum[..., -1:] - a_cum)
    states = jnp.einsum('bclgn,bcgrl,bclgrp->bcgrpn', bc, decay_to_end, xdt)
    chunk_decay = jnp.exp(a_cum[..., -1])

    def carry_state(h, inp):
        st, dec = inp
        return h * dec[..., None, None] + st, h

    h0 = jnp.zeros_like(states[:, 0])
    _, h_prev = lax.scan(carry_state, h0, (jnp.moveaxis(states, 1, 0), jnp.moveaxis(chunk_decay, 1, 0)))
    h_prev = jnp.moveaxis(h_prev, 0, 1)
    y_off = jnp.einsum('bclgn,bcgrpn,bcgrl->bclgrp', cc, h_prev, jnp.exp(a_cum))
    return (y_diag + y_off).reshape(b_, s_, h_, p_)

def ssd_mixer(z, xbc, dt_raw, conv_w, conv_b, dt_bias, a_log, d_skip, norm_w):
    b_, s_, _ = xbc.shape
    xbc = jax.nn.silu(causal_depthwise_conv(xbc, conv_w, conv_b))
    xs = xbc[..., :SSD_WIDTH].reshape(b_, s_, SSD_HEADS, HEAD_DIM)
    bm = xbc[..., SSD_WIDTH:SSD_WIDTH + SSD_GROUPS * SSD_STATE].reshape(b_, s_, SSD_GROUPS, SSD_STATE)
    cm = xbc[..., SSD_WIDTH + SSD_GROUPS * SSD_STATE:].reshape(b_, s_, SSD_GROUPS, SSD_STATE)
    dt = jax.nn.softplus((dt_raw + dt_bias).astype(jnp.float32))
    a = -jnp.exp(a_log.astype(jnp.float32))
    y = ssd_chunked_scan(xs, dt, a, bm, cm) + xs.astype(jnp.float32) * d_skip[:, None]
    hg = (y.reshape(b_, s_, SSD_WIDTH) * jax.nn.silu(z.astype(jnp.float32)))
    hg = hg.reshape(b_, s_, SSD_GROUPS, SSD_WIDTH // SSD_GROUPS)
    hg = hg * lax.rsqrt(jnp.mean(jnp.square(hg), axis=-1, keepdims=True) + RMS_EPS)
    return (hg.reshape(b_, s_, SSD_WIDTH) * norm_w).astype(xbc.dtype)

def stick_breaking_attention(q, k, v):
    b_, s_, h_, d_ = q.shape
    scale = d_ ** -0.5
    outs = []
    for start in range(0, s_, Q_BLOCK):
        end = start + Q_BLOCK
        z = jnp.einsum('bqhd,bkhd->bhqk', q[:, start:end], k[:, :end]).astype(jnp.float32) * scale
        t_idx = start + jnp.arange(Q_BLOCK)[:, None]
        s_idx = jnp.arange(end)[None, :]
        strict = s_idx < t_idx
        log_not = jnp.where(strict, jax.nn.log_sigmoid(-z), 0.0)
        tail = lax.cumsum(log_not, axis=3, reverse=True) - log_not
        weights = jnp.where(strict, jnp.exp(jax.nn.log_sigmoid(z) + tail), 0.0)
        outs.append(jnp.einsum('bhqk,bkhd->bqhd', weights.astype(v.dtype), v[:, :end]))
    return jnp.concatenate(outs, axis=1)

def conv_glu_ffn(x, w_up, conv_w, conv_b, w_down):
    up = causal_depthwise_conv(x @ w_up, conv_w, conv_b)
    gate, val = up[..., :D_FF], up[..., D_FF:]
    return (jax.nn.silu(gate) * val) @ w_down

def setup_inputs(seed: int = 0) -> dict:
    key = jax.random.key(seed)
    ks = jax.random.split(key, 26)

    def nrm(k, shape, scale):
        return jax.random.normal(k, shape, jnp.float32) * scale

    dt0 = jnp.exp(jax.random.uniform(ks[6], (DEPTH, SSD_HEADS), jnp.float32, np.log(1e-3), np.log(1e-1)))
    return {
        'x': nrm(ks[0], (BATCH, SEQ, D_MODEL), 1.0),
        'p': nrm(ks[1], (DEPTH, BATCH, SEQ, PLE_DIM), 1.0),
        'w_in': nrm(ks[2], (DEPTH, D_MODEL, IN_COLS), D_MODEL ** -0.5),
        'pool_w': nrm(ks[3], (DEPTH, POOL_GROUPS, POOL_GROUP_DIM, POOL_GROUP_DIM), POOL_GROUP_DIM ** -0.5),
        'pool_scale': 1.0 + nrm(ks[4], (DEPTH, POOL_WIDTH), 0.1),
        'ssd_conv_w': nrm(ks[5], (DEPTH, SSD_CONV, SSD_XBC_WIDTH), SSD_CONV ** -0.5),
        'ssd_conv_b': nrm(ks[7], (DEPTH, SSD_XBC_WIDTH), 0.01),
        'ssd_dt_bias': dt0 + jnp.log(-jnp.expm1(-dt0)),
        'ssd_a_log': jnp.log(jax.random.uniform(ks[8], (DEPTH, SSD_HEADS), jnp.float32, 1.0, 16.0)),
        'ssd_d': 1.0 + nrm(ks[9], (DEPTH, SSD_HEADS), 0.1),
        'ssd_norm_w': 1.0 + nrm(ks[10], (DEPTH, SSD_WIDTH), 0.05),
        'w_out': nrm(ks[11], (DEPTH, MIX_WIDTH, D_MODEL), MIX_WIDTH ** -0.5 * DEEPNORM_BETA),
        'ln1_g': 1.0 + nrm(ks[12], (DEPTH, D_MODEL), 0.05),
        'ln1_b': nrm(ks[13], (DEPTH, D_MODEL), 0.01),
        'ffn_w_up': nrm(ks[14], (DEPTH, D_MODEL, 2 * D_FF), D_MODEL ** -0.5),
        'ffn_conv_w': nrm(ks[15], (DEPTH, FFN_CONV, 2 * D_FF), FFN_CONV ** -0.5),
        'ffn_conv_b': nrm(ks[16], (DEPTH, 2 * D_FF), 0.01),
        'ffn_w_down': nrm(ks[17], (DEPTH, D_FF, D_MODEL), D_FF ** -0.5 * DEEPNORM_BETA),
        'ln2_g': 1.0 + nrm(ks[18], (DEPTH, D_MODEL), 0.05),
        'ln2_b': nrm(ks[19], (DEPTH, D_MODEL), 0.01),
        'ple_w_gate': nrm(ks[20], (DEPTH, D_MODEL, D_MODEL), D_MODEL ** -0.5),
        'ple_w_proj': nrm(ks[21], (DEPTH, PLE_DIM, D_MODEL), PLE_DIM ** -0.5 * DEEPNORM_BETA),
    }

def reference(x, p, w_in, pool_w, pool_scale, ssd_conv_w, ssd_conv_b, ssd_dt_bias, ssd_a_log, ssd_d,
              ssd_norm_w, w_out, ln1_g, ln1_b, ffn_w_up, ffn_conv_w, ffn_conv_b, ffn_w_down, ln2_g, ln2_b,
              ple_w_gate, ple_w_proj):
    b_, s_, _ = x.shape
    for i in range(DEPTH):
        h = x @ w_in[i]
        pool_out = multiscale_pool(h[..., COL_POOL:COL_Z], pool_w[i], pool_scale[i])
        ssd_out = ssd_mixer(h[..., COL_Z:COL_XBC], h[..., COL_XBC:COL_DT], h[..., COL_DT:COL_Q],
                            ssd_conv_w[i], ssd_conv_b[i], ssd_dt_bias[i], ssd_a_log[i], ssd_d[i], ssd_norm_w[i])
        q = h[..., COL_Q:COL_K].reshape(b_, s_, SB_HEADS, HEAD_DIM)
        k = h[..., COL_K:COL_V].reshape(b_, s_, SB_HEADS, HEAD_DIM)
        v = h[..., COL_V:IN_COLS].reshape(b_, s_, SB_HEADS, HEAD_DIM)
        sb_out = stick_breaking_attention(q, k, v).reshape(b_, s_, SB_WIDTH)
        mix = jnp.concatenate([pool_out.astype(x.dtype), ssd_out.astype(x.dtype), sb_out.astype(x.dtype)], axis=-1) @ w_out[i]
        x = layer_norm(DEEPNORM_ALPHA * x + mix, ln1_g[i], ln1_b[i])
        ffn = conv_glu_ffn(x, ffn_w_up[i], ffn_conv_w[i], ffn_conv_b[i], ffn_w_down[i])
        ple = jax.nn.sigmoid(x @ ple_w_gate[i]) * (p[i] @ ple_w_proj[i])
        x = layer_norm(DEEPNORM_ALPHA * x + ffn + ple, ln2_g[i], ln2_b[i])
    return x


_drawn_inputs = setup_inputs


def setup_inputs(seed=0):
    import zlib

    import numpy as np

    out = dict(_drawn_inputs(seed))
    spreads = {}
    factors = {'pool_scale': 2.836,
     'ssd_conv_b': 8.0,
     'ssd_d': 2.94,
     'ssd_norm_w': 3.986,
     'ln1_b': 5.434,
     'ffn_conv_b': 8.0,
     'ln2_b': 5.693}
    for name, (base, spread) in spreads.items():
        noise = np.random.default_rng([zlib.crc32(name.encode()), seed]).standard_normal(out[name].shape)
        drawn = base * np.exp(spread * noise) if base else spread * noise
        out[name] = __import__('jax').numpy.asarray(drawn.astype(out[name].dtype))
    for name, factor in factors.items():
        out[name] = (out[name] * factor).astype(out[name].dtype)
    return out
```

```python
from contextlib import ExitStack

import numpy as np

import concourse.bass as bass
from concourse import mybir

F32 = mybir.dt.float32
F32R = mybir.dt.float32r
I32 = mybir.dt.int32
SIGN = -2 ** 31
ALU = mybir.AluOpType
ACT = mybir.ActivationFunctionType

P = 128
D = 1024
S = 1024
HALF = 512
KT = D // P
MT = S // P
HEAD = 64
POOL_W = 256
SSD_W = 384
SSD_HEADS = 6
STATE = 128
CONV = 4
FF = 2816
FF_TILES = FF // P
PER_CHUNK = 2
CHUNKS = FF_TILES // PER_CHUNK
FF_CONV = 3
PLE_TILES = 2
ALPHA = 2.0 ** 0.25
LN_EPS = 1e-5
RMS_EPS = 1e-6
SCALE = HEAD ** -0.5
PAIRS = 3
BIG = 3.0e38
NEG = -3.0e4

COL_Z = POOL_W
COL_XBC = COL_Z + SSD_W
COL_DT = COL_XBC + SSD_W + 4 * STATE
COL_Q = COL_DT + SSD_HEADS
COL_K = COL_Q + 384
COL_V = COL_K + 384

H_TILES = ["x0", "x1", "x2", "B0", "B1", "C0", "C1", "z0", "z1", "z2", "p0", "p1"]
WINDOWS = [["v1", "q1", "k1", "x0", "x1", "x2"], ["v2", "q2", "k2", "B0", "B1", "C0"],
           ["dt", "C1", "z0", "z1", "z2", "p0", "p1"]]
IN_TILES = ["v0", "q0", "k0"] + [t for w in WINDOWS for t in w]
IN_COLS = {"q": COL_Q, "k": COL_K, "v": COL_V, "x": COL_XBC, "B": COL_XBC + SSD_W,
           "C": COL_XBC + SSD_W + 2 * STATE, "z": COL_Z, "p": 0}
TURNED = ["v0", "v1", "v2", "dt"]

UNITS = [("x", 0), ("in", 0)] + [("x", i) for i in range(1, KT)] + [("in", i) for i in range(1, len(IN_TILES))]
UNITS += [("out", i) for i in range(KT)] + [("gate", 0)] + [("p", i) for i in range(PLE_TILES)]
UNITS += [("proj", i) for i in range(PLE_TILES)] + [("gate", i) for i in range(1, KT)]
FFN0 = len(UNITS)
UNITS += [("up", i) for i in range(4)]
for _c in range(1, CHUNKS):
    UNITS += [("up", 4 * _c), ("down", 2 * _c - 2), ("down", 2 * _c - 1)] + [("up", 4 * _c + i) for i in (1, 2, 3)]
UNITS += [("down", FF_TILES - 2), ("down", FF_TILES - 1)]
UNIT = {u: n for n, u in enumerate(UNITS)}
RAWS = 2
RINGS = 3
RING_OF = {}
for _n, _u in enumerate(UNITS):
    if _u[0] in ("in", "gate", "up", "down"):
        RING_OF[_n] = len(RING_OF)
FFN_R0 = RING_OF[FFN0]

TABLES = ["ident", "ones", "tri_le", "mask_lt", "cap_lt", "cap_le", "neg_ge", "neg_lt",
          "rms_01", "rms_10", "rms_11", "rms_12", "rms_21", "pool_cnt"]
STEPS = [(g, qh, kb, hd) for g in range(PAIRS) for qh in range(2)
         for kb in range(4 * qh + 3, -1, -1) for hd in range(2)]
NSTEP = len(STEPS)
PER_PAIR = NSTEP // PAIRS


def first_col(n):
    _, qh, kb, _ = STEPS[n]
    return max(0, P * kb - HALF * qh)


def on_diagonal(n):
    _, qh, kb, _ = STEPS[n]
    return kb >= 4 * qh


def projection_plan():
    p = 0
    pro = []
    for name in ("v0", "q0", "k0"):
        for h in range(2):
            pro.append(("tile", name, h, p))
            p += 1
    for h in range(2):
        pro.append(("turn", 0, h, p))
        p += 1
    by_step = []
    for g, window in enumerate(WINDOWS):
        pieces = []
        for i, name in enumerate(window):
            for h in range(2):
                it = ("tile", name, h, p)
                p += 1
                pieces += [(it, 0, 2), (it, 1, 2)]
            if (name[0] == "q" and i == 1) or (name == "C1" and g == 2):
                for hh in range(2):
                    pieces.append((("turn", g + 1, hh, p), 0, 1))
                    p += 1
        for s in range(PER_PAIR):
            a, b = s * len(pieces) // PER_PAIR, (s + 1) * len(pieces) // PER_PAIR
            by_step.append(pieces[a:b])
    return pro, by_step


PROLOGUE, BY_STEP = projection_plan()
PLACE = {}
for _it in PROLOGUE + [x[0] for s in BY_STEP for x in s]:
    PLACE[(_it[1], _it[2]) if _it[0] != "turn" else ("turn%d" % _it[1], _it[2])] = _it[3]
DONE_AT = [[it for it, part, parts in s if part == parts - 1] for s in BY_STEP]
STARTS = {}
for _s, _ps in enumerate(BY_STEP):
    for _it, _part, _parts in _ps:
        if _it[0] == "tile" and _it[2] == 0 and _part == 0:
            STARTS[IN_TILES.index(_it[1])] = _s
SPLIT_AT = {}
for _r in range(3, len(IN_TILES)):
    SPLIT_AT.setdefault(max(STARTS[_r - 2] + 1, 0) if _r - 2 >= 3 else (0 if _r == 3 else 1), []).append(_r)


BY_RING = {r: n for n, r in RING_OF.items()}
QK_ORDER = [(it[1], it[2]) for it in PROLOGUE + [i for d in DONE_AT for i in d]
            if it[0] == "tile" and it[1][0] in "qk"]
CONV_ORDER = [3, 4, 5, 6, 0, 1, 2]
TASKS = ["cu9", "bt0", "bt1", "cb0", "cb1", "xt0", "xt1", "xt2", "xt3", "cu0", "cu1", "st0", "st1", "st2", "st3",
         "cu2", "cu3", "yy0", "cu4", "cu5", "yy1", "po0", "po1", "yy2", "rm0", "rm1", "rm2"]
DTN = MT * SSD_HEADS
PARAM_SIZES = {"conv_w": 28, "conv_b": 7, "pool_scale": 2, "pool_inv": 2, "ssd_d": 3, "norm_w": 3, "dt_bias": DTN,
               "a_log": DTN, "ln1_g": KT, "ln1_b": KT, "ff_w": 3 * 2 * FF_TILES, "ff_b": 2 * FF_TILES}
PARAMS, N_PARAMS = {}, 0
for _k, _n in PARAM_SIZES.items():
    PARAMS[_k] = N_PARAMS
    N_PARAMS += _n


def build(nc, ctx, a, out):
    kb = 1024
    top = [2 * kb]

    def put(name, shape, dt=F32, at=None):
        size = -(-4 * int(np.prod(shape[1:])) // 32) * 32
        if at is None:
            at = top[0]
            top[0] += size
        assert at + size <= 229368, (name, at, size)
        return nc.alloc_sbuf_tensor_at(name, shape, dt, offset=at)

    def sem(name):
        return ctx.enter_context(nc.semaphore(name))

    raw = put("raw", [P, RAWS, D])
    wh = put("w_hi", [P, RINGS, D], F32R)
    wl = put("w_lo", [P, RINGS, D], F32R)
    tab = put("tables", [P, len(TABLES), P])
    neg_ge = put("neg_ge_r", [P, P], F32R)
    neg_lt = put("neg_lt_r", [P, P], F32R)
    pool_w = put("pool_w", [P, 2, P])
    par = put("params", [P, N_PARAMS])
    sm = put("small", [P, 10, DTN])
    st = put("ln_stats", [P, MT, 16])
    x0 = top[0]
    xh = put("x_hi", [P, KT, S], F32R)
    xl = put("x_lo", [P, KT, S], F32R)
    mh = put("mix_hi", [P, KT, S], F32R, x0)
    ml = put("mix_lo", [P, KT, S], F32R, x0 + 32 * kb)
    xdt = put("x_dt", [P, MT, SSD_W], F32, x0 + 2 * 4 * kb)
    xw = put("x_weighted", [P, MT, SSD_W], F32, x0 + (32 + 2 * 4) * kb)
    pa = put("pool_a", [P, S], F32, x0 + 32 * kb)
    pb = put("pool_b", [P, S], F32, x0 + 36 * kb)
    h0 = top[0]
    ht = put("h_tiles", [P, len(H_TILES), S])
    a0 = top[0]
    sets = [a0, h0 + 6 * 4 * kb, a0]
    qh = [put("q_hi%d" % i, [P, S], F32R, sets[i]) for i in range(2)]
    ql = [put("q_lo%d" % i, [P, S], F32R, sets[i] + 4 * kb) for i in range(2)]
    kh = [put("k_hi%d" % i, [P, S], F32R, sets[i] + 8 * kb) for i in range(2)]
    kl = [put("k_lo%d" % i, [P, S], F32R, sets[i] + 12 * kb) for i in range(2)]
    vn = [put("v_nat%d" % i, [P, MT, P], F32, sets[i] + 16 * kb) for i in range(2)]
    vt = put("v_t", [P, S], F32, h0 + 11 * 4 * kb)
    top[0] = a0 + 20 * kb
    zs = put("z_scaled", [P, 3, HALF])
    na = put("neg_abs", [P, 2, HALF])
    sp = put("softplus", [P, 2, HALF])
    sph = put("sp_hi", [P, 3, HALF], F32R)
    spl = put("sp_lo", [P, 3, HALF], F32R)
    u = put("weights", [P, 2, HALF])
    sb = put("sb_out", [P, PAIRS, S])
    cv = put("conv", [P, 7, S], F32, a0)
    wt = put("decayed", [P, 2, S], F32, a0 + 28 * kb)
    ce = put("c_scaled", [P, 2, S], F32, a0 + 36 * kb)
    tmp = put("tmp", [P, S], F32, a0 + 44 * kb)
    bn = put("b_natural", [P, 2, MT, P], F32, h0)
    hs = put("states", [P, MT, SSD_W], F32, h0 + 8 * kb)
    cb = put("cb", [P, 2, S], F32, h0 + 20 * kb)
    oh = put("wo_hi", [P, KT, D], F32R, h0)
    ol = put("wo_lo", [P, KT, D], F32R, h0 + 32 * kb)
    acc = put("acc", [P, KT, S], F32, h0 + 64 * kb)
    yn = put("y_nat", [P, 2, D], F32, h0 + 96 * kb)
    xn = put("x_nat", [P, D], F32, h0 + 104 * kb)
    ph = put("p_hi", [P, PLE_TILES, S], F32R, h0)
    pl = put("p_lo", [P, PLE_TILES, S], F32R, h0 + 8 * kb)
    pwh = put("proj_hi", [P, PLE_TILES, D], F32R, h0 + 16 * kb)
    pwl = put("proj_lo", [P, PLE_TILES, D], F32R, h0 + 24 * kb)
    sig = put("sigmoid", [P, 2, S], F32, h0 + 48 * kb)
    hh = put("h_hi", [P, PER_CHUNK, S], F32R, h0)
    hl = put("h_lo", [P, PER_CHUNK, S], F32R, h0 + 8 * kb)
    cf = put("conv_ff", [P, 2, S], F32, h0 + 56 * kb)
    hf = put("h_ff", [P, S], F32, h0 + 104 * kb)
    lng = put("ln2_gain", [P, D], F32, h0 + 96 * kb)
    lnb = put("ln2_bias", [P, D], F32, h0 + 100 * kb)
    on = put("o_norm", [P, 4, D], F32, h0 + 16 * kb)

    ps = ctx.enter_context(nc.psum_tensor("ps", [P, 8, HALF], F32))

    def two(i):
        return ps[:, 2 * i:2 * i + 2, :].rearrange("p b n -> p (b n)")

    def table(name):
        return tab[:, TABLES.index(name), :]

    def param(name, i=0, n=1):
        c = PARAMS[name] + i
        return par[:, c:c + n]

    const_in = sem("const_in")
    const_r = sem("const_r")
    raw_in = [sem("raw_in%d" % i) for i in range(RAWS)]
    hi_done = sem("hi_done")
    split_done = sem("split_done")
    barrier = sem("barrier")
    p_full = sem("p_full")
    p_free = [sem("p_free%d" % i) for i in range(2)]
    qk_hi = sem("qk_hi")
    z_full, zs_done, na_done = sem("z_full"), sem("zs_done"), sem("na_done")
    e_done, l_done, lo_done = sem("e_done"), sem("l_done"), sem("lo_done")
    tri_full, u_done, w_done, av_done = sem("tri_full"), sem("u_done"), sem("w_done"), sem("av_done")
    o_out = sem("o_out")
    dve_chain = sem("dve_chain")
    pool_chain = sem("pool_chain")
    dt_v = sem("dt_v")
    dt_a = sem("dt_a")
    tap_done, conv_done, silu_done = sem("tap_done"), sem("conv_done"), sem("silu_done")
    d_full = sem("d_full")
    d_free = [sem("d_free%d" % i) for i in range(4)]
    decay_done = sem("decay_done")
    arg_done, wexp_done, wt_done = sem("arg_done"), sem("wexp_done"), sem("wt_done")
    xw_done = sem("xw_done")
    hg_done, sq_done, var_done, sqrt_done, nrm_done = (
        sem("hg_done"), sem("sq_done"), sem("var_done"), sem("sqrt_done"), sem("nrm_done"))
    mixh = sem("mix_hi_done")
    pooled = sem("pooled")
    x_in, y_full, y_read, v_eps, v_sqrt = sem("x_in"), sem("y_full"), sem("y_read"), sem("v_eps"), sem("v_sqrt")
    y_norm, t_full, x1_done, x1_split = sem("y_norm"), sem("t_full"), sem("x1_done"), sem("x1_split")
    u_full, u_free, sig_done = sem("u_full"), sem("u_free"), sem("sig_done")
    tap_ff, tap_mid, silu_ff, prod_mid, h_done = (
        sem("tap_ff"), sem("tap_mid"), sem("silu_ff"), sem("prod_mid"), sem("h_done"))
    dn_full, dn_added = sem("dn_full"), sem("dn_added")
    ln_in, o_full, o_eps, o_sqrt, o_aff, o_nrm, o_gain, o_bias = (
        sem("ln_in"), sem("o_full"), sem("o_eps"), sem("o_sqrt"), sem("o_aff"), sem("o_nrm"), sem("o_gain"),
        sem("o_bias"))
    stored = [sem("stored%d" % i) for i in range(4)]

    def meet(eng, k):
        eng.drain().then_inc(barrier, 1)
        eng.wait_ge(barrier, 4 * k)

    def wait_evacuated(eng, p):
        eng.wait_ge(p_free[p % 2], p // 2 + 1)

    def unit_place(n, lo):
        kind, i = UNITS[n]
        if kind == "x":
            return (xl if lo else xh)[:, i, :]
        if kind == "out":
            return (ol if lo else oh)[:, i, :]
        if kind == "p":
            return (pl if lo else ph)[:, i, :]
        if kind == "proj":
            return (pwl if lo else pwh)[:, i, :]
        return (wl if lo else wh)[:, RING_OF[n] % RINGS, :]

    def wait_ring_free(eng, n, it=0):
        if n not in RING_OF or RING_OF[n] < RINGS:
            return
        kind, i = UNITS[BY_RING[RING_OF[n] - RINGS]]
        if kind == "in":
            eng.wait_ge(p_full, PLACE[(IN_TILES[i], 1)] + 1)
        elif kind == "gate":
            eng.wait_ge(u_full, 2 * i + 1)
        elif kind == "up":
            eng.wait_ge(u_full, 2 * KT + i + 1 + 4 * it)
        else:
            eng.wait_ge(dn_full, 16 * (i // 2 + 1) + 16 * it)

    def hi(n, it=0):
        nc.scalar.wait_ge(raw_in[n % RAWS], 16 * (n // RAWS + 1) + 16 * 6 // RAWS * it)
        wait_ring_free(nc.scalar, n, it)
        nc.scalar.activation(unit_place(n, False), raw[:, n % RAWS, :], ACT.Copy).then_inc(hi_done, 1)

    def lo(n, it=0):
        nc.vector.wait_ge(hi_done, n + 1 + 6 * it)
        nc.vector.tensor_tensor(unit_place(n, True), raw[:, n % RAWS, :], unit_place(n, False).bitcast(F32),
                                ALU.subtract).then_inc(split_done, 1)

    block = ctx.enter_context(nc.Block())

    @block.sync
    def _(eng):
        def unit_source(n):
            kind, i = UNITS[n]
            return a["u_" + kind][i]

        def load(n):
            if n >= RAWS:
                eng.wait_ge(split_done, n - RAWS + 1)
            eng.dma_start(raw[:, n % RAWS, :], unit_source(n)).then_inc(raw_in[n % RAWS], 16)

        load(0)
        load(1)
        eng.dma_start(par[:, :], a["params"]).then_inc(const_in, 16)
        eng.dma_start(tab[:, :, :].rearrange("p t n -> p (t n)"), a["tables"]).then_inc(const_in, 16)
        eng.dma_start(pool_w[:, :, :].rearrange("p t n -> p (t n)"), a["pool_w"]).then_inc(const_in, 16)
        for n in range(2, UNIT[("out", 0)]):
            load(n)
        eng.wait_ge(barrier, 8)
        for n in range(UNIT[("out", 0)], UNIT[("out", 0)] + KT):
            load(n)
        for m in range(MT):
            if m:
                eng.wait_ge(y_read, m)
            eng.dma_start(xn[:, :], a["x_nat"][m]).then_inc(x_in, 16)
            if m < 2:
                load(UNIT[("gate", 0)] + m)
        for n in range(UNIT[("p", 1)], FFN0 + 4):
            load(n)
        eng.wait_ge(t_full, MT)
        eng.dma_start(lng[:, :], a["ln2_g"].partition_broadcast(P)).then_inc(ln_in, 16)
        eng.dma_start(lnb[:, :], a["ln2_b"].partition_broadcast(P)).then_inc(ln_in, 16)
        n0 = FFN0 + 4
        with eng.Fori(0, CHUNKS - 1) as it:
            for j in range(6):
                n = n0 + j
                eng.wait_ge(split_done, n - RAWS + 1 + 6 * it)
                kind, i = UNITS[n]
                src = a["u_up"][i + 4 * it] if kind == "up" else a["u_down"][i + 2 * it]
                eng.dma_start(raw[:, n % RAWS, :], src).then_inc(raw_in[n % RAWS], 16)
        for n in range(len(UNITS) - 2, len(UNITS)):
            load(n)
        for m in range(MT):
            eng.wait_ge(o_bias, m + 1)
            eng.dma_start(out[m * P:(m + 1) * P, :], on[:, m % 4, :]).then_inc(stored[m % 4], 16)
        for i in range(4):
            eng.wait_ge(stored[i], 16 * MT // 4)

    @block.tensor
    def _(eng):
        mm = nc.tensor.matmul

        def three(dst, w_hi, w_lo, x_hi, x_lo, first, last):
            mm(dst, w_hi, x_hi, start=first, stop=False)
            mm(dst, w_hi, x_lo, start=False, stop=False)
            return mm(dst, w_lo, x_hi, start=False, stop=last)

        def piece(it, part, parts):
            kind, name, h, p = it
            bank = ps[:, p % 2, :]
            if part == 0 and p >= 2:
                wait_evacuated(eng, p - 2)
            if kind == "tile":
                i = IN_TILES.index(name)
                n = UNIT[("in", i)]
                slot = RING_OF[n] % RINGS
                if part == 0 and h == 0:
                    eng.wait_ge(split_done, n + 1)
                for kt in range(part * KT // parts, (part + 1) * KT // parts):
                    if i == 0 and h == 0:
                        eng.wait_ge(split_done, UNIT[("x", kt)] + 1)
                    c = slice(kt * P, (kt + 1) * P)
                    s_ = slice(h * HALF, (h + 1) * HALF)
                    last = three(bank, wh[:, slot, c], wl[:, slot, c], xh[:, kt, s_], xl[:, kt, s_],
                                 kt == 0, kt == KT - 1)
            elif kind == "turn":
                for hh_ in range(2):
                    wait_evacuated(eng, PLACE[(TURNED[name], hh_)])
                for j in range(4):
                    last = nc.tensor.transpose(bank[:, j * P:(j + 1) * P], vt[:, (4 * h + j) * P:(4 * h + j + 1) * P],
                                               table("ident"))
            if part == parts - 1:
                last.then_inc(p_full, 1)

        def z_scores(n):
            g, q_half, key, hd = STEPS[n]
            if n % PER_PAIR == 0:
                for name in ("q%d" % g, "k%d" % g):
                    for h in range(2):
                        wait_evacuated(eng, PLACE[(name, h)])
            if n >= 2:
                eng.wait_ge(zs_done, n - 1)
            r = slice(HEAD * hd, HEAD * hd + HEAD)
            kc = slice(key * P, (key + 1) * P)
            c0 = first_col(n)
            qc = slice(q_half * HALF + c0, (q_half + 1) * HALF)
            s_ = g % 2
            three(ps[:, 2 + n % 2, c0:], kh[s_][r, kc], kl[s_][r, kc], qh[s_][r, qc], ql[s_][r, qc],
                  True, True).then_inc(z_full, 1)

        def suffix(n):
            hd, c0 = STEPS[n][3], first_col(n)
            first = STEPS[n][2] == 4 * STEPS[n][1] + 3
            eng.wait_ge(lo_done, n + 1)
            dst = ps[:, 4 + hd, c0:]
            mm(dst, neg_ge[:, :], sph[:, n % 3, c0:], start=first, stop=False, skip_group_check=True)
            mm(dst, neg_ge[:, :], spl[:, n % 3, c0:], start=False, stop=True,
               skip_group_check=True).then_inc(tri_full, 1)

        def rest_and_values(n):
            g, q_half, key, hd = STEPS[n]
            c0 = first_col(n)
            eng.wait_ge(u_done, n + 1)
            if key:
                dst = ps[:, 4 + hd, c0:]
                mm(dst, neg_lt[:, :], sph[:, n % 3, c0:], start=False, stop=False, skip_group_check=True)
                mm(dst, neg_lt[:, :], spl[:, n % 3, c0:], start=False, stop=True, skip_group_check=True)
            first = key == 4 * q_half + 3
            o = 2 * g + q_half
            if first and o >= 2:
                eng.wait_ge(o_out, o - 1)
            if first and q_half == 0:
                for h in range(2):
                    wait_evacuated(eng, PLACE[("turn%d" % g, h)])
            eng.wait_ge(w_done, n + 1)
            r = slice(HEAD * hd, HEAD * hd + HEAD)
            mm(ps[r, 6 + o % 2, c0:], vn[g % 2][:, key, r], u[:, n % 2, c0:], start=first, stop=True,
               skip_group_check=True).then_inc(av_done, 1)

        for it in PROLOGUE:
            if it[0] == "turn":
                eng.wait_ge(const_in, 48)
                eng.wait_ge(const_r, 1)
            piece(it, 0, 1)
        for n in range(-2, NSTEP + 1):
            if 0 <= n + 2 < NSTEP:
                z_scores(n + 2)
            if 0 <= n < NSTEP:
                for pc in BY_STEP[n]:
                    piece(*pc)
                suffix(n)
            if 0 <= n - 1 < NSTEP:
                rest_and_values(n - 1)
        meet(eng, 1)

        def bank_pair(name):
            t = TASKS.index(name)
            if t >= 4:
                eng.wait_ge(d_free[t % 4], t // 4)
            return two(t % 4)

        def turn(dst, src):
            return nc.tensor.transpose(dst, src, table("ident"))

        for name in TASKS:
            kind, i = name[:2], int(name[2])
            if kind == "cu":
                eng.wait_ge(dt_v, 3)
            elif kind == "bt":
                eng.wait_ge(silu_done, i + 1)
            elif kind == "cb":
                eng.wait_ge(silu_done, 2 + i + 1)
            elif kind == "xt":
                eng.wait_ge(silu_done, 7)
            elif kind == "st":
                eng.wait_ge(xw_done, 2 * (i + 1))
                eng.wait_ge(d_free[TASKS.index("bt1") % 4], TASKS.index("bt1") // 4 + 1)
            elif kind == "yy":
                eng.wait_ge(wt_done, 2 * (i + 1))
                eng.wait_ge(d_free[TASKS.index("st3") % 4], TASKS.index("st3") // 4 + 1)
            elif kind == "po":
                eng.wait_ge(pooled, 2)
            elif kind == "rm":
                eng.wait_ge(sq_done, 3)
            dst = bank_pair(name)
            if kind == "cu" and i == 9:
                mm(dst[:, 0:DTN], table("tri_le"), sm[:, 5, :], start=True, stop=True)
                last = mm(dst[:, 64:64 + DTN], table("ones"), sm[:, 5, :], start=True, stop=True)
            elif kind == "cu":
                for c in range(MT):
                    col = sm[:, 5, c * SSD_HEADS + i:c * SSD_HEADS + i + 1]
                    last = mm(dst[:, c * P:(c + 1) * P], col.broadcast_to([P, P]), table("tri_le"),
                              start=True, stop=True)
            elif kind == "bt":
                for c in range(MT):
                    last = turn(dst[:, c * P:(c + 1) * P], cv[:, 3 + i, c * P:(c + 1) * P])
            elif kind == "cb":
                for c in range(MT):
                    t = slice(c * P, (c + 1) * P)
                    last = mm(dst[:, t], cv[:, 3 + i, t], cv[:, 5 + i, t], start=True, stop=True)
            elif kind == "xt":
                for c in range(2):
                    for j in range(3):
                        last = turn(dst[:, c * HALF + j * P:c * HALF + (j + 1) * P],
                                    cv[:, j, (2 * i + c) * P:(2 * i + c + 1) * P])
            elif kind == "st":
                for c in range(2 if i < 3 else 1):
                    for g in range(2):
                        w = SSD_W // 2
                        last = mm(dst[:, c * HALF + g * w:c * HALF + (g + 1) * w], bn[:, g, 2 * i + c, :],
                                  xw[:, 2 * i + c, g * w:(g + 1) * w], start=True, stop=True)
            elif kind == "yy":
                for c in range(MT):
                    t = slice(c * P, (c + 1) * P)
                    for hd in range(2):
                        r = slice(HEAD * hd, HEAD * hd + HEAD)
                        f = slice((2 * i + hd) * HEAD, (2 * i + hd + 1) * HEAD)
                        mm(dst[r, t], xdt[:, c, f], wt[:, hd, t], start=True, stop=False)
                        last = mm(dst[r, t], hs[:, c, f], ce[:, hd, t], start=False, stop=True)
            elif kind == "po":
                for h in range(2):
                    s_ = slice(h * HALF, (h + 1) * HALF)
                    last = mm(dst[:, s_], pool_w[:, i, :], ht[:, 10 + i, s_], start=True, stop=True)
            elif kind == "rm":
                src = [[(0, "ones"), (1, "rms_10")], [(0, "rms_01"), (1, "rms_11"), (2, "rms_21")],
                       [(1, "rms_12"), (2, "ones")]][i]
                for h in range(2):
                    s_ = slice(h * HALF, (h + 1) * HALF)
                    for j, (tile, name_) in enumerate(src):
                        last = mm(dst[:, s_], table(name_), cv[:, 3 + tile, s_], start=j == 0,
                                  stop=j == len(src) - 1)
            last.then_inc(d_full, 1)
        meet(eng, 2)

        def back(m):
            eng.wait_ge(y_norm, m + 1)
            if m >= 2:
                eng.wait_ge(x1_done, m - 1)
            dst = two(2 + m % 2)
            for kt in range(KT):
                last = turn(dst[:, kt * P:(kt + 1) * P], yn[:, m % 2, kt * P:(kt + 1) * P])
            last.then_inc(t_full, 1)

        for m in range(MT):
            if m >= 2:
                eng.wait_ge(y_read, m - 1)
            t = slice(m * P, (m + 1) * P)
            for h in range(2):
                for kt in range(KT):
                    if m == 0 and h == 0:
                        eng.wait_ge(split_done, UNIT[("out", kt)] + 1)
                    c = slice(h * HALF, (h + 1) * HALF)
                    last = three(two(m % 2)[:, c], mh[:, kt, t], ml[:, kt, t], oh[:, kt, c], ol[:, kt, c],
                                 kt == 0, kt == KT - 1)
            last.then_inc(y_full, 1)
            if m:
                back(m - 1)

        def column_tile(item, slot, n, it=0, halves=(0, 1)):
            eng.wait_ge(split_done, n + 1 + 6 * it)
            for h in halves:
                s_ = slice(h * HALF, (h + 1) * HALF)
                for kt in range(KT):
                    c = slice(kt * P, (kt + 1) * P)
                    last = three(two(item % 2)[:, s_], wh[:, slot, c], wl[:, slot, c], mh[:, kt, s_], ml[:, kt, s_],
                                 kt == 0, kt == KT - 1)
            if 1 in halves:
                last.then_inc(u_full, 1)

        def gate_item(j, halves=(0, 1)):
            n = UNIT[("gate", j)]
            column_tile(2 * j, RING_OF[n] % RINGS, n, 0, halves)

        def proj_item(j):
            c = slice(j * P, (j + 1) * P)
            for h in range(2):
                s_ = slice(h * HALF, (h + 1) * HALF)
                for i in range(PLE_TILES):
                    last = three(two(1)[:, s_], pwh[:, i, c], pwl[:, i, c], ph[:, i, s_], pl[:, i, s_],
                                 i == 0, i == PLE_TILES - 1)
            last.then_inc(u_full, 1)

        eng.wait_ge(x1_split, MT // 2)
        gate_item(0, (0,))
        back(MT - 1)
        eng.wait_ge(x1_split, MT)
        gate_item(0, (1,))
        eng.wait_ge(split_done, UNIT[("proj", 1)] + 1)
        eng.wait_ge(y_read, MT)
        proj_item(0)
        for j in range(1, KT):
            eng.wait_ge(sig_done, j)
            gate_item(j)
            eng.wait_ge(u_free, 2 * j - 1)
            proj_item(j)

        def up(t, n, it=0):
            if t == 0:
                eng.wait_ge(sig_done, KT)
            else:
                eng.wait_ge(u_free, 2 * KT + t - 1 + 4 * it)
            column_tile(2 * KT + t, RING_OF[n] % RINGS, n, it)

        def turn_back(m):
            if m in (0, MT // 2):
                eng.wait_ge(dn_added, 16 * (CHUNKS - 1) + 8 + 8 * (m // 4))
            if m == 0:
                eng.wait_ge(u_free, 2 * KT + 4 * CHUNKS)
            elif m >= 2:
                eng.wait_ge(o_nrm, m - 1)
            for kt in range(KT):
                last = turn(two(m % 2)[:, kt * P:(kt + 1) * P], acc[:, kt, m * P:(m + 1) * P])
            last.then_inc(o_full, 1)

        def down(n, d, it=0, by_half=False):
            eng.wait_ge(split_done, n + 2 + 6 * it)
            eng.wait_ge(h_done, d // 8 + 2 + 2 * it)
            for k in range(16):
                j, h = (k % 8, k // 8) if by_half else (k // 2, k % 2)
                if by_half and k in (11, 12, 14, 15):
                    turn_back(k - 11 if k < 13 else k - 12)
                if d + k >= 4:
                    eng.wait_ge(dn_added, d + k - 3 + 16 * it)
                s_ = slice(h * HALF, (h + 1) * HALF)
                c = slice(j * P, (j + 1) * P)
                for i in range(2):
                    slot = (RING_OF[n] + i) % RINGS
                    last = three(ps[:, 4 + k % 4, :], wh[:, slot, c], wl[:, slot, c], hh[:, i, s_], hl[:, i, s_],
                                 i == 0, i == 1)
                last.then_inc(dn_full, 1)

        for t in range(4):
            up(t, FFN0 + t)
        n1 = FFN0 + 4

        def chunk(c, n, it=0):
            up(4 * c, n, it)
            down(n + 1, 16 * (c - 1), it)
            for t in (1, 2, 3):
                up(4 * c + t, n + 2 + t, it)

        chunk(1, n1)
        with eng.Fori(0, CHUNKS - 3) as it:
            chunk(2, n1 + 6, it)
        chunk(CHUNKS - 1, n1 + 6 * (CHUNKS - 2))
        down(len(UNITS) - 2, 16 * (CHUNKS - 1), by_half=True)
        for m in range(MT // 2, MT):
            turn_back(m)

    @block.scalar
    def _(eng):
        act = nc.scalar.activation

        def evacuate(it):
            kind, name, h, p = it
            if kind == "turn" and name == 3:
                return
            eng.wait_ge(p_full, p + 1)
            bank = ps[:, p % 2, :]
            s_ = slice(h * HALF, (h + 1) * HALF)
            if kind == "turn":
                act(vn[name % 2][:, 4 * h:4 * h + 4, :].rearrange("p m n -> p (m n)"), bank,
                    ACT.Copy).then_inc(p_free[p % 2], 1)
            elif name in H_TILES:
                if name == "p1":
                    for hh_ in range(2):
                        wait_evacuated(eng, PLACE[("turn3", hh_)])
                act(ht[:, H_TILES.index(name), s_], bank, ACT.Copy).then_inc(p_free[p % 2], 1)
            elif name in TURNED:
                g = TURNED.index(name)
                if g:
                    for hh_ in range(2):
                        wait_evacuated(eng, PLACE[("turn%d" % (g - 1), hh_)])
                act(vt[:, s_], bank, ACT.Copy).then_inc(p_free[p % 2], 1)
            else:
                g = int(name[1])
                act((qh if name[0] == "q" else kh)[g % 2][:, s_], bank, ACT.Copy).then_inc(qk_hi, 1)

        for n in range(2):
            hi(n)
        eng.wait_ge(const_in, 48)
        act(neg_ge[:, :], table("neg_ge"), ACT.Copy)
        act(neg_lt[:, :], table("neg_lt"), ACT.Copy).then_inc(const_r, 1)
        for n in range(2, UNIT[("in", 2)] + 1):
            hi(n)
        nc.scalar.preload_act_table_set("natural_log_exp_and_others")
        for it in PROLOGUE:
            evacuate(it)
        for n in range(-2, NSTEP + 2):
            for it in (DONE_AT[n - 1] if 1 <= n <= NSTEP else []):
                evacuate(it)
            if 0 <= n + 2 < NSTEP:
                k, c0 = n + 2, first_col(n + 2)
                eng.wait_ge(z_full, k + 1)
                if k >= 3:
                    eng.wait_ge(u_done, k - 2)
                act(zs[:, k % 3, c0:], ps[:, 2 + k % 2, c0:], ACT.Copy, scale=SCALE).then_inc(zs_done, 1)
            if 0 <= n + 1 < NSTEP:
                k, c0 = n + 1, first_col(n + 1)
                eng.wait_ge(na_done, k + 1)
                act(na[:, k % 2, c0:], na[:, k % 2, c0:], ACT.Exp).then_inc(e_done, 1)
                eng.wait_ge(e_done, k + 1)
                act(na[:, k % 2, c0:], na[:, k % 2, c0:], ACT.Ln, bias=1.0).then_inc(l_done, 1)
            for r in SPLIT_AT.get(n, []):
                hi(UNIT[("in", r)])
            if 0 <= n < NSTEP:
                c0 = first_col(n)
                eng.wait_ge(u_done, n + 1)
                act(u[:, n % 2, c0:], u[:, n % 2, c0:], ACT.Exp).then_inc(w_done, 1)
            if n >= 2 and STEPS[n - 2][2] == 0 and STEPS[n - 2][3] == 1:
                g, q_half = STEPS[n - 2][:2]
                eng.wait_ge(av_done, n - 1)
                act(sb[:, g, q_half * HALF:(q_half + 1) * HALF], ps[:, 6 + q_half, :],
                    ACT.Copy).then_inc(o_out, 1)
        meet(eng, 1)

        eng.wait_ge(dt_v, 1)
        act(sm[:, 2, :], sm[:, 1, :], ACT.Exp).then_inc(dt_a, 1)
        eng.wait_ge(dt_a, 1)
        act(sm[:, 2, :], sm[:, 2, :], ACT.Ln, bias=1.0).then_inc(dt_a, 1)
        act(sm[:, 4, :], param("a_log", 0, DTN), ACT.Exp).then_inc(dt_a, 1)
        for j in CONV_ORDER:
            act(cv[:, j, :], ht[:, j, :], ACT.Identity, scale=param("conv_w", 4 * j + 3),
                bias=param("conv_b", j)).then_inc(tap_done, 1)
        for g in range(PAIRS):
            act(mh[:, 5 + g, :], sb[:, g, :], ACT.Copy).then_inc(mixh, 1)
        for k, j in enumerate(CONV_ORDER):
            eng.wait_ge(conv_done, k + 1)
            act(cv[:, j, :], cv[:, j, :], ACT.Silu).then_inc(silu_done, 1)
        for j in range(3):
            act(ht[:, 7 + j, :], ht[:, 7 + j, :], ACT.Silu).then_inc(silu_done, 1)

        def task(name):
            t = TASKS.index(name)
            eng.wait_ge(d_full, t + 1)
            return two(t % 4), d_free[t % 4]

        eng.wait_ge(conv_done, 7)
        for g in range(2):
            src, free = task("bt%d" % g)
            act(bn[:, g, :, :].rearrange("p m n -> p (m n)"), src, ACT.Copy).then_inc(free, 1)
        for g in range(2):
            src, free = task("cb%d" % g)
            act(cb[:, g, :], src, ACT.Copy).then_inc(free, 1)
        eng.wait_ge(decay_done, 1)
        act(sm[:, 8, :], sm[:, 8, :], ACT.Exp).then_inc(dt_a, 1)
        act(sm[:, 9, :], sm[:, 7, :], ACT.Exp).then_inc(dt_a, 1)
        for h in range(SSD_HEADS):
            eng.wait_ge(arg_done, h + 1)
            if h >= 2:
                eng.wait_ge(d_full, TASKS.index("yy%d" % (h // 2 - 1)) + 1)
            act(wt[:, h % 2, :], tmp[:, :], ACT.Exp).then_inc(wexp_done, 1)
            src, free = task("cu%d" % h)
            act(ce[:, h % 2, :], src, ACT.Exp).then_inc(free, 1)
        for i in range(3):
            if i == 2:
                for k in range(2):
                    src, free = task("po%d" % k)
                    act(mh[:, k, :], src, ACT.Copy, scale=param("pool_scale", k)).then_inc(mixh, 1)
            eng.wait_ge(hg_done, i + 1)
            act(cv[:, 3 + i, :], cv[:, i, :], ACT.Square).then_inc(sq_done, 1)
        for i in range(3):
            eng.wait_ge(var_done, i + 1)
            act(tmp[:, :], tmp[:, :], ACT.Sqrt).then_inc(sqrt_done, 1)
            eng.wait_ge(nrm_done, i + 1)
            act(mh[:, 2 + i, :], cv[:, i, :], ACT.Copy).then_inc(mixh, 1)
        meet(eng, 2)

        for k in range(KT):
            hi(UNIT[("out", k)])
        def gain_bias(m):
            eng.wait_ge(t_full, m + 1)
            for kt in range(KT):
                last = act(acc[:, kt, m * P:(m + 1) * P], two(2 + m % 2)[:, kt * P:(kt + 1) * P], ACT.Identity,
                           scale=param("ln1_g", kt), bias=param("ln1_b", kt))
            last.then_inc(x1_done, 1)

        hi(UNIT[("gate", 0)])
        for m in range(MT):
            eng.wait_ge(v_eps, m + 1)
            act(st[:, m, 15:16], st[:, m, 14:15], ACT.Sqrt).then_inc(v_sqrt, 1)
            if m:
                gain_bias(m - 1)
        for i in range(PLE_TILES):
            hi(UNIT[("p", i)])
        gain_bias(MT - 1)

        for i in range(PLE_TILES):
            hi(UNIT[("proj", i)])
        hi(UNIT[("gate", 1)])
        for j in range(KT):
            if j + 2 < KT:
                hi(UNIT[("gate", j + 2)])
            else:
                hi(FFN0 + j + 2 - KT)
            eng.wait_ge(u_full, 2 * j + 1)
            if j >= 2:
                eng.wait_ge(u_free, 2 * j - 2)
            act(sig[:, j % 2, :], two(0), ACT.Sigmoid).then_inc(sig_done, 1)

        def tap(c, t, it=0):
            item = 2 * KT + 4 * c + t
            eng.wait_ge(u_full, item + 1 + 4 * it)
            if c or t >= 2:
                eng.wait_ge(h_done, 2 * c + t // 2 + 2 * it)
            w, b = PARAMS["ff_w"] + 3 * (4 * c + t) + 2, PARAMS["ff_b"] + 4 * c + t
            act(cf[:, t % 2, :], two(item % 2), ACT.Identity, scale=column(w, 12, it),
                bias=column(b, 4, it)).then_inc(tap_ff, 1)

        def column(c, step, it):
            return par[:, c:c + 1] if isinstance(it, int) else par[:, bass.ds(c + step * it, 1)]

        def gate(c, i, it=0):
            eng.wait_ge(u_free, 2 * KT + 4 * c + 2 * i + 1 + 4 * it)
            act(cf[:, 0, :], cf[:, 0, :], ACT.Silu).then_inc(silu_ff, 1)

        for n in (2, 3):
            hi(FFN0 + n)
        tap(0, 0)
        gate(0, 0)
        tap(0, 1)
        hi(FFN0 + 4)
        tap(0, 2)
        gate(0, 1)
        hi(FFN0 + 5)
        tap(0, 3)
        hi(FFN0 + 6)

        def chunk(c, n, it=0, last=False):
            tap(c, 0, it)
            gate(c, 0, it)
            for j in (3, 4, 5):
                hi(n + j, it)
            tap(c, 1, it)
            if not last:
                hi(n + 6, it)
            tap(c, 2, it)
            gate(c, 1, it)
            hi(n + (6 if last else 7), it)
            tap(c, 3, it)
            hi(n + (7 if last else 8), it)

        n1 = FFN0 + 4
        chunk(1, n1)
        with eng.Fori(0, CHUNKS - 3) as it:
            chunk(2, n1 + 6, it)
        chunk(CHUNKS - 1, n1 + 6 * (CHUNKS - 2), last=True)

        def normalise(m):
            eng.wait_ge(o_aff, m + 1)
            if m >= 4:
                eng.wait_ge(stored[m % 4], 16 * (m // 4))
            act(on[:, m % 4, :], two(m % 2), ACT.Identity, scale=st[:, m, 13:14],
                bias=st[:, m, 12:13]).then_inc(o_nrm, 1)

        for m in range(MT):
            eng.wait_ge(o_eps, m + 1)
            act(st[:, m, 15:16], st[:, m, 14:15], ACT.Sqrt).then_inc(o_sqrt, 1)
            if m:
                normalise(m - 1)
        normalise(MT - 1)

    @block.vector
    def _(eng):
        v = nc.vector
        chained = [0]

        def link(ins):
            chained[0] += 1
            ins.then_inc(dve_chain, 1)
            eng.wait_ge(dve_chain, chained[0])

        def evacuate(it):
            kind, name, h, p = it
            if kind == "turn" and name == 3:
                eng.wait_ge(p_full, p + 1)
                f = slice(4 * h * SSD_HEADS, 4 * (h + 1) * SSD_HEADS)
                by_tile = lambda ap: ap.rearrange("p (m n) -> p m n", m=4)
                v.tensor_tensor(by_tile(sm[:, 0, f]), by_tile(ps[:, p % 2, :])[:, :, 0:SSD_HEADS],
                                by_tile(param("dt_bias", 4 * h * SSD_HEADS, 4 * SSD_HEADS)),
                                ALU.add).then_inc(p_free[p % 2], 1)
            elif kind == "tile" and name[0] in "qk":
                g, s_ = int(name[1]), slice(h * HALF, (h + 1) * HALF)
                eng.wait_ge(qk_hi, QK_ORDER.index((name, h)) + 1)
                hi_, lo_ = (qh, ql) if name[0] == "q" else (kh, kl)
                v.tensor_tensor(lo_[g % 2][:, s_], ps[:, p % 2, :], hi_[g % 2][:, s_].bitcast(F32),
                                ALU.subtract).then_inc(p_free[p % 2], 1)

        for n in range(2):
            lo(n)
        eng.wait_ge(const_in, 48)
        for n in range(2, UNIT[("in", 2)] + 1):
            lo(n)
        for it in PROLOGUE:
            evacuate(it)
        for n in range(-2, NSTEP + 2):
            for it in (DONE_AT[n - 1] if 1 <= n <= NSTEP else []):
                evacuate(it)
            if 0 <= n + 2 < NSTEP:
                k, c0 = n + 2, first_col(n + 2)
                eng.wait_ge(zs_done, k + 1)
                v.tensor_scalar(na[:, k % 2, c0:].bitcast(I32), zs[:, k % 3, c0:].bitcast(I32), SIGN, None,
                                ALU.bitwise_or).then_inc(na_done, 1)
            if 0 <= n + 1 < NSTEP:
                k, c0 = n + 1, first_col(n + 1)
                eng.wait_ge(l_done, k + 1)
                link(v.scalar_tensor_tensor(out=sp[:, k % 2, c0:], in0=zs[:, k % 3, c0:], scalar=0.0,
                                            in1=na[:, k % 2, c0:], op0=ALU.max, op1=ALU.add))
                if on_diagonal(k):
                    d = sp[:, k % 2, c0:c0 + P]
                    link(v.tensor_tensor(d, d, table("mask_lt"), ALU.mult))
                if k >= 3:
                    eng.wait_ge(av_done, k - 2)
                link(v.tensor_copy(sph[:, k % 3, c0:], sp[:, k % 2, c0:]))
                v.tensor_tensor(spl[:, k % 3, c0:], sp[:, k % 2, c0:], sph[:, k % 3, c0:].bitcast(F32),
                                ALU.subtract).then_inc(lo_done, 1)
            for r in SPLIT_AT.get(n, []):
                lo(UNIT[("in", r)])
            if 0 <= n < NSTEP:
                c0, hd = first_col(n), STEPS[n][3]
                eng.wait_ge(tri_full, n + 1)
                if n >= 2:
                    eng.wait_ge(av_done, n - 1)
                ins = v.tensor_tensor(u[:, n % 2, c0:], zs[:, n % 3, c0:], ps[:, 4 + hd, c0:], ALU.add)
                if on_diagonal(n):
                    link(ins)
                    d = u[:, n % 2, c0:c0 + P]
                    ins = v.tensor_tensor(d, d, table("cap_lt"), ALU.min)
                ins.then_inc(u_done, 1)
        meet(eng, 1)

        v.tensor_scalar(sm[:, 1, :].bitcast(I32), sm[:, 0, :].bitcast(I32), SIGN, None,
                        ALU.bitwise_or).then_inc(dt_v, 1)
        eng.wait_ge(dt_a, 3)
        link(v.scalar_tensor_tensor(out=sm[:, 3, :], in0=sm[:, 0, :], scalar=0.0, in1=sm[:, 2, :],
                                    op0=ALU.max, op1=ALU.add))
        v.scalar_tensor_tensor(out=sm[:, 5, :], in0=sm[:, 3, :], scalar=-1.0, in1=sm[:, 4, :],
                               op0=ALU.mult, op1=ALU.mult).then_inc(dt_v, 2)
        for k, j in enumerate(CONV_ORDER):
            eng.wait_ge(tap_done, k + 1)
            for b in range(1, CONV):
                ins = v.scalar_tensor_tensor(out=cv[:, j, b:], in0=ht[:, j, :S - b],
                                             scalar=param("conv_w", 4 * j + 3 - b), in1=cv[:, j, b:],
                                             op0=ALU.mult, op1=ALU.add)
                if b < CONV - 1:
                    link(ins)
            ins.then_inc(conv_done, 1)
        for g in range(PAIRS):
            eng.wait_ge(mixh, g + 1)
            v.tensor_tensor(ml[:, 5 + g, :], sb[:, g, :], mh[:, 5 + g, :].bitcast(F32), ALU.subtract)

        def task(name):
            t = TASKS.index(name)
            eng.wait_ge(d_full, t + 1)
            return two(t % 4), d_free[t % 4]

        def evacuated(name):
            t = TASKS.index(name)
            eng.wait_ge(d_free[t % 4], t // 4 + 1)

        def per_head(row, c):
            return sm[:, row, c * SSD_HEADS:(c + 1) * SSD_HEADS].unsqueeze(2).broadcast_to([P, SSD_HEADS, HEAD])

        def heads(ap):
            return ap.rearrange("p (h d) -> p h d", h=SSD_HEADS)

        src, free = task("cu9")
        v.tensor_copy(sm[:, 6:8, :], src[:, 0:128].rearrange("p (k n) -> p k n", k=2)[:, :, 0:DTN]).then_inc(free, 1)
        eng.wait_ge(free, 1)
        v.tensor_tensor(sm[:, 8, :], sm[:, 7, :], sm[:, 6, :], ALU.subtract).then_inc(decay_done, 1)
        link(v.memset(hs[:, 0, :], 0.0))
        eng.wait_ge(dt_a, 5)
        for k in range(4):
            src, free = task("xt%d" % k)
            for c in range(2):
                ch = 2 * k + c
                ins = v.tensor_tensor(heads(xdt[:, ch, :]), heads(src[:, c * HALF:c * HALF + SSD_W]),
                                      per_head(3, ch), ALU.mult)
                if c:
                    ins.then_inc(free, 1)
                    evacuated("xt%d" % k)
                else:
                    link(ins)
                v.tensor_tensor(heads(xw[:, ch, :]), heads(xdt[:, ch, :]), per_head(8, ch),
                                ALU.mult).then_inc(xw_done, 1)

        def decays(h):
            g = h // 3
            src, _ = task("cu%d" % h)
            if h:
                eng.wait_ge(wexp_done, h)
            so_far = sm[:, 6, :].rearrange("p (c h) -> p c h", h=SSD_HEADS)[:, :, h:h + 1].broadcast_to([P, MT, P])
            t3 = tmp[:, :].rearrange("p (c n) -> p c n", c=MT)
            link(v.tensor_tensor(t3, src.rearrange("p (c n) -> p c n", c=MT), so_far, ALU.subtract))
            v.tensor_tensor(t3, t3, table("cap_le").unsqueeze(1).broadcast_to([P, MT, P]),
                            ALU.min).then_inc(arg_done, 1)
            eng.wait_ge(wexp_done, h + 1)
            v.tensor_tensor(wt[:, h % 2, :], wt[:, h % 2, :], cb[:, g, :], ALU.mult)
            evacuated("cu%d" % h)
            v.tensor_tensor(ce[:, h % 2, :], ce[:, h % 2, :], cv[:, 5 + g, :], ALU.mult).then_inc(wt_done, 1)

        def gated(i):
            src, free = task("yy%d" % i)
            eng.wait_ge(silu_done, 10)
            v.scalar_tensor_tensor(out=cv[:, i, :], in0=cv[:, i, :], scalar=param("ssd_d", i), in1=src,
                                   op0=ALU.mult, op1=ALU.add).then_inc(free, 1)
            eng.wait_ge(free, TASKS.index("yy%d" % i) // 4 + 1)
            v.tensor_tensor(cv[:, i, :], cv[:, i, :], ht[:, 7 + i, :], ALU.mult).then_inc(hg_done, 1)

        decays(0)
        decays(1)
        for k in range(4):
            src, free = task("st%d" % k)
            for c in range(2 if k < 3 else 1):
                ch = 2 * k + c
                link(v.tensor_tensor(heads(hs[:, ch + 1, :]), heads(hs[:, ch, :]), per_head(9, ch), ALU.mult))
                ins = v.tensor_tensor(hs[:, ch + 1, :], hs[:, ch + 1, :], src[:, c * HALF:c * HALF + SSD_W], ALU.add)
                if c or k == 3:
                    ins.then_inc(free, 1)
                    evacuated("st%d" % k)
                else:
                    link(ins)
        decays(2)
        decays(3)
        gated(0)
        decays(4)
        decays(5)
        gated(1)
        for k in range(2):
            src, free = task("po%d" % k)
            eng.wait_ge(mixh, 4 + k)
            v.scalar_tensor_tensor(out=ml[:, k, :], in0=src, scalar=param("pool_scale", k),
                                   in1=mh[:, k, :].bitcast(F32), op0=ALU.mult, op1=ALU.subtract).then_inc(free, 1)
        gated(2)
        for i in range(3):
            src, free = task("rm%d" % i)
            if i:
                eng.wait_ge(nrm_done, i)
            link(v.tensor_scalar(tmp[:, :], src, 1.0 / (SSD_W // 2), RMS_EPS, ALU.mult, ALU.add))
            v.reciprocal(tmp[:, :], tmp[:, :]).then_inc(var_done, 1)
            eng.wait_ge(sqrt_done, i + 1)
            v.scalar_tensor_tensor(out=cv[:, i, :], in0=cv[:, i, :], scalar=param("norm_w", i), in1=tmp[:, :],
                                   op0=ALU.mult, op1=ALU.mult).then_inc(nrm_done, 1)
            eng.wait_ge(mixh, 6 + i)
            v.tensor_tensor(ml[:, 2 + i, :], cv[:, i, :], mh[:, 2 + i, :].bitcast(F32), ALU.subtract)
        meet(eng, 2)

        for k in range(KT):
            lo(UNIT[("out", k)])
        lo(UNIT[("gate", 0)])

        def statistics(m, rows):
            v.bn_stats(st[:, m, 0:6], rows[:, 0:HALF])
            link(v.bn_stats(st[:, m, 6:12], rows[:, HALF:D]))
            link(v.bn_aggr(st[:, m, 12:14], st[:, m, 0:12]))
            return v.tensor_scalar(st[:, m, 14:15], st[:, m, 13:14], LN_EPS, None, ALU.add)

        def split_x1(m):
            eng.wait_ge(x1_done, m + 1)
            t = slice(m * P, (m + 1) * P)
            link(v.tensor_copy(mh[:, :, t], acc[:, :, t]))
            v.tensor_tensor(ml[:, :, t], acc[:, :, t], mh[:, :, t].bitcast(F32), ALU.subtract).then_inc(x1_split, 1)

        for m in range(MT):
            eng.wait_ge(y_full, m + 1)
            eng.wait_ge(x_in, 16 * (m + 1))
            if m >= 2:
                eng.wait_ge(t_full, m - 1)
            v.scalar_tensor_tensor(out=yn[:, m % 2, :], in0=xn[:, :], scalar=ALPHA, in1=two(m % 2),
                                   op0=ALU.mult, op1=ALU.add).then_inc(y_read, 1)
            eng.wait_ge(y_read, m + 1)
            statistics(m, yn[:, m % 2, :]).then_inc(v_eps, 1)
            if m:
                split_x1(m - 1)
            eng.wait_ge(v_sqrt, m + 1)
            link(v.reciprocal(st[:, m, 15:16], st[:, m, 15:16]))
            v.tensor_scalar(yn[:, m % 2, :], yn[:, m % 2, :], st[:, m, 12:13], st[:, m, 15:16], ALU.subtract,
                            ALU.mult).then_inc(y_norm, 1)
        for i in range(PLE_TILES):
            lo(UNIT[("p", i)])
        split_x1(MT - 1)

        for i in range(PLE_TILES):
            lo(UNIT[("proj", i)])
        lo(UNIT[("gate", 1)])
        for j in range(KT):
            if j + 2 < KT:
                lo(UNIT[("gate", j + 2)])
            else:
                lo(FFN0 + j + 2 - KT)
            eng.wait_ge(sig_done, j + 1)
            eng.wait_ge(u_full, 2 * j + 2)
            v.tensor_tensor(sig[:, j % 2, :], sig[:, j % 2, :], two(1), ALU.mult).then_inc(u_free, 1)
            eng.wait_ge(u_free, 2 * j + 1)
            v.scalar_tensor_tensor(out=acc[:, j, :], in0=acc[:, j, :], scalar=ALPHA, in1=sig[:, j % 2, :],
                                   op0=ALU.mult, op1=ALU.add).then_inc(u_free, 1)

        def column(c, step, it):
            return par[:, c:c + 1] if isinstance(it, int) else par[:, bass.ds(c + step * it, 1)]

        def conv(c, t, it=0):
            item = 2 * KT + 4 * c + t
            src = two(item % 2)
            w = PARAMS["ff_w"] + 3 * (4 * c + t)
            eng.wait_ge(tap_ff, 4 * c + t + 1 + 4 * it)
            v.scalar_tensor_tensor(out=cf[:, t % 2, 1:], in0=src[:, :S - 1], scalar=column(w + 1, 12, it),
                                   in1=cf[:, t % 2, 1:], op0=ALU.mult, op1=ALU.add).then_inc(tap_mid, 1)
            eng.wait_ge(tap_mid, 4 * c + t + 1 + 4 * it)
            v.scalar_tensor_tensor(out=cf[:, t % 2, 2:], in0=src[:, :S - 2], scalar=column(w, 12, it),
                                   in1=cf[:, t % 2, 2:], op0=ALU.mult, op1=ALU.add).then_inc(u_free, 1)

        def product(c, i, it=0):
            eng.wait_ge(silu_ff, 2 * c + i + 1 + 2 * it)
            eng.wait_ge(u_free, 2 * KT + 4 * c + 2 * i + 2 + 4 * it)
            v.tensor_tensor(hf[:, :], cf[:, 0, :], cf[:, 1, :], ALU.mult).then_inc(prod_mid, 1)
            eng.wait_ge(prod_mid, 2 * (2 * c + i) + 1 + 4 * it)
            if c:
                eng.wait_ge(dn_full, 16 * c + 16 * it)
            v.tensor_copy(hh[:, i, :], hf[:, :]).then_inc(prod_mid, 1)
            eng.wait_ge(prod_mid, 2 * (2 * c + i) + 2 + 4 * it)
            v.tensor_tensor(hl[:, i, :], hf[:, :], hh[:, i, :].bitcast(F32), ALU.subtract).then_inc(h_done, 1)

        def add_down(c, it=0, by_half=False, halves=range(16)):
            for k in halves:
                eng.wait_ge(dn_full, 16 * c + k + 1 + 16 * it)
                j, h = (k % 8, k // 8) if by_half else (k // 2, k % 2)
                dst = acc[:, j, h * HALF:(h + 1) * HALF]
                if k == 0:
                    eng.wait_ge(u_free, 2 * KT)
                    if c:
                        eng.wait_ge(dn_added, 16 * c + 16 * it)
                v.tensor_tensor(dst, dst, ps[:, 4 + k % 4, :], ALU.add).then_inc(dn_added, 1)

        lo(FFN0 + 2)
        lo(FFN0 + 3)
        conv(0, 0)
        conv(0, 1)
        lo(FFN0 + 4)
        product(0, 0)
        conv(0, 2)
        lo(FFN0 + 5)
        conv(0, 3)
        product(0, 1)
        lo(FFN0 + 6)

        def chunk(c, n, it=0, last=False):
            conv(c, 0, it)
            lo(n + 3, it)
            add_down(c - 1, it)
            lo(n + 4, it)
            lo(n + 5, it)
            conv(c, 1, it)
            product(c, 0, it)
            if not last:
                lo(n + 6, it)
            conv(c, 2, it)
            lo(n + (6 if last else 7), it)
            conv(c, 3, it)
            product(c, 1, it)
            lo(n + (7 if last else 8), it)

        n1 = FFN0 + 4
        chunk(1, n1)
        with eng.Fori(0, CHUNKS - 3) as it:
            chunk(2, n1 + 6, it)
        chunk(CHUNKS - 1, n1 + 6 * (CHUNKS - 2), last=True)
        for k in range(12):
            add_down(CHUNKS - 1, 0, True, [k])

        eng.wait_ge(ln_in, 32)

        def gain(m):
            eng.wait_ge(o_nrm, m + 1)
            v.tensor_tensor(on[:, m % 4, :], on[:, m % 4, :], lng[:, :], ALU.mult).then_inc(o_gain, 1)

        for m in range(MT):
            eng.wait_ge(o_full, m + 1)
            statistics(m, two(m % 2)).then_inc(o_eps, 1)
            if m < 4:
                add_down(CHUNKS - 1, 0, True, [12 + m])
            if m:
                gain(m - 1)
            eng.wait_ge(o_sqrt, m + 1)
            link(v.reciprocal(st[:, m, 13:14], st[:, m, 15:16]))
            v.scalar_tensor_tensor(out=st[:, m, 12:13], in0=st[:, m, 12:13], scalar=-1.0, in1=st[:, m, 13:14],
                                   op0=ALU.mult, op1=ALU.mult).then_inc(o_aff, 1)
        gain(MT - 1)

    @block.gpsimd
    def _(eng):
        g = nc.gpsimd
        chained = [0]

        def link(ins):
            chained[0] += 1
            ins.then_inc(pool_chain, 1)
            eng.wait_ge(pool_chain, chained[0])

        def doubled(dst, src, k, rows):
            g.tensor_copy(dst[rows, :k], src[rows, :k])
            link(g.tensor_tensor(dst[rows, k:], src[rows, k:], src[rows, :S - k], ALU.add))

        meet(eng, 1)
        every, upper, lower = slice(0, P), slice(HEAD, P), slice(0, HEAD)
        for i in range(2):
            x_ = ht[:, 10 + i, :]
            doubled(pa, ht[:, 10 + i, :], 1, every)
            s_, d_, k = pa, pb, 2
            if i == 1:
                doubled(pb, pa, 2, every)
                doubled(pa, pb, 4, every)
                k = 8
            g.tensor_copy(pb[lower, :], pa[lower, :])
            doubled(pb, pa, k, upper)
            link(g.tensor_tensor(pb[:, 0:16], pb[:, 0:16], table("pool_cnt")[:, 16 * i:16 * i + 16], ALU.mult))
            link(g.tensor_scalar(pb[:, :], pb[:, :], param("pool_inv", i), None, ALU.mult))
            g.tensor_tensor(x_, pb[:, :], x_, ALU.subtract).then_inc(pooled, 1)
            eng.wait_ge(pooled, i + 1)
        meet(eng, 2)
        eng.wait_ge(ln_in, 32)
        for m in range(MT):
            eng.wait_ge(o_gain, m + 1)
            g.tensor_tensor(on[:, m % 4, :], on[:, m % 4, :], lnb[:, :], ALU.add).then_inc(o_bias, 1)


def _tiles(w):
    n = w.shape[1] // P
    return w.reshape(KT, P, n, P).transpose(2, 1, 0, 3).reshape(n, P, D)


def _tables():
    i, j = np.arange(P)[:, None], np.arange(P)[None, :]
    one = lambda c: np.broadcast_to(c, (P, P)).astype(np.float32)
    cnt = np.ones((P, P), np.float32)
    for tile in range(2):
        for half in range(2):
            w = (2, 4, 8, 16)[2 * tile + half]
            cnt[HEAD * half:HEAD * half + HEAD, 16 * tile:16 * tile + 16] = w / np.minimum(np.arange(16) + 1, w)
    t = {"ident": one(i == j), "ones": one(i >= 0), "tri_le": one(i <= j), "mask_lt": one(i < j),
         "cap_lt": np.where(i < j, BIG, NEG), "cap_le": np.where(i <= j, BIG, NEG),
         "neg_ge": -one(i >= j), "neg_lt": -one(i < j),
         "rms_01": one(j < HEAD), "rms_10": one(i < HEAD), "rms_11": one((i < HEAD) == (j < HEAD)),
         "rms_12": one(i >= HEAD), "rms_21": one(j >= HEAD), "pool_cnt": cnt}
    return np.concatenate([t[k].astype(np.float32) for k in TABLES], axis=1)


def _columns(v):
    return v.reshape(-1, P).T


def kernel(**inputs):
    import concourse.bacc as bacc
    from concourse.bass_utils import run_bass_kernel_spmd

    g = {k: np.asarray(v) for k, v in inputs.items()}
    w_in = g["w_in"][0]
    dt_cols = np.pad(w_in[:, COL_DT:COL_Q], ((0, 0), (0, P - SSD_HEADS)))
    cols = np.concatenate([dt_cols if t == "dt" else
                           w_in[:, IN_COLS[t[0]] + P * int(t[1]):IN_COLS[t[0]] + P * int(t[1]) + P]
                           for t in IN_TILES], axis=1)
    x = g["x"][0]
    order = [k for c in range(CHUNKS) for t in range(PER_CHUNK) for k in (PER_CHUNK * c + t,
                                                                        FF_TILES + PER_CHUNK * c + t)]
    up = _tiles(g["ffn_w_up"][0])[order]
    pool = np.zeros((P, 2, P), np.float32)
    for k in range(4):
        r = slice(HEAD * (k % 2), HEAD * (k % 2) + HEAD)
        pool[r, k // 2, r] = g["pool_w"][0, k]
    pool_inv = np.repeat(np.array([[1 / 2, 1 / 8], [1 / 4, 1 / 16]], np.float32), HEAD, axis=0)
    lanes = lambda v, n: np.broadcast_to(np.tile(v, n), (P, n * len(v)))
    cw = g["ssd_conv_w"][0].reshape(CONV, 7, P).transpose(2, 1, 0).reshape(P, 28)
    fw = g["ffn_conv_w"][0].reshape(FF_CONV, 2 * FF_TILES, P).transpose(2, 1, 0)[:, order].reshape(P, -1)
    fb = _columns(g["ffn_conv_b"][0])[:, order]
    params = {"conv_w": cw, "conv_b": _columns(g["ssd_conv_b"][0]), "pool_scale": _columns(g["pool_scale"][0]),
              "pool_inv": pool_inv, "ssd_d": _columns(np.repeat(g["ssd_d"][0], HEAD)),
              "norm_w": _columns(g["ssd_norm_w"][0]), "dt_bias": lanes(g["ssd_dt_bias"][0], MT),
              "a_log": lanes(g["ssd_a_log"][0], MT), "ln1_g": _columns(g["ln1_g"][0]),
              "ln1_b": _columns(g["ln1_b"][0]), "ff_w": fw, "ff_b": fb}
    arrays = {
        "u_x": x.T.reshape(KT, P, S), "u_in": _tiles(cols), "u_out": g["w_out"][0].reshape(KT, P, D),
        "u_p": g["p"][0, 0].T.reshape(PLE_TILES, P, S), "u_proj": g["ple_w_proj"][0].reshape(PLE_TILES, P, D),
        "u_gate": _tiles(g["ple_w_gate"][0]), "u_up": up, "u_down": g["ffn_w_down"][0].reshape(FF_TILES, P, D),
        "x_nat": x.reshape(MT, P, D), "tables": _tables(), "pool_w": pool.reshape(P, 2 * P),
        "params": np.concatenate([params[k] for k in PARAM_SIZES], axis=1),
        "ln2_g": g["ln2_g"][0], "ln2_b": g["ln2_b"][0],
    }
    arrays = {k: np.ascontiguousarray(v) for k, v in arrays.items()}
    nc = bacc.Bacc("TRN2", target_bir_lowering=False, num_devices=1, dynamic_dma_scratch_size=1024)
    aps = {k: nc.dram_tensor(k, v.shape, mybir.dt.from_np(v.dtype), kind="ExternalInput").ap()
           for k, v in arrays.items()}
    out = nc.dram_tensor("out", (S, D), F32, kind="ExternalOutput").ap()
    with ExitStack() as ctx:
        build(nc, ctx, aps, out)
    r = run_bass_kernel_spmd(nc, [arrays], core_ids=[0])
    return r.results[0]["out"].reshape(1, S, D)
```

```python
from contextlib import ExitStack

import numpy as np

import concourse.bass as bass
from concourse import mybir

F32 = mybir.dt.float32
F32R = mybir.dt.float32r
I32 = mybir.dt.int32
SIGN = -2 ** 31
ALU = mybir.AluOpType
ACT = mybir.ActivationFunctionType

P = 128
D = 1024
S = 1024
HALF = 512
KT = D // P
MT = S // P
HEAD = 64
POOL_W = 256
SSD_W = 384
SSD_HEADS = 6
STATE = 128
CONV = 4
FF = 2816
FF_TILES = FF // P
PER_CHUNK = 2
CHUNKS = FF_TILES // PER_CHUNK
FF_CONV = 3
PLE_TILES = 2
ALPHA = 2.0 ** 0.25
LN_EPS = 1e-5
RMS_EPS = 1e-6
SCALE = HEAD ** -0.5
PAIRS = 3
BIG = 3.0e38
NEG = -3.0e4

COL_Z = POOL_W
COL_XBC = COL_Z + SSD_W
COL_DT = COL_XBC + SSD_W + 4 * STATE
COL_Q = COL_DT + SSD_HEADS
COL_K = COL_Q + 384
COL_V = COL_K + 384

H_TILES = ["x0", "x1", "x2", "B0", "B1", "C0", "C1", "z0", "z1", "z2", "p0", "p1"]
WINDOWS = [["v1", "q1", "k1", "x0", "x1", "x2"], ["v2", "q2", "k2", "B0", "B1", "C0"],
           ["dt", "C1", "z0", "z1", "z2", "p0", "p1"]]
IN_TILES = ["v0", "q0", "k0"] + [t for w in WINDOWS for t in w]
IN_COLS = {"q": COL_Q, "k": COL_K, "v": COL_V, "x": COL_XBC, "B": COL_XBC + SSD_W,
           "C": COL_XBC + SSD_W + 2 * STATE, "z": COL_Z, "p": 0}
TURNED = ["v0", "v1", "v2", "dt"]

UNITS = [("in", 0), ("in", 1)] + [("x", i) for i in range(KT)] + [("in", i) for i in range(2, len(IN_TILES))]
OUT_ORDER = [5, 6, 7, 0, 1, 2, 3, 4]
UNITS += [("out", i) for i in OUT_ORDER] + [("gate", 0)] + [("p", i) for i in range(PLE_TILES)]
UNITS += [("proj", i) for i in range(PLE_TILES)] + [("gate", i) for i in range(1, KT)]
FFN0 = len(UNITS)
UNITS += [("up", i) for i in range(4)]
for _c in range(1, CHUNKS - 1):
    UNITS += [("up", 4 * _c), ("down", 2 * _c - 2), ("down", 2 * _c - 1)] + [("up", 4 * _c + i) for i in (1, 2, 3)]
UNITS += [("up", 4 * (CHUNKS - 1) + i) for i in range(4)] + [("down", i) for i in range(FF_TILES - 4, FF_TILES)]
UNIT = {u: n for n, u in enumerate(UNITS)}
RAWS = 2
RINGS = 3
RING_OF = {}
for _n, _u in enumerate(UNITS):
    if _u[0] in ("in", "gate", "up", "down"):
        RING_OF[_n] = len(RING_OF)
FFN_R0 = RING_OF[FFN0]

TABLES = ["ident", "ones", "tri_le", "mask_lt", "cap_lt", "cap_le", "neg_ge", "neg_lt",
          "rms_0", "rms_1", "rms_2", "from_first", "from_last", "pool_cnt"]
STEPS = [(g, qh, kb, hd) for g in range(PAIRS) for qh in range(2)
         for kb in range(4 * qh + 3, -1, -1) for hd in range(2)]
NSTEP = len(STEPS)
PER_PAIR = NSTEP // PAIRS


def first_col(n):
    _, qh, kb, _ = STEPS[n]
    return max(0, P * kb - HALF * qh)


def on_diagonal(n):
    _, qh, kb, _ = STEPS[n]
    return kb >= 4 * qh


def raw_place(n):
    return n if n < UNIT[("x", 0)] else n - KT


def projection_plan():
    p = 0
    pro = []
    for name in ("v0", "q0", "k0"):
        for h in range(2):
            pro.append(("tile", name, h, p))
            p += 1
    for h in range(2):
        pro.append(("turn", 0, h, p))
        p += 1
    by_step = []
    for g, window in enumerate(WINDOWS):
        pieces = []
        for i, name in enumerate(window):
            for h in range(2):
                it = ("tile", name, h, p)
                p += 1
                pieces += [(it, 0, 2), (it, 1, 2)]
            if name == "z2":
                pieces.append((("sums", "sums", 0, p), 0, 1))
                p += 1
            if (name[0] == "q" and i == 1) or (name == "C1" and g == 2):
                for hh in range(2):
                    pieces.append((("turn", g + 1, hh, p), 0, 1))
                    p += 1
        for s in range(PER_PAIR):
            a, b = s * len(pieces) // PER_PAIR, (s + 1) * len(pieces) // PER_PAIR
            by_step.append(pieces[a:b])
    return pro, by_step


PROLOGUE, BY_STEP = projection_plan()
PLACE = {}
for _it in PROLOGUE + [x[0] for s in BY_STEP for x in s]:
    PLACE[(_it[1], _it[2]) if _it[0] != "turn" else ("turn%d" % _it[1], _it[2])] = _it[3]
DONE_AT = [[it for it, part, parts in s if part == parts - 1] for s in BY_STEP]
STARTS = {}
for _s, _ps in enumerate(BY_STEP):
    for _it, _part, _parts in _ps:
        if _it[0] == "tile" and _it[2] == 0 and _part == 0:
            STARTS[IN_TILES.index(_it[1])] = _s
SPLIT_AT = {}
for _r in range(5, len(IN_TILES)):
    SPLIT_AT.setdefault(STARTS[_r - 2] + 1, []).append(_r)
CONV_AT = [26, 31, 36, 50, 54, 58, 63]
DT_AT = 57
SUMS_AT = 2 + next(s for s, d in enumerate(DONE_AT) if any(it[0] == "sums" for it in d))

BY_RING = {r: n for n, r in RING_OF.items()}
QK_ORDER = [(it[1], it[2]) for it in PROLOGUE + [i for d in DONE_AT for i in d]
            if it[0] == "tile" and it[1][0] in "qk"]
TASKS = ["xt0", "xt1", "xt2", "xt3", "bt0", "bt1", "cb0", "cb1", "st0", "st1", "st2", "st3", "cu0", "cu1",
         "cu2", "cu3", "yy0", "cu4", "cu5", "yy1", "po0", "po1", "yy2", "rm0", "sp0", "sp1"]
TAIL = TASKS.index("rm0")


def task_place(name):
    pairs = [t % 4 if t < TAIL else 2 + (t - TAIL) % 2 for t in range(len(TASKS))]
    t = TASKS.index(name)
    return pairs[t], pairs[:t].count(pairs[t])


DTN = MT * SSD_HEADS
PARAM_SIZES = {"conv_w": 28, "conv_b": 7, "pool_scale": 2, "pool_inv": 2, "ssd_d": 3, "norm_w": 3, "dt_bias": DTN,
               "a_log": DTN, "rms_eps": 1, "ln1_g": KT, "ln1_b": KT, "ff_w": 3 * 2 * FF_TILES, "ff_b": 2 * FF_TILES}
PARAMS, N_PARAMS = {}, 0
for _k, _n in PARAM_SIZES.items():
    PARAMS[_k] = N_PARAMS
    N_PARAMS += _n


def build(nc, ctx, a, out):
    kb = 1024
    top = [2 * kb]

    def put(name, shape, dt=F32, at=None):
        size = -(-4 * int(np.prod(shape[1:])) // 32) * 32
        if at is None:
            at = top[0]
            top[0] += size
        assert at + size <= 229368, (name, at, size)
        return nc.alloc_sbuf_tensor_at(name, shape, dt, offset=at)

    def sem(name):
        return ctx.enter_context(nc.semaphore(name))

    raw = put("raw", [P, RAWS, D])
    wh = put("w_hi", [P, RINGS, D], F32R)
    wl = put("w_lo", [P, RINGS, D], F32R)
    tab = put("tables", [P, len(TABLES), P])
    neg_ge = put("neg_ge_r", [P, P], F32R)
    neg_lt = put("neg_lt_r", [P, P], F32R)
    pool_w = put("pool_w", [P, 2, P])
    par = put("params", [P, N_PARAMS])
    sm = put("small", [P, 10, DTN])
    st = put("ln_stats", [P, MT, 16])
    x0 = top[0]
    xh = put("x_hi", [P, KT, S], F32R)
    xl = put("x_lo", [P, KT, S], F32R)
    mh = put("mix_hi", [P, KT, S], F32R, x0)
    ml = put("mix_lo", [P, KT, S], F32R, x0 + 32 * kb)
    xdt = put("x_dt", [P, MT, SSD_W], F32, x0 + 2 * 4 * kb)
    xw = put("x_weighted", [P, MT, SSD_W], F32, x0 + (32 + 2 * 4) * kb)
    pa = put("pool_a", [P, S], F32, x0 + 32 * kb)
    pb = put("pool_b", [P, S], F32, x0 + 36 * kb)

    slot0 = top[0]

    def over(name, shape, first, dt=F32, of=0):
        assert first + (4 * int(np.prod(shape[1:])) + of * kb) / (4 * kb) <= 28, name
        return put(name, shape, dt, slot0 + (4 * first + of) * kb)

    stage = over("x_stage", [P, KT, S], 0)
    ht = over("h_tiles", [P, len(H_TILES), S], 1)
    sets = [13, 7]
    qh = [over("q_hi%d" % i, [P, S], sets[i], F32R) for i in range(2)]
    ql = [over("q_lo%d" % i, [P, S], sets[i] + 1, F32R) for i in range(2)]
    kh = [over("k_hi%d" % i, [P, S], sets[i] + 2, F32R) for i in range(2)]
    kl = [over("k_lo%d" % i, [P, S], sets[i] + 3, F32R) for i in range(2)]
    vn = [over("v_nat%d" % i, [P, MT, P], sets[i] + 4) for i in range(2)]
    vt = over("v_t", [P, S], 12)
    zs = over("z_scaled", [P, 3, HALF], 18)
    sph = over("sp_hi", [P, 3, HALF], 18, F32R, 6)
    spl = over("sp_lo", [P, 3, HALF], 18, F32R, 12)
    na = over("neg_abs", [P, 2, HALF], 18, F32, 18)
    u = over("weights", [P, 2, HALF], 18, F32, 22)
    sp = over("softplus", [P, HALF], 18, F32, 26)
    sb = over("sb_out", [P, PAIRS, S], 25)
    cv = over("conv", [P, 7, S], 0)
    bn = over("b_natural", [P, 2, MT, P], 13)
    hs = over("states", [P, MT, SSD_W], 15)
    cb = over("cb", [P, 2, S], 18)
    wt = over("decayed", [P, 2, S], 20)
    ce = over("c_scaled", [P, 2, S], 22)
    tmp = over("tmp", [P, S], 24)
    out_slots = {5: (25, 26), 6: (27, 13), 7: (14, 11), 0: (12, 15), 1: (16, 17), 2: (18, 19), 3: (20, 21),
                 4: (22, 23)}
    oh = [over("wo_hi%d" % k, [P, D], out_slots[k][0], F32R) for k in range(KT)]
    ol = [over("wo_lo%d" % k, [P, D], out_slots[k][1], F32R) for k in range(KT)]
    acc = over("acc", [P, KT, S], 0)
    yn = over("y_nat", [P, 2, D], 8)
    xn = over("x_nat", [P, D], 10)
    ph = over("p_hi", [P, PLE_TILES, S], 11, F32R)
    pl = over("p_lo", [P, PLE_TILES, S], 13, F32R)
    pwh = over("proj_hi", [P, PLE_TILES, D], 15, F32R)
    pwl = over("proj_lo", [P, PLE_TILES, D], 17, F32R)
    sig = over("sigmoid", [P, 2, S], 19)
    hh = over("h_hi", [P, PER_CHUNK, S], 11, F32R)
    hl = over("h_lo", [P, PER_CHUNK, S], 13, F32R)
    cf = over("conv_ff", [P, 2, S], 21)
    hf = over("h_ff", [P, S], 24)
    lng = over("ln2_gain", [P, D], 8)
    lnb = over("ln2_bias", [P, D], 9)
    on = over("o_norm", [P, 4, D], 11)
    h2h = over("last_h_hi", [P, PER_CHUNK, S], 15, F32R)
    h2l = over("last_h_lo", [P, PER_CHUNK, S], 17, F32R)

    ps = ctx.enter_context(nc.psum_tensor("ps", [P, 8, HALF], F32))

    def two(i):
        return ps[:, 2 * i:2 * i + 2, :].rearrange("p b n -> p (b n)")

    def table(name):
        return tab[:, TABLES.index(name), :]

    def param(name, i=0, n=1):
        c = PARAMS[name] + i
        return par[:, c:c + n]

    const_in = sem("const_in")
    const_r = sem("const_r")
    x_raw = [sem("x_raw%d" % i) for i in range(KT)]
    raw_in = [sem("raw_in%d" % i) for i in range(RAWS)]
    hi_done = sem("hi_done")
    split_done = sem("split_done")
    barrier = sem("barrier")
    p_full = sem("p_full")
    p_free = [sem("p_free%d" % i) for i in range(2)]
    qk_hi = sem("qk_hi")
    z_full, zs_done, na_done = sem("z_full"), sem("zs_done"), sem("na_done")
    e_done, l_done, lo_done = sem("e_done"), sem("l_done"), sem("lo_done")
    tri_full, u_done, w_done, av_done = sem("tri_full"), sem("u_done"), sem("w_done"), sem("av_done")
    o_out = sem("o_out")
    dve_chain = sem("dve_chain")
    pool_chain = sem("pool_chain")
    dt_v = sem("dt_v")
    dt_a = sem("dt_a")
    tap_done, conv_done, silu_done = sem("tap_done"), sem("conv_done"), sem("silu_done")
    d_full = sem("d_full")
    d_free = [sem("d_free%d" % i) for i in range(4)]
    decay_done = sem("decay_done")
    arg_done, wexp_done, wt_done = sem("arg_done"), sem("wexp_done"), sem("wt_done")
    xw_done = sem("xw_done")
    hg_done, sq_done, ln_done, nrm_done = sem("hg_done"), sem("sq_done"), sem("ln_done"), sem("nrm_done")
    rms_done = sem("rms_done")
    mixh = sem("mix_hi_done")
    sb_split = sem("sb_split")
    pooled = sem("pooled")
    x_in, y_full, y_read, v_eps, v_sqrt = sem("x_in"), sem("y_full"), sem("y_read"), sem("v_eps"), sem("v_sqrt")
    y_norm, t_full, x1_done, x1_split = sem("y_norm"), sem("t_full"), sem("x1_done"), sem("x1_split")
    u_full, u_free, sig_done = sem("u_full"), sem("u_free"), sem("sig_done")
    tap_ff, tap_mid, silu_ff, prod_mid, h_done = (
        sem("tap_ff"), sem("tap_mid"), sem("silu_ff"), sem("prod_mid"), sem("h_done"))
    dn_full, dn_added = sem("dn_full"), sem("dn_added")
    ln_in, o_full, o_eps, o_sqrt, o_aff, o_nrm, o_gain, o_bias = (
        sem("ln_in"), sem("o_full"), sem("o_eps"), sem("o_sqrt"), sem("o_aff"), sem("o_nrm"), sem("o_gain"),
        sem("o_bias"))
    stored = [sem("stored%d" % i) for i in range(4)]

    def meet(eng, k):
        eng.drain().then_inc(barrier, 1)
        eng.wait_ge(barrier, 4 * k)

    def wait_evacuated(eng, p):
        eng.wait_ge(p_free[p % 2], p // 2 + 1)

    def bank_of(p):
        return ps[:, p if p < 4 else p % 2, :]

    def unit_place(n, lo):
        kind, i = UNITS[n]
        if kind == "x":
            return (xl if lo else xh)[:, i, :]
        if kind == "out":
            return (ol if lo else oh)[i][:, :]
        if kind == "p":
            return (pl if lo else ph)[:, i, :]
        if kind == "proj":
            return (pwl if lo else pwh)[:, i, :]
        return (wl if lo else wh)[:, RING_OF[n] % RINGS, :]

    def wait_ring_free(eng, n, it=0):
        if n not in RING_OF or RING_OF[n] < RINGS:
            return
        kind, i = UNITS[BY_RING[RING_OF[n] - RINGS]]
        if kind == "in":
            eng.wait_ge(p_full, PLACE[(IN_TILES[i], 1)] + 1)
        elif kind == "gate":
            eng.wait_ge(u_full, 2 * i + 1)
        elif kind == "up":
            eng.wait_ge(u_full, 2 * KT + i + 1 + 4 * it)
        else:
            eng.wait_ge(dn_full, 16 * (i // 2 + 1) + 16 * it)

    def unit_raw(n):
        return stage[:, UNITS[n][1], :] if UNITS[n][0] == "x" else raw[:, n % RAWS, :]

    def hi(n, it=0):
        if UNITS[n][0] == "x":
            nc.scalar.wait_ge(x_raw[UNITS[n][1]], 16)
        else:
            nc.scalar.wait_ge(raw_in[n % RAWS], 16 * (raw_place(n) // RAWS + 1) + 16 * 6 // RAWS * it)
        wait_ring_free(nc.scalar, n, it)
        nc.scalar.activation(unit_place(n, False), unit_raw(n), ACT.Copy).then_inc(hi_done, 1)

    def lo(n, it=0, eng=nc.vector):
        eng.wait_ge(hi_done, n + 1 + 6 * it)
        eng.tensor_tensor(unit_place(n, True), unit_raw(n), unit_place(n, False).bitcast(F32),
                                ALU.subtract).then_inc(split_done, 1)

    block = ctx.enter_context(nc.Block())

    @block.sync
    def _(eng):
        def unit_source(n):
            kind, i = UNITS[n]
            return a["u_" + kind][i]

        def load(n):
            if raw_place(n) >= RAWS:
                eng.wait_ge(split_done, n - RAWS + 1 if raw_place(n) >= 2 * RAWS else n - KT - RAWS + 1)
            eng.dma_start(raw[:, n % RAWS, :], unit_source(n)).then_inc(raw_in[n % RAWS], 16)

        def load_x(i):
            eng.dma_start(stage[:, i, :], unit_source(UNIT[("x", i)])).then_inc(x_raw[i], 16)

        load(0)
        load_x(0)
        load(1)
        for i in range(1, KT):
            load_x(i)
        eng.dma_start(tab[:, :, :].rearrange("p t n -> p (t n)"), a["tables"]).then_inc(const_in, 16)
        eng.dma_start(par[:, :], a["params"]).then_inc(const_in, 16)
        eng.dma_start(pool_w[:, :, :].rearrange("p t n -> p (t n)"), a["pool_w"]).then_inc(const_in, 16)
        for n in range(UNIT[("in", 2)], UNIT[("out", OUT_ORDER[-1])] + 1):
            load(n)
        eng.wait_ge(hg_done, 3)
        for m in range(MT):
            if m:
                eng.wait_ge(y_read, m)
            eng.dma_start(xn[:, :], a["x_nat"][m]).then_inc(x_in, 16)
            if m < 2:
                load(UNIT[("gate", 0)] + m)
        for n in range(UNIT[("p", 1)], FFN0 + 4):
            load(n)
        eng.wait_ge(t_full, MT)
        eng.dma_start(lng[:, :], a["ln2_g"].partition_broadcast(P)).then_inc(ln_in, 16)
        eng.dma_start(lnb[:, :], a["ln2_b"].partition_broadcast(P)).then_inc(ln_in, 16)
        n0 = FFN0 + 4
        with eng.Fori(0, CHUNKS - 2) as it:
            for j in range(6):
                n = n0 + j
                eng.wait_ge(split_done, n - RAWS + 1 + 6 * it)
                kind, i = UNITS[n]
                src = a["u_up"][i + 4 * it] if kind == "up" else a["u_down"][i + 2 * it]
                eng.dma_start(raw[:, n % RAWS, :], src).then_inc(raw_in[n % RAWS], 16)
        for n in range(len(UNITS) - 8, len(UNITS)):
            load(n)
        for m in range(MT):
            eng.wait_ge(o_bias, m + 1)
            eng.dma_start(out[m * P:(m + 1) * P, :], on[:, m % 4, :]).then_inc(stored[m % 4], 16)
        for i in range(4):
            eng.wait_ge(stored[i], 16 * MT // 4)

    @block.tensor
    def _(eng):
        mm = nc.tensor.matmul

        def three(dst, w_hi, w_lo, x_hi, x_lo, first, last):
            mm(dst, w_hi, x_hi, start=first, stop=False)
            mm(dst, w_hi, x_lo, start=False, stop=False)
            return mm(dst, w_lo, x_hi, start=False, stop=last)

        def piece(it, part, parts):
            kind, name, h, p = it
            bank = bank_of(p)
            if part == 0 and p >= 4:
                wait_evacuated(eng, p - 2 if p >= 6 else p - 4)
            if kind == "tile":
                i = IN_TILES.index(name)
                n = UNIT[("in", i)]
                slot = RING_OF[n] % RINGS
                if part == 0 and h == 0:
                    eng.wait_ge(split_done, n + 1)
                for kt in range(part * KT // parts, (part + 1) * KT // parts):
                    c = slice(kt * P, (kt + 1) * P)
                    s_ = slice(h * HALF, (h + 1) * HALF)
                    last = three(bank, wh[:, slot, c], wl[:, slot, c], xh[:, kt, s_], xl[:, kt, s_],
                                 kt == 0, kt == KT - 1)
            elif kind == "turn":
                for hh_ in range(2):
                    wait_evacuated(eng, PLACE[(TURNED[name], hh_)])
                for j in range(4):
                    last = nc.tensor.transpose(bank[:, j * P:(j + 1) * P], vt[:, (4 * h + j) * P:(4 * h + j + 1) * P],
                                               table("ident"))
            else:
                eng.wait_ge(dt_v, 2)
                mm(bank[:, 0:DTN], table("tri_le"), sm[:, 5, :], start=True, stop=True)
                last = mm(bank[:, 64:64 + DTN], table("ones"), sm[:, 5, :], start=True, stop=True)
            if part == parts - 1:
                last.then_inc(p_full, 1)

        def z_scores(n):
            g, q_half, key, hd = STEPS[n]
            if n % PER_PAIR == 0:
                for name in ("q%d" % g, "k%d" % g):
                    for h in range(2):
                        wait_evacuated(eng, PLACE[(name, h)])
            if n >= 2:
                eng.wait_ge(zs_done, n - 1)
            r = slice(HEAD * hd, HEAD * hd + HEAD)
            kc = slice(key * P, (key + 1) * P)
            c0 = first_col(n)
            qc = slice(q_half * HALF + c0, (q_half + 1) * HALF)
            s_ = g % 2
            three(ps[:, 2 + n % 2, c0:], kh[s_][r, kc], kl[s_][r, kc], qh[s_][r, qc], ql[s_][r, qc],
                  True, True).then_inc(z_full, 1)

        def suffix(n):
            hd, c0 = STEPS[n][3], first_col(n)
            first = STEPS[n][2] == 4 * STEPS[n][1] + 3
            eng.wait_ge(lo_done, n + 1)
            dst = ps[:, 4 + hd, c0:]
            mm(dst, neg_ge[:, :], sph[:, n % 3, c0:], start=first, stop=False, skip_group_check=True)
            mm(dst, neg_ge[:, :], spl[:, n % 3, c0:], start=False, stop=True,
               skip_group_check=True).then_inc(tri_full, 1)

        def rest_and_values(n):
            g, q_half, key, hd = STEPS[n]
            c0 = first_col(n)
            eng.wait_ge(u_done, n + 1)
            if key:
                dst = ps[:, 4 + hd, c0:]
                mm(dst, neg_lt[:, :], sph[:, n % 3, c0:], start=False, stop=False, skip_group_check=True)
                mm(dst, neg_lt[:, :], spl[:, n % 3, c0:], start=False, stop=True, skip_group_check=True)
            first = key == 4 * q_half + 3
            o = 2 * g + q_half
            if first and o >= 2:
                eng.wait_ge(o_out, o - 1)
            if first and q_half == 0:
                for h in range(2):
                    wait_evacuated(eng, PLACE[("turn%d" % g, h)])
            eng.wait_ge(w_done, n + 1)
            r = slice(HEAD * hd, HEAD * hd + HEAD)
            mm(ps[r, 6 + o % 2, c0:], vn[g % 2][:, key, r], u[:, n % 2, c0:], start=first, stop=True,
               skip_group_check=True).then_inc(av_done, 1)

        for kt in range(KT):
            eng.wait_ge(split_done, UNIT[("x", kt)] + 1)
            c = slice(kt * P, (kt + 1) * P)
            for kind, name, h, p in PROLOGUE[:4]:
                s_ = slice(h * HALF, (h + 1) * HALF)
                i = IN_TILES.index(name)
                last = three(bank_of(p), wh[:, i, c], wl[:, i, c], xh[:, kt, s_], xl[:, kt, s_],
                             kt == 0, kt == KT - 1)
                if kt == KT - 1:
                    last.then_inc(p_full, 1)
        for it in PROLOGUE[4:]:
            if it[0] == "turn":
                eng.wait_ge(const_in, 48)
                eng.wait_ge(const_r, 1)
            piece(it, 0, 1)
        for n in range(-2, NSTEP):
            if n >= 0:
                suffix(n)
            if n + 2 < NSTEP:
                z_scores(n + 2)
            if n >= 0:
                for pc in BY_STEP[n]:
                    piece(*pc)
                rest_and_values(n)
        meet(eng, 1)

        def bank_pair(name):
            pair, before = task_place(name)
            if before:
                eng.wait_ge(d_free[pair], before)
            return two(pair)

        def turn(dst, src):
            return nc.tensor.transpose(dst, src, table("ident"))

        def evacuated(name):
            pair, before = task_place(name)
            eng.wait_ge(d_free[pair], before + 1)

        def out_rows(m, kts):
            if kts[0] == OUT_ORDER[0] and m < 2:
                pairs = [task_place(name) for name in TASKS]
                eng.wait_ge(d_free[m], max(b + 1 for q, b in pairs if q == m))
                eng.wait_ge(sb_split, 3)
            t = slice(m * P, (m + 1) * P)
            for kt in kts:
                eng.wait_ge(split_done, UNIT[("out", kt)] + 1)
                if kt < 2:
                    evacuated("po%d" % kt)
                for h in range(2):
                    c = slice(h * HALF, (h + 1) * HALF)
                    last = three(two(m % 2)[:, c], mh[:, kt, t], ml[:, kt, t], oh[kt][:, c], ol[kt][:, c],
                                 kt == OUT_ORDER[0], kt == OUT_ORDER[-1])
            return last

        for name in TASKS:
            kind, i = name[:2], int(name[2])
            if kind == "cu":
                eng.wait_ge(dt_v, 2)
            elif kind == "bt":
                eng.wait_ge(silu_done, 3 + i + 1)
            elif kind == "cb":
                eng.wait_ge(silu_done, 5 + i + 1)
            elif kind == "xt":
                eng.wait_ge(silu_done, 3)
            elif kind == "st":
                eng.wait_ge(xw_done, 2 * (i + 1))
                evacuated("bt1")
            elif kind == "yy":
                eng.wait_ge(wt_done, 2 * (i + 1))
                evacuated("st3")
            elif kind == "po":
                eng.wait_ge(pooled, 2)
            elif kind == "rm":
                out_rows(0, (5, 6))
                out_rows(1, (5, 6))
                eng.wait_ge(sq_done, 3)
            elif kind == "sp":
                if i == 0:
                    out_rows(0, (7, 0))
                    out_rows(1, (7, 0))
                eng.wait_ge(rms_done, 1)
            dst = bank_pair(name)
            if kind == "cu":
                for c in range(MT):
                    col = sm[:, 5, c * SSD_HEADS + i:c * SSD_HEADS + i + 1]
                    last = mm(dst[:, c * P:(c + 1) * P], col.broadcast_to([P, P]), table("tri_le"),
                              start=True, stop=True)
            elif kind == "bt":
                for c in range(MT):
                    last = turn(dst[:, c * P:(c + 1) * P], cv[:, 3 + i, c * P:(c + 1) * P])
            elif kind == "cb":
                for c in range(MT):
                    t = slice(c * P, (c + 1) * P)
                    last = mm(dst[:, t], cv[:, 3 + i, t], cv[:, 5 + i, t], start=True, stop=True)
            elif kind == "xt":
                for c in range(2):
                    for j in range(3):
                        last = turn(dst[:, c * HALF + j * P:c * HALF + (j + 1) * P],
                                    cv[:, j, (2 * i + c) * P:(2 * i + c + 1) * P])
            elif kind == "st":
                for c in range(2 if i < 3 else 1):
                    for g in range(2):
                        w = SSD_W // 2
                        last = mm(dst[:, c * HALF + g * w:c * HALF + (g + 1) * w], bn[:, g, 2 * i + c, :],
                                  xw[:, 2 * i + c, g * w:(g + 1) * w], start=True, stop=True)
            elif kind == "yy":
                for c in range(MT):
                    t = slice(c * P, (c + 1) * P)
                    for hd in range(2):
                        r = slice(HEAD * hd, HEAD * hd + HEAD)
                        f = slice((2 * i + hd) * HEAD, (2 * i + hd + 1) * HEAD)
                        mm(dst[r, t], xdt[:, c, f], wt[:, hd, t], start=True, stop=False)
                        last = mm(dst[r, t], hs[:, c, f], ce[:, hd, t], start=False, stop=True)
            elif kind == "po":
                for h in range(2):
                    s_ = slice(h * HALF, (h + 1) * HALF)
                    last = mm(dst[:, s_], pool_w[:, i, :], ht[:, 10 + i, s_], start=True, stop=True)
            elif kind == "rm":
                for h in range(2):
                    s_ = slice(h * HALF, (h + 1) * HALF)
                    for j in range(3):
                        last = mm(dst[:, s_], table("rms_%d" % j), cv[:, 3 + j, s_], start=j == 0, stop=j == 2)
            elif kind == "sp":
                for h in range(2):
                    s_ = slice(h * HALF, (h + 1) * HALF)
                    last = mm(dst[:, s_], table(("from_first", "from_last")[i]), tmp[:, s_], start=True, stop=True)
            last.then_inc(d_full, 1)
        out_rows(0, (1,))
        out_rows(1, (1,))
        meet(eng, 2)

        def back(m):
            eng.wait_ge(y_norm, m + 1)
            if m >= 2:
                eng.wait_ge(x1_done, m - 1)
            dst = two(2 + m % 2)
            for kt in range(KT):
                last = turn(dst[:, kt * P:(kt + 1) * P], yn[:, m % 2, kt * P:(kt + 1) * P])
            last.then_inc(t_full, 1)

        for m in range(MT):
            if m >= 2:
                eng.wait_ge(y_read, m - 1)
            out_rows(m, (2, 3, 4) if m < 2 else OUT_ORDER).then_inc(y_full, 1)
            if m:
                back(m - 1)

        def column_tile(item, slot, n, it=0, halves=(0, 1)):
            eng.wait_ge(split_done, n + 1 + 6 * it)
            for h in halves:
                s_ = slice(h * HALF, (h + 1) * HALF)
                for kt in range(KT):
                    c = slice(kt * P, (kt + 1) * P)
                    last = three(two(item % 2)[:, s_], wh[:, slot, c], wl[:, slot, c], mh[:, kt, s_], ml[:, kt, s_],
                                 kt == 0, kt == KT - 1)
            if 1 in halves:
                last.then_inc(u_full, 1)

        def gate_item(j, halves=(0, 1)):
            n = UNIT[("gate", j)]
            column_tile(2 * j, RING_OF[n] % RINGS, n, 0, halves)

        def proj_item(j):
            c = slice(j * P, (j + 1) * P)
            for h in range(2):
                s_ = slice(h * HALF, (h + 1) * HALF)
                for i in range(PLE_TILES):
                    last = three(two(1)[:, s_], pwh[:, i, c], pwl[:, i, c], ph[:, i, s_], pl[:, i, s_],
                                 i == 0, i == PLE_TILES - 1)
            last.then_inc(u_full, 1)

        eng.wait_ge(x1_split, MT // 2)
        gate_item(0, (0,))
        back(MT - 1)
        eng.wait_ge(x1_split, MT)
        gate_item(0, (1,))
        eng.wait_ge(split_done, UNIT[("proj", 1)] + 1)
        eng.wait_ge(y_read, MT)
        proj_item(0)
        for j in range(1, KT):
            eng.wait_ge(sig_done, j)
            gate_item(j)
            eng.wait_ge(u_free, 2 * j - 1)
            proj_item(j)

        def up(t, n, it=0):
            if t == 0:
                eng.wait_ge(sig_done, KT)
            else:
                eng.wait_ge(u_free, 2 * KT + t - 1 + 4 * it)
            column_tile(2 * KT + t, RING_OF[n] % RINGS, n, it)

        def turn_back(m):
            if m in (0, MT // 2):
                eng.wait_ge(dn_added, 16 * (CHUNKS - 1) + 8 + 8 * (m // 4))
            if m == 0:
                eng.wait_ge(u_free, 2 * KT + 4 * CHUNKS)
            elif m >= 2:
                eng.wait_ge(o_nrm, m - 1)
            for kt in range(KT):
                last = turn(two(m % 2)[:, kt * P:(kt + 1) * P], acc[:, kt, m * P:(m + 1) * P])
            last.then_inc(o_full, 1)

        def down(n, d, it=0, by_half=False):
            hi_, lo_ = (h2h, h2l) if by_half else (hh, hl)

            def part(k, i, first, last):
                j, h = (k % 8, k // 8) if by_half else (k // 2, k % 2)
                s_, c = slice(h * HALF, (h + 1) * HALF), slice(j * P, (j + 1) * P)
                slot = (RING_OF[n] + i) % RINGS
                return three(ps[:, 4 + k % 4, :], wh[:, slot, c], wl[:, slot, c], hi_[:, i, s_], lo_[:, i, s_],
                             first, last)

            if by_half:
                eng.wait_ge(split_done, n + 1)
                eng.wait_ge(h_done, d // 8 + 2)
                for k in range(4):
                    eng.wait_ge(dn_added, d + k - 3)
                    part(k, 0, True, False)
            eng.wait_ge(split_done, n + 2 + 6 * it)
            eng.wait_ge(h_done, d // 8 + 2 + 2 * it)
            for k in range(16):
                if by_half and k in (11, 12, 14, 15):
                    turn_back(k - 11 if k < 13 else k - 12)
                if d + k >= 4 and not (by_half and k < 4):
                    eng.wait_ge(dn_added, d + k - 3 + 16 * it)
                if not (by_half and k < 4):
                    part(k, 0, True, False)
                part(k, 1, False, True).then_inc(dn_full, 1)

        for t in range(4):
            up(t, FFN0 + t)
        n1 = FFN0 + 4

        def chunk(c, n, it=0):
            up(4 * c, n, it)
            down(n + 1, 16 * (c - 1), it)
            for t in (1, 2, 3):
                up(4 * c + t, n + 2 + t, it)

        chunk(1, n1)
        with eng.Fori(0, CHUNKS - 3) as it:
            chunk(2, n1 + 6, it)
        n = len(UNITS) - 8
        for t in range(4):
            up(4 * (CHUNKS - 1) + t, n + t)
        down(n + 4, 16 * (CHUNKS - 2))
        down(len(UNITS) - 2, 16 * (CHUNKS - 1), by_half=True)
        for m in range(MT // 2, MT):
            turn_back(m)

    @block.scalar
    def _(eng):
        act = nc.scalar.activation

        def evacuate(it):
            kind, name, h, p = it
            if kind == "sums" or (kind == "turn" and name == 3):
                return
            eng.wait_ge(p_full, p + 1)
            bank = bank_of(p)
            s_ = slice(h * HALF, (h + 1) * HALF)
            if kind == "turn":
                act(vn[name % 2][:, 4 * h:4 * h + 4, :].rearrange("p m n -> p (m n)"), bank,
                    ACT.Copy).then_inc(p_free[p % 2], 1)
            elif name in H_TILES:
                if name == "p1":
                    for hh_ in range(2):
                        wait_evacuated(eng, PLACE[("turn3", hh_)])
                act(ht[:, H_TILES.index(name), s_], bank, ACT.Copy).then_inc(p_free[p % 2], 1)
            elif name in TURNED:
                g = TURNED.index(name)
                if g:
                    for hh_ in range(2):
                        wait_evacuated(eng, PLACE[("turn%d" % (g - 1), hh_)])
                act(vt[:, s_], bank, ACT.Copy).then_inc(p_free[p % 2], 1)
            else:
                g = int(name[1])
                act((qh if name[0] == "q" else kh)[g % 2][:, s_], bank, ACT.Copy).then_inc(qk_hi, 1)

        for n in range(UNIT[("in", 2)]):
            hi(n)
        eng.wait_ge(const_in, 48)
        act(neg_ge[:, :], table("neg_ge"), ACT.Copy)
        act(neg_lt[:, :], table("neg_lt"), ACT.Copy).then_inc(const_r, 1)
        nc.scalar.preload_act_table_set("natural_log_exp_and_others")
        hi(UNIT[("in", 2)])
        for it in PROLOGUE[:4]:
            evacuate(it)
        hi(UNIT[("in", 3)])
        hi(UNIT[("in", 4)])
        for it in PROLOGUE[4:]:
            evacuate(it)
        for n in range(-2, NSTEP + 1):
            if 0 <= n + 1 < NSTEP:
                k, c0 = n + 1, first_col(n + 1)
                eng.wait_ge(na_done, k + 1)
                act(na[:, k % 2, c0:], na[:, k % 2, c0:], ACT.Exp).then_inc(e_done, 1)
                eng.wait_ge(e_done, k + 1)
                act(na[:, k % 2, c0:], na[:, k % 2, c0:], ACT.Ln, bias=1.0).then_inc(l_done, 1)
            if 0 <= n < NSTEP:
                c0 = first_col(n)
                eng.wait_ge(u_done, n + 1)
                act(u[:, n % 2, c0:], u[:, n % 2, c0:], ACT.Exp).then_inc(w_done, 1)
            if 0 <= n + 2 < NSTEP:
                k, c0 = n + 2, first_col(n + 2)
                eng.wait_ge(z_full, k + 1)
                if k >= 3:
                    eng.wait_ge(u_done, k - 2)
                act(zs[:, k % 3, c0:], ps[:, 2 + k % 2, c0:], ACT.Copy, scale=SCALE).then_inc(zs_done, 1)
            for it in (DONE_AT[n - 1] if 1 <= n <= NSTEP else []):
                evacuate(it)
            for r in SPLIT_AT.get(n, []):
                hi(UNIT[("in", r)])
            if n in CONV_AT:
                j = CONV_AT.index(n)
                for hh_ in range(2):
                    wait_evacuated(eng, PLACE[(H_TILES[j], hh_)])
                if j:
                    eng.wait_ge(conv_done, j)
                act(cv[:, j, :], ht[:, j, :], ACT.Identity, scale=param("conv_w", 4 * j + 3),
                    bias=param("conv_b", j)).then_inc(tap_done, 1)
            if n == DT_AT + 1:
                eng.wait_ge(dt_v, 1)
                act(sm[:, 2, :], sm[:, 1, :], ACT.Exp).then_inc(dt_a, 1)
                eng.wait_ge(dt_a, 1)
                act(sm[:, 2, :], sm[:, 2, :], ACT.Ln, bias=1.0)
                act(sm[:, 4, :], param("a_log", 0, DTN), ACT.Exp).then_inc(dt_a, 1)
            if n == SUMS_AT:
                eng.wait_ge(decay_done, 1)
                act(sm[:, 8, :], sm[:, 8, :], ACT.Exp).then_inc(dt_a, 1)
                act(sm[:, 9, :], sm[:, 7, :], ACT.Exp).then_inc(dt_a, 1)
            if n >= 1 and STEPS[n - 1][2] == 0 and STEPS[n - 1][3] == 1:
                g, q_half = STEPS[n - 1][:2]
                eng.wait_ge(av_done, n)
                act(sb[:, g, q_half * HALF:(q_half + 1) * HALF], ps[:, 6 + q_half, :],
                    ACT.Copy).then_inc(o_out, 1)
        meet(eng, 1)

        def task(name):
            eng.wait_ge(d_full, TASKS.index(name) + 1)
            pair = task_place(name)[0]
            return two(pair), d_free[pair]

        for j in range(7):
            act(cv[:, j, :], cv[:, j, :], ACT.Silu).then_inc(silu_done, 1)
        for g in range(2):
            src, free = task("bt%d" % g)
            act(bn[:, g, :, :].rearrange("p m n -> p (m n)"), src, ACT.Copy).then_inc(free, 1)
        for j in range(3):
            act(ht[:, 7 + j, :], ht[:, 7 + j, :], ACT.Silu).then_inc(silu_done, 1)
        for g in range(2):
            src, free = task("cb%d" % g)
            act(cb[:, g, :], src, ACT.Copy).then_inc(free, 1)
        def exponents(h):
            eng.wait_ge(arg_done, h + 1)
            if h >= 2:
                eng.wait_ge(d_full, TASKS.index("yy%d" % (h // 2 - 1)) + 1)
            act(wt[:, h % 2, :], tmp[:, :], ACT.Exp).then_inc(wexp_done, 1)
            src, free = task("cu%d" % h)
            act(ce[:, h % 2, :], src, ACT.Exp).then_inc(free, 1)

        def squared(i):
            eng.wait_ge(hg_done, i + 1)
            act(cv[:, 3 + i, :], cv[:, i, :], ACT.Square).then_inc(sq_done, 1)

        exponents(0)
        exponents(1)
        eng.wait_ge(sb_split, 3)
        hi(UNIT[("out", 5)])
        eng.wait_ge(d_full, TASKS.index("st3") + 1)
        hi(UNIT[("out", 6)])
        exponents(2)
        exponents(3)
        exponents(4)
        exponents(5)
        squared(0)
        for k in range(2):
            src, free = task("po%d" % k)
            act(mh[:, k, :], src, ACT.Copy, scale=param("pool_scale", k)).then_inc(mixh, 1)
        hi(UNIT[("out", 7)])
        squared(1)
        squared(2)
        hi(UNIT[("out", 0)])
        hi(UNIT[("out", 1)])
        src, free = task("rm0")
        act(tmp[:, :], src, ACT.Ln, scale=1.0 / (SSD_W // 2), bias=param("rms_eps")).then_inc(free, 1)
        eng.wait_ge(free, task_place("rm0")[1] + 1)
        act(tmp[:, :], tmp[:, :], ACT.Exp, scale=-0.5).then_inc(rms_done, 1)
        for k in (2, 3, 4):
            hi(UNIT[("out", k)])
        for i in (1, 0, 2):
            eng.wait_ge(nrm_done, (1, 0, 2).index(i) + 1)
            act(mh[:, 2 + i, :], cv[:, i, :], ACT.Copy).then_inc(mixh, 1)
        meet(eng, 2)

        def gain_bias(m):
            eng.wait_ge(t_full, m + 1)
            for kt in range(KT):
                last = act(acc[:, kt, m * P:(m + 1) * P], two(2 + m % 2)[:, kt * P:(kt + 1) * P], ACT.Identity,
                           scale=param("ln1_g", kt), bias=param("ln1_b", kt))
            last.then_inc(x1_done, 1)

        hi(UNIT[("gate", 0)])
        for m in range(MT):
            eng.wait_ge(v_eps, m + 1)
            act(st[:, m, 15:16], st[:, m, 14:15], ACT.Sqrt).then_inc(v_sqrt, 1)
            if m:
                gain_bias(m - 1)
        for i in range(PLE_TILES):
            hi(UNIT[("p", i)])
        gain_bias(MT - 1)

        for i in range(PLE_TILES):
            hi(UNIT[("proj", i)])
        hi(UNIT[("gate", 1)])
        for j in range(KT):
            if j + 2 < KT:
                hi(UNIT[("gate", j + 2)])
            else:
                hi(FFN0 + j + 2 - KT)
            eng.wait_ge(u_full, 2 * j + 1)
            if j >= 2:
                eng.wait_ge(u_free, 2 * j - 2)
            act(sig[:, j % 2, :], two(0), ACT.Sigmoid).then_inc(sig_done, 1)

        def tap(c, t, it=0):
            item = 2 * KT + 4 * c + t
            eng.wait_ge(u_full, item + 1 + 4 * it)
            if c or t >= 2:
                eng.wait_ge(h_done, 2 * c + t // 2 + 2 * it)
            w, b = PARAMS["ff_w"] + 3 * (4 * c + t) + 2, PARAMS["ff_b"] + 4 * c + t
            act(cf[:, t % 2, :], two(item % 2), ACT.Identity, scale=column(w, 12, it),
                bias=column(b, 4, it)).then_inc(tap_ff, 1)

        def column(c, step, it):
            return par[:, c:c + 1] if isinstance(it, int) else par[:, bass.ds(c + step * it, 1)]

        def gate(c, i, it=0):
            eng.wait_ge(u_free, 2 * KT + 4 * c + 2 * i + 1 + 4 * it)
            act(cf[:, 0, :], cf[:, 0, :], ACT.Silu).then_inc(silu_ff, 1)

        for n in (2, 3):
            hi(FFN0 + n)
        tap(0, 0)
        gate(0, 0)
        tap(0, 1)
        hi(FFN0 + 4)
        tap(0, 2)
        gate(0, 1)
        hi(FFN0 + 5)
        tap(0, 3)
        hi(FFN0 + 6)

        def chunk(c, n, it=0):
            tap(c, 0, it)
            hi(n + 3, it)
            gate(c, 0, it)
            hi(n + 4, it)
            hi(n + 5, it)
            tap(c, 1, it)
            hi(n + 6, it)
            tap(c, 2, it)
            gate(c, 1, it)
            hi(n + 7, it)
            tap(c, 3, it)
            hi(n + 8, it)

        n1 = FFN0 + 4
        chunk(1, n1)
        with eng.Fori(0, CHUNKS - 3) as it:
            chunk(2, n1 + 6, it)
        c, n = CHUNKS - 1, len(UNITS) - 8
        tap(c, 0)
        hi(n + 3)
        gate(c, 0)
        tap(c, 1)
        hi(n + 4)
        tap(c, 2)
        gate(c, 1)
        hi(n + 5)
        tap(c, 3)
        hi(n + 6)
        hi(n + 7)

        for m in range(MT):
            eng.wait_ge(o_eps, m + 1)
            act(st[:, m, 15:16], st[:, m, 14:15], ACT.Sqrt).then_inc(o_sqrt, 1)
            eng.wait_ge(o_aff, m + 1)
            if m >= 4:
                eng.wait_ge(stored[m % 4], 16 * (m // 4))
            act(on[:, m % 4, :], two(m % 2), ACT.Identity, scale=st[:, m, 13:14],
                bias=st[:, m, 12:13]).then_inc(o_nrm, 1)

    @block.vector
    def _(eng):
        v = nc.vector
        chained = [0]

        def link(ins):
            chained[0] += 1
            ins.then_inc(dve_chain, 1)
            eng.wait_ge(dve_chain, chained[0])

        def evacuate(it):
            kind, name, h, p = it
            if kind == "sums":
                eng.wait_ge(p_full, p + 1)
                v.tensor_copy(sm[:, 6:8, :], ps[:, p % 2, 0:128].rearrange("p (k n) -> p k n", k=2)[:, :, 0:DTN]
                              ).then_inc(p_free[p % 2], 1)
                wait_evacuated(eng, p)
                v.tensor_tensor(sm[:, 8, :], sm[:, 7, :], sm[:, 6, :], ALU.subtract).then_inc(decay_done, 1)
            elif kind == "turn" and name == 3:
                eng.wait_ge(p_full, p + 1)
                f = slice(4 * h * SSD_HEADS, 4 * (h + 1) * SSD_HEADS)
                by_tile = lambda ap: ap.rearrange("p (m n) -> p m n", m=4)
                v.tensor_tensor(by_tile(sm[:, 0, f]), by_tile(ps[:, p % 2, :])[:, :, 0:SSD_HEADS],
                                by_tile(param("dt_bias", 4 * h * SSD_HEADS, 4 * SSD_HEADS)),
                                ALU.add).then_inc(p_free[p % 2], 1)
            elif kind == "tile" and name[0] in "qk":
                g, s_ = int(name[1]), slice(h * HALF, (h + 1) * HALF)
                eng.wait_ge(qk_hi, QK_ORDER.index((name, h)) + 1)
                hi_, lo_ = (qh, ql) if name[0] == "q" else (kh, kl)
                v.tensor_tensor(lo_[g % 2][:, s_], bank_of(p), hi_[g % 2][:, s_].bitcast(F32),
                                ALU.subtract).then_inc(p_free[p % 2], 1)

        for n in range(UNIT[("in", 2)] + 1):
            lo(n)
        eng.wait_ge(const_in, 48)
        for it in PROLOGUE[:4]:
            evacuate(it)
        lo(UNIT[("in", 3)])
        lo(UNIT[("in", 4)])
        for it in PROLOGUE[4:]:
            evacuate(it)
        for n in range(-2, NSTEP + 1):
            if 0 <= n < NSTEP:
                c0, hd = first_col(n), STEPS[n][3]
                eng.wait_ge(tri_full, n + 1)
                if n >= 2:
                    eng.wait_ge(av_done, n - 1)
                ins = v.tensor_tensor(u[:, n % 2, c0:], zs[:, n % 3, c0:], ps[:, 4 + hd, c0:], ALU.add)
                if on_diagonal(n):
                    link(ins)
                    d = u[:, n % 2, c0:c0 + P]
                    ins = v.tensor_tensor(d, d, table("cap_lt"), ALU.min)
                ins.then_inc(u_done, 1)
            if 0 <= n + 1 < NSTEP:
                k, c0 = n + 1, first_col(n + 1)
                eng.wait_ge(l_done, k + 1)
                if k:
                    eng.wait_ge(lo_done, k)
                link(v.scalar_tensor_tensor(out=sp[:, c0:], in0=zs[:, k % 3, c0:], scalar=0.0,
                                            in1=na[:, k % 2, c0:], op0=ALU.max, op1=ALU.add))
                if on_diagonal(k):
                    d = sp[:, c0:c0 + P]
                    link(v.tensor_tensor(d, d, table("mask_lt"), ALU.mult))
                if k >= 3:
                    eng.wait_ge(av_done, k - 2)
                link(v.tensor_copy(sph[:, k % 3, c0:], sp[:, c0:]))
                v.tensor_tensor(spl[:, k % 3, c0:], sp[:, c0:], sph[:, k % 3, c0:].bitcast(F32),
                                ALU.subtract).then_inc(lo_done, 1)
            if 0 <= n + 2 < NSTEP:
                k, c0 = n + 2, first_col(n + 2)
                eng.wait_ge(zs_done, k + 1)
                v.tensor_scalar(na[:, k % 2, c0:].bitcast(I32), zs[:, k % 3, c0:].bitcast(I32), SIGN, None,
                                ALU.bitwise_or).then_inc(na_done, 1)
            for it in (DONE_AT[n - 1] if 1 <= n <= NSTEP else []):
                evacuate(it)
            for r in SPLIT_AT.get(n, []):
                lo(UNIT[("in", r)])
            for j, at in enumerate(CONV_AT):
                b = n - at
                if 1 <= b < CONV:
                    if b == 1:
                        eng.wait_ge(tap_done, j + 1)
                    ins = v.scalar_tensor_tensor(out=cv[:, j, b:], in0=ht[:, j, :S - b],
                                                 scalar=param("conv_w", 4 * j + 3 - b), in1=cv[:, j, b:],
                                                 op0=ALU.mult, op1=ALU.add)
                    if b < CONV - 1:
                        link(ins)
                    else:
                        ins.then_inc(conv_done, 1)
            if n == DT_AT:
                wait_evacuated(eng, PLACE[("turn3", 1)])
                v.tensor_scalar(sm[:, 1, :].bitcast(I32), sm[:, 0, :].bitcast(I32), SIGN, None,
                                ALU.bitwise_or).then_inc(dt_v, 1)
            if n == DT_AT + 2:
                eng.wait_ge(dt_a, 2)
                link(v.scalar_tensor_tensor(out=sm[:, 3, :], in0=sm[:, 0, :], scalar=0.0, in1=sm[:, 2, :],
                                            op0=ALU.max, op1=ALU.add))
                v.scalar_tensor_tensor(out=sm[:, 5, :], in0=sm[:, 3, :], scalar=-1.0, in1=sm[:, 4, :],
                                       op0=ALU.mult, op1=ALU.mult).then_inc(dt_v, 1)
        meet(eng, 1)

        def task(name):
            eng.wait_ge(d_full, TASKS.index(name) + 1)
            pair = task_place(name)[0]
            return two(pair), d_free[pair]

        def evacuated(name):
            pair, before = task_place(name)
            eng.wait_ge(d_free[pair], before + 1)

        def per_head(row, c):
            return sm[:, row, c * SSD_HEADS:(c + 1) * SSD_HEADS].unsqueeze(2).broadcast_to([P, SSD_HEADS, HEAD])

        def heads(ap):
            return ap.rearrange("p (h d) -> p h d", h=SSD_HEADS)

        v.memset(hs[:, 0, :], 0.0)
        for g in range(PAIRS):
            v.tensor_copy(mh[:, 5 + g, :], sb[:, g, :]).then_inc(mixh, 1)
            eng.wait_ge(mixh, g + 1)
            v.tensor_tensor(ml[:, 5 + g, :], sb[:, g, :], mh[:, 5 + g, :].bitcast(F32),
                            ALU.subtract).then_inc(sb_split, 1)
        eng.wait_ge(dt_a, 4)
        for k in range(4):
            src, free = task("xt%d" % k)
            for c in range(2):
                ch = 2 * k + c
                ins = v.tensor_tensor(heads(xdt[:, ch, :]), heads(src[:, c * HALF:c * HALF + SSD_W]),
                                      per_head(3, ch), ALU.mult)
                if c:
                    ins.then_inc(free, 1)
                    evacuated("xt%d" % k)
                else:
                    link(ins)
                v.tensor_tensor(heads(xw[:, ch, :]), heads(xdt[:, ch, :]), per_head(8, ch),
                                ALU.mult).then_inc(xw_done, 1)

        def argument(h):
            src, _ = task("cu%d" % h)
            if h:
                eng.wait_ge(wexp_done, h)
            for c in range(MT):
                t = slice(c * P, (c + 1) * P)
                ins = v.scalar_tensor_tensor(out=tmp[:, t], in0=src[:, t],
                                             scalar=sm[:, 6, c * SSD_HEADS + h:c * SSD_HEADS + h + 1],
                                             in1=table("cap_le"), op0=ALU.subtract, op1=ALU.min)
            ins.then_inc(arg_done, 1)

        def decayed(h):
            g = h // 3
            eng.wait_ge(wexp_done, h + 1)
            v.tensor_tensor(wt[:, h % 2, :], wt[:, h % 2, :], cb[:, g, :], ALU.mult)
            evacuated("cu%d" % h)
            v.tensor_tensor(ce[:, h % 2, :], ce[:, h % 2, :], cv[:, 5 + g, :], ALU.mult).then_inc(wt_done, 1)

        def gated(i):
            src, free = task("yy%d" % i)
            eng.wait_ge(silu_done, 10)
            v.scalar_tensor_tensor(out=cv[:, i, :], in0=cv[:, i, :], scalar=param("ssd_d", i), in1=src,
                                   op0=ALU.mult, op1=ALU.add).then_inc(free, 1)
            evacuated("yy%d" % i)
            v.tensor_tensor(cv[:, i, :], cv[:, i, :], ht[:, 7 + i, :], ALU.mult).then_inc(hg_done, 1)

        for k in range(4):
            src, free = task("st%d" % k)
            for c in range(2 if k < 3 else 1):
                ch = 2 * k + c
                link(v.tensor_tensor(heads(hs[:, ch + 1, :]), heads(hs[:, ch, :]), per_head(9, ch), ALU.mult))
                ins = v.tensor_tensor(hs[:, ch + 1, :], hs[:, ch + 1, :], src[:, c * HALF:c * HALF + SSD_W], ALU.add)
                if c or k == 3:
                    ins.then_inc(free, 1)
                    evacuated("st%d" % k)
                else:
                    link(ins)
        argument(0)
        argument(1)
        decayed(0)
        argument(2)
        decayed(1)
        argument(3)
        decayed(2)
        gated(0)
        argument(4)
        decayed(3)
        argument(5)
        decayed(4)
        gated(1)
        decayed(5)
        for k in range(2):
            src, free = task("po%d" % k)
            eng.wait_ge(mixh, 4 + k)
            v.scalar_tensor_tensor(out=ml[:, k, :], in0=src, scalar=param("pool_scale", k),
                                   in1=mh[:, k, :].bitcast(F32), op0=ALU.mult, op1=ALU.subtract).then_inc(free, 1)
        gated(2)
        for k, i in enumerate((1, 0, 2)):
            if k == 0:
                eng.wait_ge(rms_done, 1)
                src, free = tmp[:, :], None
            else:
                src, free = task("sp%d" % (i // 2))
            ins = v.scalar_tensor_tensor(out=cv[:, i, :], in0=cv[:, i, :], scalar=param("norm_w", i), in1=src,
                                         op0=ALU.mult, op1=ALU.mult)
            ins.then_inc(nrm_done, 1)
            if k:
                eng.wait_ge(mixh, 6 + k - 1)
                j = (1, 0, 2)[k - 1]
                v.tensor_tensor(ml[:, 2 + j, :], cv[:, j, :], mh[:, 2 + j, :].bitcast(F32), ALU.subtract)
        eng.wait_ge(mixh, 8)
        v.tensor_tensor(ml[:, 4, :], cv[:, 2, :], mh[:, 4, :].bitcast(F32), ALU.subtract)
        meet(eng, 2)

        eng.wait_ge(split_done, UNIT[("gate", 0)])
        lo(UNIT[("gate", 0)])

        def statistics(m, rows):
            v.bn_stats(st[:, m, 0:6], rows[:, 0:HALF])
            link(v.bn_stats(st[:, m, 6:12], rows[:, HALF:D]))
            link(v.bn_aggr(st[:, m, 12:14], st[:, m, 0:12]))
            return v.tensor_scalar(st[:, m, 14:15], st[:, m, 13:14], LN_EPS, None, ALU.add)

        def split_x1(m):
            eng.wait_ge(x1_done, m + 1)
            t = slice(m * P, (m + 1) * P)
            link(v.tensor_copy(mh[:, :, t], acc[:, :, t]))
            v.tensor_tensor(ml[:, :, t], acc[:, :, t], mh[:, :, t].bitcast(F32), ALU.subtract).then_inc(x1_split, 1)

        for m in range(MT):
            eng.wait_ge(y_full, m + 1)
            eng.wait_ge(x_in, 16 * (m + 1))
            if m >= 2:
                eng.wait_ge(t_full, m - 1)
            v.scalar_tensor_tensor(out=yn[:, m % 2, :], in0=xn[:, :], scalar=ALPHA, in1=two(m % 2),
                                   op0=ALU.mult, op1=ALU.add).then_inc(y_read, 1)
            eng.wait_ge(y_read, m + 1)
            statistics(m, yn[:, m % 2, :]).then_inc(v_eps, 1)
            if m:
                split_x1(m - 1)
            eng.wait_ge(v_sqrt, m + 1)
            link(v.reciprocal(st[:, m, 15:16], st[:, m, 15:16]))
            v.tensor_scalar(yn[:, m % 2, :], yn[:, m % 2, :], st[:, m, 12:13], st[:, m, 15:16], ALU.subtract,
                            ALU.mult).then_inc(y_norm, 1)
        for i in range(PLE_TILES):
            lo(UNIT[("p", i)])
        split_x1(MT - 1)

        for i in range(PLE_TILES):
            lo(UNIT[("proj", i)])
        lo(UNIT[("gate", 1)])
        for j in range(KT):
            if j + 2 < KT:
                lo(UNIT[("gate", j + 2)])
            else:
                lo(FFN0 + j + 2 - KT)
            eng.wait_ge(sig_done, j + 1)
            eng.wait_ge(u_full, 2 * j + 2)
            v.tensor_tensor(sig[:, j % 2, :], sig[:, j % 2, :], two(1), ALU.mult).then_inc(u_free, 1)
            eng.wait_ge(u_free, 2 * j + 1)
            v.scalar_tensor_tensor(out=acc[:, j, :], in0=acc[:, j, :], scalar=ALPHA, in1=sig[:, j % 2, :],
                                   op0=ALU.mult, op1=ALU.add).then_inc(u_free, 1)

        def column(c, step, it):
            return par[:, c:c + 1] if isinstance(it, int) else par[:, bass.ds(c + step * it, 1)]

        def conv(c, t, it=0):
            item = 2 * KT + 4 * c + t
            src = two(item % 2)
            w = PARAMS["ff_w"] + 3 * (4 * c + t)
            eng.wait_ge(tap_ff, 4 * c + t + 1 + 4 * it)
            v.scalar_tensor_tensor(out=cf[:, t % 2, 1:], in0=src[:, :S - 1], scalar=column(w + 1, 12, it),
                                   in1=cf[:, t % 2, 1:], op0=ALU.mult, op1=ALU.add).then_inc(tap_mid, 1)
            eng.wait_ge(tap_mid, 4 * c + t + 1 + 4 * it)
            v.scalar_tensor_tensor(out=cf[:, t % 2, 2:], in0=src[:, :S - 2], scalar=column(w, 12, it),
                                   in1=cf[:, t % 2, 2:], op0=ALU.mult, op1=ALU.add).then_inc(u_free, 1)

        def product(c, i, it=0):
            eng.wait_ge(silu_ff, 2 * c + i + 1 + 2 * it)
            eng.wait_ge(u_free, 2 * KT + 4 * c + 2 * i + 2 + 4 * it)
            v.tensor_tensor(hf[:, :], cf[:, 0, :], cf[:, 1, :], ALU.mult).then_inc(prod_mid, 1)
            eng.wait_ge(prod_mid, 2 * (2 * c + i) + 1 + 4 * it)
            last = c == CHUNKS - 1
            hi_, lo_ = (h2h, h2l) if last else (hh, hl)
            if c and not last:
                eng.wait_ge(dn_full, 16 * c + 16 * it)
            v.tensor_copy(hi_[:, i, :], hf[:, :]).then_inc(prod_mid, 1)
            eng.wait_ge(prod_mid, 2 * (2 * c + i) + 2 + 4 * it)
            v.tensor_tensor(lo_[:, i, :], hf[:, :], hi_[:, i, :].bitcast(F32), ALU.subtract).then_inc(h_done, 1)

        def add_down(c, it=0, by_half=False, ks=range(16)):
            for k in ks:
                eng.wait_ge(dn_full, 16 * c + k + 1 + 16 * it)
                j, h = (k % 8, k // 8) if by_half else (k // 2, k % 2)
                dst = acc[:, j, h * HALF:(h + 1) * HALF]
                if k == 0:
                    eng.wait_ge(u_free, 2 * KT)
                    if c:
                        eng.wait_ge(dn_added, 16 * c + 16 * it)
                v.tensor_tensor(dst, dst, ps[:, 4 + k % 4, :], ALU.add).then_inc(dn_added, 1)

        lo(FFN0 + 2)
        lo(FFN0 + 3)
        conv(0, 0)
        conv(0, 1)
        lo(FFN0 + 4)
        product(0, 0)
        conv(0, 2)
        lo(FFN0 + 5)
        conv(0, 3)
        product(0, 1)
        lo(FFN0 + 6)

        def chunk(c, n, it=0):
            conv(c, 0, it)
            add_down(c - 1, it, ks=range(6))
            lo(n + 3, it)
            add_down(c - 1, it, ks=range(6, 16))
            lo(n + 4, it)
            lo(n + 5, it)
            conv(c, 1, it)
            product(c, 0, it)
            lo(n + 6, it)
            conv(c, 2, it)
            lo(n + 7, it)
            conv(c, 3, it)
            product(c, 1, it)
            lo(n + 8, it)

        n1 = FFN0 + 4
        chunk(1, n1)
        with eng.Fori(0, CHUNKS - 3) as it:
            chunk(2, n1 + 6, it)
        c, n = CHUNKS - 1, len(UNITS) - 8
        conv(c, 0)
        lo(n + 3)
        conv(c, 1)
        product(c, 0)
        lo(n + 4)
        conv(c, 2)
        lo(n + 5)
        conv(c, 3)
        product(c, 1)
        add_down(c - 1, ks=range(8))
        lo(n + 6)
        add_down(c - 1, ks=range(8, 16))
        lo(n + 7)
        for k in range(12):
            add_down(CHUNKS - 1, 0, True, [k])

        eng.wait_ge(ln_in, 32)

        def gain(m):
            eng.wait_ge(o_nrm, m + 1)
            v.tensor_tensor(on[:, m % 4, :], on[:, m % 4, :], lng[:, :], ALU.mult).then_inc(o_gain, 1)

        for m in range(MT):
            eng.wait_ge(o_full, m + 1)
            statistics(m, two(m % 2)).then_inc(o_eps, 1)
            if m < 4:
                add_down(CHUNKS - 1, 0, True, [12 + m])
            if m:
                gain(m - 1)
            eng.wait_ge(o_sqrt, m + 1)
            link(v.reciprocal(st[:, m, 13:14], st[:, m, 15:16]))
            v.scalar_tensor_tensor(out=st[:, m, 12:13], in0=st[:, m, 12:13], scalar=-1.0, in1=st[:, m, 13:14],
                                   op0=ALU.mult, op1=ALU.mult).then_inc(o_aff, 1)
        gain(MT - 1)

    @block.gpsimd
    def _(eng):
        g = nc.gpsimd
        chained = [0]

        def link(ins):
            chained[0] += 1
            ins.then_inc(pool_chain, 1)
            eng.wait_ge(pool_chain, chained[0])

        def doubled(dst, src, k, rows):
            g.tensor_copy(dst[rows, :k], src[rows, :k])
            link(g.tensor_tensor(dst[rows, k:], src[rows, k:], src[rows, :S - k], ALU.add))

        meet(eng, 1)
        every, upper, lower = slice(0, P), slice(HEAD, P), slice(0, HEAD)
        for i in range(2):
            x_ = ht[:, 10 + i, :]
            doubled(pa, ht[:, 10 + i, :], 1, every)
            s_, d_, k = pa, pb, 2
            if i == 1:
                doubled(pb, pa, 2, every)
                doubled(pa, pb, 4, every)
                k = 8
            g.tensor_copy(pb[lower, :], pa[lower, :])
            doubled(pb, pa, k, upper)
            link(g.tensor_tensor(pb[:, 0:16], pb[:, 0:16], table("pool_cnt")[:, 16 * i:16 * i + 16], ALU.mult))
            link(g.tensor_scalar(pb[:, :], pb[:, :], param("pool_inv", i), None, ALU.mult))
            g.tensor_tensor(x_, pb[:, :], x_, ALU.subtract).then_inc(pooled, 1)
            eng.wait_ge(pooled, i + 1)
        for k in OUT_ORDER:
            lo(UNIT[("out", k)], eng=g)
        meet(eng, 2)
        eng.wait_ge(ln_in, 32)
        for m in range(MT):
            eng.wait_ge(o_gain, m + 1)
            g.tensor_tensor(on[:, m % 4, :], on[:, m % 4, :], lnb[:, :], ALU.add).then_inc(o_bias, 1)


def _tiles(w):
    n = w.shape[1] // P
    return w.reshape(KT, P, n, P).transpose(2, 1, 0, 3).reshape(n, P, D)


def _tables():
    i, j = np.arange(P)[:, None], np.arange(P)[None, :]
    one = lambda c: np.broadcast_to(c, (P, P)).astype(np.float32)
    cnt = np.ones((P, P), np.float32)
    for tile in range(2):
        for half in range(2):
            w = (2, 4, 8, 16)[2 * tile + half]
            cnt[HEAD * half:HEAD * half + HEAD, 16 * tile:16 * tile + 16] = w / np.minimum(np.arange(16) + 1, w)
    t = {"ident": one(i == j), "ones": one(i >= 0), "tri_le": one(i <= j), "mask_lt": one(i < j),
         "cap_lt": np.where(i < j, BIG, NEG), "cap_le": np.where(i <= j, BIG, NEG),
         "neg_ge": -one(i >= j), "neg_lt": -one(i < j),
         "rms_0": one(j < HEAD), "rms_1": one((i < HEAD) == (j < HEAD)), "rms_2": one(j >= HEAD),
         "from_first": one(i == 0), "from_last": one(i == P - 1), "pool_cnt": cnt}
    return np.concatenate([t[k].astype(np.float32) for k in TABLES], axis=1)


def _columns(v):
    return v.reshape(-1, P).T


def kernel(**inputs):
    import concourse.bacc as bacc
    from concourse.bass_utils import run_bass_kernel_spmd

    g = {k: np.asarray(v) for k, v in inputs.items()}
    w_in = g["w_in"][0]
    dt_cols = np.pad(w_in[:, COL_DT:COL_Q], ((0, 0), (0, P - SSD_HEADS)))
    cols = np.concatenate([dt_cols if t == "dt" else
                           w_in[:, IN_COLS[t[0]] + P * int(t[1]):IN_COLS[t[0]] + P * int(t[1]) + P]
                           for t in IN_TILES], axis=1)
    x = g["x"][0]
    order = [k for c in range(CHUNKS) for t in range(PER_CHUNK) for k in (PER_CHUNK * c + t,
                                                                        FF_TILES + PER_CHUNK * c + t)]
    up = _tiles(g["ffn_w_up"][0])[order]
    pool = np.zeros((P, 2, P), np.float32)
    for k in range(4):
        r = slice(HEAD * (k % 2), HEAD * (k % 2) + HEAD)
        pool[r, k // 2, r] = g["pool_w"][0, k]
    pool_inv = np.repeat(np.array([[1 / 2, 1 / 8], [1 / 4, 1 / 16]], np.float32), HEAD, axis=0)
    lanes = lambda v, n: np.broadcast_to(np.tile(v, n), (P, n * len(v)))
    cw = g["ssd_conv_w"][0].reshape(CONV, 7, P).transpose(2, 1, 0).reshape(P, 28)
    fw = g["ffn_conv_w"][0].reshape(FF_CONV, 2 * FF_TILES, P).transpose(2, 1, 0)[:, order].reshape(P, -1)
    fb = _columns(g["ffn_conv_b"][0])[:, order]
    params = {"conv_w": cw, "conv_b": _columns(g["ssd_conv_b"][0]), "pool_scale": _columns(g["pool_scale"][0]),
              "pool_inv": pool_inv, "ssd_d": _columns(np.repeat(g["ssd_d"][0], HEAD)),
              "norm_w": _columns(g["ssd_norm_w"][0]), "dt_bias": lanes(g["ssd_dt_bias"][0], MT),
              "a_log": lanes(g["ssd_a_log"][0], MT), "rms_eps": np.full((P, 1), RMS_EPS, np.float32),
              "ln1_g": _columns(g["ln1_g"][0]),
              "ln1_b": _columns(g["ln1_b"][0]), "ff_w": fw, "ff_b": fb}
    arrays = {
        "u_x": x.T.reshape(KT, P, S), "u_in": _tiles(cols), "u_out": g["w_out"][0].reshape(KT, P, D),
        "u_p": g["p"][0, 0].T.reshape(PLE_TILES, P, S), "u_proj": g["ple_w_proj"][0].reshape(PLE_TILES, P, D),
        "u_gate": _tiles(g["ple_w_gate"][0]), "u_up": up, "u_down": g["ffn_w_down"][0].reshape(FF_TILES, P, D),
        "x_nat": x.reshape(MT, P, D), "tables": _tables(), "pool_w": pool.reshape(P, 2 * P),
        "params": np.concatenate([params[k] for k in PARAM_SIZES], axis=1),
        "ln2_g": g["ln2_g"][0], "ln2_b": g["ln2_b"][0],
    }
    arrays = {k: np.ascontiguousarray(v) for k, v in arrays.items()}
    nc = bacc.Bacc("TRN2", target_bir_lowering=False, num_devices=1, dynamic_dma_scratch_size=1024)
    aps = {k: nc.dram_tensor(k, v.shape, mybir.dt.from_np(v.dtype), kind="ExternalInput").ap()
           for k, v in arrays.items()}
    out = nc.dram_tensor("out", (S, D), F32, kind="ExternalOutput").ap()
    with ExitStack() as ctx:
        build(nc, ctx, aps, out)
    r = run_bass_kernel_spmd(nc, [arrays], core_ids=[0])
    return r.results[0]["out"].reshape(1, S, D)
```

```python
from contextlib import ExitStack

import numpy as np

import concourse.bass as bass
from concourse import mybir

F32 = mybir.dt.float32
F32R = mybir.dt.float32r
I32 = mybir.dt.int32
SIGN = -2 ** 31
ALU = mybir.AluOpType
ACT = mybir.ActivationFunctionType

P = 128
D = 1024
S = 1024
HALF = 512
KT = D // P
MT = S // P
HEAD = 64
POOL_W = 256
SSD_W = 384
SSD_HEADS = 6
STATE = 128
CONV = 4
FF = 2816
FF_TILES = FF // P
PER_CHUNK = 2
CHUNKS = FF_TILES // PER_CHUNK
FF_CONV = 3
PLE_TILES = 2
ALPHA = 2.0 ** 0.25
LN_EPS = 1e-5
RMS_EPS = 1e-6
SCALE = HEAD ** -0.5
PAIRS = 3
BIG = 3.0e38
NEG = -3.0e4

COL_Z = POOL_W
COL_XBC = COL_Z + SSD_W
COL_DT = COL_XBC + SSD_W + 4 * STATE
COL_Q = COL_DT + SSD_HEADS
COL_K = COL_Q + 384
COL_V = COL_K + 384

H_TILES = ["x0", "x1", "x2", "B0", "B1", "C0", "C1", "z0", "z1", "z2", "p0", "p1"]
WINDOWS = [["v1", "q1", "k1", "x0", "x1", "x2"], ["v2", "q2", "k2", "B0", "B1", "C0"],
           ["dt", "C1", "z0", "z1", "z2", "p0", "p1"]]
IN_TILES = ["v0", "q0", "k0"] + [t for w in WINDOWS for t in w]
IN_COLS = {"q": COL_Q, "k": COL_K, "v": COL_V, "x": COL_XBC, "B": COL_XBC + SSD_W,
           "C": COL_XBC + SSD_W + 2 * STATE, "z": COL_Z, "p": 0}
TURNED = ["v0", "v1", "v2", "dt"]

UNITS = [("in", 0), ("in", 1)] + [("x", i) for i in range(KT)] + [("in", i) for i in range(2, len(IN_TILES))]
OUT_ORDER = [5, 6, 7, 0, 1, 3, 2, 4]
UNITS += [("out", i) for i in OUT_ORDER] + [("gate", 0), ("gate", 1)] + [("p", i) for i in range(PLE_TILES)]
UNITS += [("proj", i) for i in range(PLE_TILES)] + [("gate", i) for i in range(2, KT)]
FFN0 = len(UNITS)
UNITS += [("up", i) for i in range(4)]
for _c in range(1, CHUNKS - 1):
    UNITS += [("up", 4 * _c), ("down", 2 * _c - 2), ("down", 2 * _c - 1)] + [("up", 4 * _c + i) for i in (1, 2, 3)]
UNITS += [("up", 4 * (CHUNKS - 1) + i) for i in range(4)] + [("down", i) for i in range(FF_TILES - 4, FF_TILES)]
UNIT = {u: n for n, u in enumerate(UNITS)}
RAWS = 2
RINGS = 3
RING_OF = {}
for _n, _u in enumerate(UNITS):
    if _u[0] in ("in", "gate", "up", "down") and _n < len(UNITS) - 2:
        RING_OF[_n] = len(RING_OF)

TABLES = ["ident", "ones", "tri_le", "mask_lt", "cap_lt", "cap_le", "neg_ge", "neg_lt",
          "pool_cnt", "rms_0", "rms_1", "rms_2", "from_first", "from_last"]
STEPS = [(g, qh, kb, hd) for g in range(PAIRS) for qh in range(2)
         for kb in range(4 * qh + 3, -1, -1) for hd in range(2)]
NSTEP = len(STEPS)
PER_PAIR = NSTEP // PAIRS


def first_col(n):
    _, qh, kb, _ = STEPS[n]
    return max(0, P * kb - HALF * qh)


def on_diagonal(n):
    _, qh, kb, _ = STEPS[n]
    return kb >= 4 * qh


def ple_item(kind, j):
    return (2 * j if j > 1 else j) + (0 if kind == "gate" else 1 if j > 1 else 2)


def raw_place(n):
    return n if n < UNIT[("x", 0)] else n - KT


def projection_plan():
    p = 0
    pro = []
    for name in ("v0", "q0", "k0"):
        for h in range(2):
            pro.append(("tile", name, h, p))
            p += 1
    for h in range(2):
        pro.append(("turn", 0, h, p))
        p += 1
    by_step = []
    for g, window in enumerate(WINDOWS):
        pieces = []
        for i, name in enumerate(window):
            for h in range(2):
                it = ("tile", name, h, p)
                p += 1
                pieces += [(it, 0, 2), (it, 1, 2)]
            if name == "z2":
                pieces.append((("sums", "sums", 0, p), 0, 1))
                p += 1
            if (name[0] == "q" and i == 1) or (name == "C1" and g == 2):
                for hh in range(2):
                    pieces.append((("turn", g + 1, hh, p), 0, 1))
                    p += 1
        cost = [1 if it[0] == "sums" else 2 if it[0] == "turn" else 8 if it[1] == "dt" else 12
                for it, _, _ in pieces]
        used, i = 0, 0
        for s in range(PER_PAIR):
            now = []
            while i < len(pieces) and (used + cost[i] / 2 <= (s + 1) * sum(cost) / PER_PAIR or s == PER_PAIR - 1):
                if any(part == parts - 1 and it[3] == pieces[i][0][3] - 2 for it, part, parts in now):
                    break
                now.append(pieces[i])
                used += cost[i]
                i += 1
            by_step.append(now)
        assert i == len(pieces)
    return pro, by_step


PROLOGUE, BY_STEP = projection_plan()
PLACE = {}
for _it in PROLOGUE + [x[0] for s in BY_STEP for x in s]:
    PLACE[(_it[1], _it[2]) if _it[0] != "turn" else ("turn%d" % _it[1], _it[2])] = _it[3]
DONE_AT = [[it for it, part, parts in s if part == parts - 1] for s in BY_STEP]
STARTS = {}
for _s, _ps in enumerate(BY_STEP):
    for _it, _part, _parts in _ps:
        if _it[0] == "tile" and _it[2] == 0 and _part == 0:
            STARTS[IN_TILES.index(_it[1])] = _s
SPLIT_AT = {}
for _r in range(5, len(IN_TILES)):
    SPLIT_AT.setdefault(STARTS[_r - 2] + 1, []).append(_r)


def evacuated_at(*names):
    return 1 + max(s for s, d in enumerate(DONE_AT) for it in d if it[:2] in names)


CONV_AT, TAPS_AT = [], []
for _name in H_TILES[:7]:
    CONV_AT.append(max([evacuated_at(("tile", _name)) + 1] + [t[-1] + 1 for t in TAPS_AT[-1:]]))
    TAPS_AT.append([s for s in range(CONV_AT[-1] + 1, NSTEP) if s not in SPLIT_AT][:CONV - 1])
DT_AT = evacuated_at(("turn", 3)) + 1
SUMS_AT = 2 + next(s for s, d in enumerate(DONE_AT) if any(it[0] == "sums" for it in d))

GAIN_ON_VECTOR = (3, 5, 6, 7)
LAST_UP = 2 * KT + 4 * CHUNKS - 1
BY_RING = {r: n for n, r in RING_OF.items()}
QK_ORDER = [(it[1], it[2]) for it in PROLOGUE + [i for d in DONE_AT for i in d]
            if it[0] == "tile" and it[1][0] in "qk"]
TASKS = ["xt0", "xt1", "bt0", "bt1", "xt2", "xt3", "st0", "st1", "st2", "st3", "cb0", "cb1", "cu0", "cu1",
         "cu2", "cu3", "yy0", "cu4", "cu5", "yy1", "po0", "po1", "yy2", "rm0", "sp0", "sp2"]
TAIL = TASKS.index("rm0")


def task_place(name):
    pairs = [t % 4 if t < TAIL else 2 + (t - TAIL) % 2 for t in range(len(TASKS))]
    t = TASKS.index(name)
    return pairs[t], pairs[:t].count(pairs[t])


DTN = MT * SSD_HEADS
PARAM_SIZES = {"conv_w": 28, "conv_b": 7, "pool_scale": 2, "pool_inv": 2, "ssd_d": 3, "norm_w": 3, "dt_bias": DTN,
               "a_log": DTN, "ln1_g": KT, "ln1_b": KT, "ff_w": 3 * 2 * FF_TILES, "ff_b": 2 * FF_TILES}
PARAMS, N_PARAMS = {}, 0
for _k, _n in PARAM_SIZES.items():
    PARAMS[_k] = N_PARAMS
    N_PARAMS += _n


def build(nc, ctx, a, out):
    kb = 1024
    top = [2 * kb]

    def put(name, shape, dt=F32, at=None):
        size = -(-4 * int(np.prod(shape[1:])) // 32) * 32
        if at is None:
            at = top[0]
            top[0] += size
        assert at + size <= 229368, (name, at, size)
        return nc.alloc_sbuf_tensor_at(name, shape, dt, offset=at)

    def sem(name):
        return ctx.enter_context(nc.semaphore(name))

    raw = put("raw", [P, RAWS, D])
    wh = put("w_hi", [P, RINGS, D], F32R)
    wl = put("w_lo", [P, RINGS, D], F32R)
    tab = put("tables", [P, len(TABLES), P])
    neg_ge = put("neg_ge_r", [P, P], F32R)
    neg_lt = put("neg_lt_r", [P, P], F32R)
    pool_w = put("pool_w", [P, 2, P])
    par = put("params", [P, N_PARAMS])
    sm = put("small", [P, 10, DTN])
    st = put("ln_stats", [P, MT, 16])
    x0 = top[0]
    xh = put("x_hi", [P, KT, S], F32R)
    xl = put("x_lo", [P, KT, S], F32R)
    mh = put("mix_hi", [P, KT, S], F32R, x0)
    ml = put("mix_lo", [P, KT, S], F32R, x0 + 32 * kb)
    xdt = put("x_dt", [P, MT, SSD_W], F32, x0 + 2 * 4 * kb)
    xw = put("x_weighted", [P, MT, SSD_W], F32, x0 + (32 + 2 * 4) * kb)
    pa = put("pool_a", [P, S], F32, x0 + 32 * kb)
    pb = put("pool_b", [P, S], F32, x0 + 36 * kb)

    slot0 = top[0]

    def over(name, shape, first, dt=F32, of=0):
        assert first + (4 * int(np.prod(shape[1:])) + of * kb) / (4 * kb) <= 28, name
        return put(name, shape, dt, slot0 + (4 * first + of) * kb)

    stage = over("x_stage", [P, KT, S], 0)
    ht = over("h_tiles", [P, len(H_TILES), S], 1)
    sets = [13, 7]
    qh = [over("q_hi%d" % i, [P, S], sets[i], F32R) for i in range(2)]
    ql = [over("q_lo%d" % i, [P, S], sets[i] + 1, F32R) for i in range(2)]
    kh = [over("k_hi%d" % i, [P, S], sets[i] + 2, F32R) for i in range(2)]
    kl = [over("k_lo%d" % i, [P, S], sets[i] + 3, F32R) for i in range(2)]
    vn = [over("v_nat%d" % i, [P, MT, P], sets[i] + 4) for i in range(2)]
    vt = over("v_t", [P, S], 12)
    zs = over("z_scaled", [P, 3, HALF], 18)
    sph = over("sp_hi", [P, 3, HALF], 18, F32R, 6)
    spl = over("sp_lo", [P, 3, HALF], 18, F32R, 12)
    na = over("abs_z", [P, 2, HALF], 18, F32, 18)
    u = over("weights", [P, 2, HALF], 18, F32, 22)
    sp = over("softplus", [P, HALF], 18, F32, 26)
    sb = over("sb_out", [P, PAIRS, S], 25)
    cv = over("conv", [P, 7, S], 0)
    bn = over("b_natural", [P, 2, MT, P], 13)
    hs = over("states", [P, MT, SSD_W], 15)
    cb = over("cb", [P, 2, S], 18)
    wt = [over("decayed%d" % i, [P, 2, S], (20, 25)[i]) for i in range(2)]
    ce = [over("c_scaled%d" % i, [P, 2, S], (22, 13)[i]) for i in range(2)]
    tmp = over("tmp", [P, S], 24)
    out_slots = {5: (25, 26), 6: (27, 13), 7: (14, 11), 0: (12, 15), 1: (16, 17), 2: (18, 19), 3: (20, 21),
                 4: (22, 23)}
    oh = [over("wo_hi%d" % k, [P, D], out_slots[k][0], F32R) for k in range(KT)]
    ol = [over("wo_lo%d" % k, [P, D], out_slots[k][1], F32R) for k in range(KT)]
    acc = over("acc", [P, KT, S], 0)
    yn = over("y_nat", [P, 2, D], 8)
    xn = over("x_nat", [P, D], 10)
    ph = over("p_hi", [P, PLE_TILES, S], 11, F32R)
    pl = over("p_lo", [P, PLE_TILES, S], 13, F32R)
    pwh = over("proj_hi", [P, PLE_TILES, D], 15, F32R)
    pwl = over("proj_lo", [P, PLE_TILES, D], 17, F32R)
    sig = over("sigmoid", [P, 2, S], 19)
    hh = over("h_hi", [P, PER_CHUNK, S], 11, F32R)
    hl = over("h_lo", [P, PER_CHUNK, S], 13, F32R)
    cf = over("conv_ff", [P, 2, S], 21)
    hf = over("h_ff", [P, S], 24)
    lng = over("ln2_gain", [P, D], 8)
    lnb = over("ln2_bias", [P, D], 9)
    on = over("o_norm", [P, 4, D], 24)
    h2h = over("last_h_hi", [P, PER_CHUNK, S], 15, F32R)
    h2l = over("last_h_lo", [P, PER_CHUNK, S], 17, F32R)
    last_w = [[over("last_w%d%d" % (i, j), [P, D], s_, F32R) for j, s_ in enumerate(at)]
              for i, at in enumerate(((10, 23), (19, 20)))]

    ps = ctx.enter_context(nc.psum_tensor("ps", [P, 8, HALF], F32))

    def two(i):
        return ps[:, 2 * i:2 * i + 2, :].rearrange("p b n -> p (b n)")

    def table(name):
        return tab[:, TABLES.index(name), :]

    def param(name, i=0, n=1):
        c = PARAMS[name] + i
        return par[:, c:c + n]

    const_in = sem("const_in")
    const_r = sem("const_r")
    x_raw = [sem("x_raw%d" % i) for i in range(KT)]
    raw_in = [sem("raw_in%d" % i) for i in range(RAWS)]
    hi_done = sem("hi_done")
    split_done = sem("split_done")
    barrier = sem("barrier")
    p_full = sem("p_full")
    p_free = [sem("p_free%d" % i) for i in range(2)]
    qk_hi = sem("qk_hi")
    z_full, zs_done = sem("z_full"), sem("zs_done")
    e_done, l_done, lo_done = sem("e_done"), sem("l_done"), sem("lo_done")
    tri_full, u_done, w_done, av_done = sem("tri_full"), sem("u_done"), sem("w_done"), sem("av_done")
    o_out = sem("o_out")
    dve_chain = sem("dve_chain")
    pool_chain = sem("pool_chain")
    dt_v = sem("dt_v")
    dt_a = sem("dt_a")
    tap_done, conv_done, silu_done = sem("tap_done"), sem("conv_done"), sem("silu_done")
    d_full = sem("d_full")
    d_free = [sem("d_free%d" % i) for i in range(4)]
    decay_done = sem("decay_done")
    arg_done, wexp_done, wt_done = sem("arg_done"), sem("wexp_done"), sem("wt_done")
    xdt_done = sem("xdt_done")
    xw_done = sem("xw_done")
    hg_done, sq_done, nrm_done = sem("hg_done"), sem("sq_done"), sem("nrm_done")
    var_done, sqrt_done = sem("var_done"), sem("sqrt_done")
    rms_done = sem("rms_done")
    mixh = sem("mix_hi_done")
    ssd_split = sem("ssd_split")
    sb_split = sem("sb_split")
    pool_sum = sem("pool_sum")
    pool_scaled = sem("pool_scaled")
    pooled = sem("pooled")
    x_in, y_full, y_read, v_eps, v_sqrt = sem("x_in"), sem("y_full"), sem("y_read"), sem("v_eps"), sem("v_sqrt")
    y_norm, t_full, x1_done, x1_split = sem("y_norm"), sem("t_full"), sem("x1_done"), sem("x1_split")
    u_full, u_free, sig_done = sem("u_full"), sem("u_free"), sem("sig_done")
    tap_ff, tap_mid, silu_ff, prod_mid, h_done = (
        sem("tap_ff"), sem("tap_mid"), sem("silu_ff"), sem("prod_mid"), sem("h_done"))
    dn_full, dn_added = sem("dn_full"), sem("dn_added")
    half_full, half_tap, half_mid, half_conv, half_done = (
        sem("half_full"), sem("half_tap"), sem("half_mid"), sem("half_conv"), sem("half_done"))
    ln_in, o_full, o_eps, o_sqrt, o_aff, o_nrm, o_gain, o_bias = (
        sem("ln_in"), sem("o_full"), sem("o_eps"), sem("o_sqrt"), sem("o_aff"), sem("o_nrm"), sem("o_gain"),
        sem("o_bias"))
    o_last = sem("o_last")
    stored = [sem("stored%d" % i) for i in range(4)]

    def meet(eng, k):
        eng.drain().then_inc(barrier, 1)
        eng.wait_ge(barrier, 4 * k)

    def wait_evacuated(eng, p):
        eng.wait_ge(p_free[p % 2], p // 2 + 1)

    def bank_of(p):
        return ps[:, p if p < 4 else p % 2, :]

    def unit_place(n, lo):
        kind, i = UNITS[n]
        if kind == "x":
            return (xl if lo else xh)[:, i, :]
        if kind == "out":
            return (ol if lo else oh)[i][:, :]
        if kind == "p":
            return (pl if lo else ph)[:, i, :]
        if kind == "proj":
            return (pwl if lo else pwh)[:, i, :]
        if n not in RING_OF:
            return last_w[n - (len(UNITS) - 2)][int(lo)][:, :]
        return (wl if lo else wh)[:, RING_OF[n] % RINGS, :]

    def wait_ring_free(eng, n, it=0):
        if n not in RING_OF or RING_OF[n] < RINGS:
            return
        kind, i = UNITS[BY_RING[RING_OF[n] - RINGS]]
        if kind == "in":
            eng.wait_ge(p_full, PLACE[(IN_TILES[i], 1)] + 1)
        elif kind == "gate":
            eng.wait_ge(u_full, ple_item("gate", i) + 1)
        elif kind == "up":
            eng.wait_ge(u_full, 2 * KT + i + 1 + 4 * it)
        else:
            eng.wait_ge(dn_full, 16 * (i // 2 + 1) + 16 * it)

    def unit_raw(n):
        return stage[:, UNITS[n][1], :] if UNITS[n][0] == "x" else raw[:, n % RAWS, :]

    def hi(n, it=0):
        if UNITS[n][0] == "x":
            nc.scalar.wait_ge(x_raw[UNITS[n][1]], 16)
        else:
            nc.scalar.wait_ge(raw_in[n % RAWS], 16 * (raw_place(n) // RAWS + 1) + 16 * 6 // RAWS * it)
        wait_ring_free(nc.scalar, n, it)
        nc.scalar.activation(unit_place(n, False), unit_raw(n), ACT.Copy).then_inc(hi_done, 1)

    def lo(n, it=0, eng=nc.vector):
        eng.wait_ge(hi_done, n + 1 + 6 * it)
        eng.tensor_tensor(unit_place(n, True), unit_raw(n), unit_place(n, False).bitcast(F32),
                                ALU.subtract).then_inc(split_done, 1)

    def per_head(row, c):
        return sm[:, row, c * SSD_HEADS:(c + 1) * SSD_HEADS].unsqueeze(2).broadcast_to([P, SSD_HEADS, HEAD])

    def heads(ap):
        return ap.rearrange("p (h d) -> p h d", h=SSD_HEADS)

    block = ctx.enter_context(nc.Block())

    @block.sync
    def _(eng):
        def unit_source(n):
            kind, i = UNITS[n]
            return a["u_" + kind][i]

        def load(n):
            if raw_place(n) >= RAWS:
                eng.wait_ge(split_done, n - RAWS + 1 if raw_place(n) >= 2 * RAWS else n - KT - RAWS + 1)
            eng.dma_start(raw[:, n % RAWS, :], unit_source(n)).then_inc(raw_in[n % RAWS], 16)

        def load_x(i):
            eng.dma_start(stage[:, i, :], unit_source(UNIT[("x", i)])).then_inc(x_raw[i], 16)

        load(0)
        load_x(0)
        load(1)
        for i in range(1, KT):
            load_x(i)
        eng.dma_start(tab[:, :, :].rearrange("p t n -> p (t n)"), a["tables"]).then_inc(const_in, 16)
        eng.dma_start(par[:, :], a["params"]).then_inc(const_in, 16)
        eng.dma_start(pool_w[:, :, :].rearrange("p t n -> p (t n)"), a["pool_w"]).then_inc(const_in, 16)
        for n in range(UNIT[("in", 2)], UNIT[("out", OUT_ORDER[-1])] + 1):
            load(n)
        eng.wait_ge(hg_done, 3)
        for m in range(MT):
            if m:
                eng.wait_ge(y_read, m)
            eng.dma_start(xn[:, :], a["x_nat"][m]).then_inc(x_in, 16)
            if m == 0:
                load(UNIT[("gate", 0)])
                load(UNIT[("gate", 1)])
        for n in range(UNIT[("p", 0)], FFN0 + 4):
            load(n)
        eng.wait_ge(t_full, MT)
        eng.dma_start(lng[:, :], a["ln2_g"].partition_broadcast(P)).then_inc(ln_in, 16)
        eng.dma_start(lnb[:, :], a["ln2_b"].partition_broadcast(P)).then_inc(ln_in, 16)
        n0 = FFN0 + 4
        with eng.Fori(0, CHUNKS - 2) as it:
            for j in range(6):
                n = n0 + j
                eng.wait_ge(split_done, n - RAWS + 1 + 6 * it)
                kind, i = UNITS[n]
                src = a["u_up"][i + 4 * it] if kind == "up" else a["u_down"][i + 2 * it]
                eng.dma_start(raw[:, n % RAWS, :], src).then_inc(raw_in[n % RAWS], 16)
        for n in range(len(UNITS) - 8, len(UNITS)):
            load(n)
        for m in range(MT):
            if m < MT - 1:
                eng.wait_ge(o_bias, m + 1)
            else:
                eng.wait_ge(o_last, 1)
            eng.dma_start(out[m * P:(m + 1) * P, :], on[:, m % 4, :]).then_inc(stored[m % 4], 16)
        for i in range(4):
            eng.wait_ge(stored[i], 16 * MT // 4)

    @block.tensor
    def _(eng):
        mm = nc.tensor.matmul

        def three(dst, w_hi, w_lo, x_hi, x_lo, first, last):
            mm(dst, w_hi, x_hi, start=first, stop=False)
            mm(dst, w_hi, x_lo, start=False, stop=False)
            return mm(dst, w_lo, x_hi, start=False, stop=last)

        def piece(it, part, parts):
            kind, name, h, p = it
            bank = bank_of(p)
            if part == 0 and p >= 4:
                wait_evacuated(eng, p - 2 if p >= 6 else p - 4)
            if kind == "tile":
                i = IN_TILES.index(name)
                n = UNIT[("in", i)]
                slot = RING_OF[n] % RINGS
                if part == 0 and h == 0:
                    eng.wait_ge(split_done, n + 1)
                for kt in range(part * KT // parts, (part + 1) * KT // parts):
                    c = slice(kt * P, (kt + 1) * P)
                    s_ = slice(h * HALF, (h + 1) * HALF)
                    if name == "dt":
                        mm(bank, wh[:, slot, c], xh[:, kt, s_], start=kt == 0, stop=False)
                        last = mm(bank, wh[:, slot, c], xl[:, kt, s_], start=False, stop=kt == KT - 1)
                    else:
                        last = three(bank, wh[:, slot, c], wl[:, slot, c], xh[:, kt, s_], xl[:, kt, s_],
                                     kt == 0, kt == KT - 1)
            elif kind == "turn":
                for hh_ in range(2):
                    wait_evacuated(eng, PLACE[(TURNED[name], hh_)])
                for j in range(4):
                    last = nc.tensor.transpose(bank[:, j * P:(j + 1) * P], vt[:, (4 * h + j) * P:(4 * h + j + 1) * P],
                                               table("ident"))
            else:
                eng.wait_ge(dt_v, 2)
                mm(bank[:, 0:DTN], table("tri_le"), sm[:, 5, :], start=True, stop=True)
                last = mm(bank[:, 64:64 + DTN], table("ones"), sm[:, 5, :], start=True, stop=True)
            if part == parts - 1:
                last.then_inc(p_full, 1)

        def z_scores(n):
            g, q_half, key, hd = STEPS[n]
            if n % PER_PAIR == 0:
                for name in ("q%d" % g, "k%d" % g):
                    for h in range(2):
                        wait_evacuated(eng, PLACE[(name, h)])
            if n >= 2:
                eng.wait_ge(zs_done, n - 1)
            r = slice(HEAD * hd, HEAD * hd + HEAD)
            kc = slice(key * P, (key + 1) * P)
            c0 = first_col(n)
            qc = slice(q_half * HALF + c0, (q_half + 1) * HALF)
            s_ = g % 2
            three(ps[:, 2 + n % 2, c0:], kh[s_][r, kc], kl[s_][r, kc], qh[s_][r, qc], ql[s_][r, qc],
                  True, True).then_inc(z_full, 1)

        def suffix(n):
            hd, c0 = STEPS[n][3], first_col(n)
            first = STEPS[n][2] == 4 * STEPS[n][1] + 3
            eng.wait_ge(lo_done, n + 1)
            dst = ps[:, 4 + hd, c0:]
            mm(dst, neg_ge[:, :], sph[:, n % 3, c0:], start=first, stop=False, skip_group_check=True)
            mm(dst, neg_ge[:, :], spl[:, n % 3, c0:], start=False, stop=True,
               skip_group_check=True).then_inc(tri_full, 1)

        def rest_and_values(n):
            g, q_half, key, hd = STEPS[n]
            c0 = first_col(n)
            eng.wait_ge(u_done, n + 1)
            if key:
                dst = ps[:, 4 + hd, c0:]
                mm(dst, neg_lt[:, :], sph[:, n % 3, c0:], start=False, stop=False, skip_group_check=True)
                mm(dst, neg_lt[:, :], spl[:, n % 3, c0:], start=False, stop=True, skip_group_check=True)
            first = key == 4 * q_half + 3
            o = 2 * g + q_half
            if first and o >= 2:
                eng.wait_ge(o_out, o - 1)
            if first and q_half == 0:
                for h in range(2):
                    wait_evacuated(eng, PLACE[("turn%d" % g, h)])
            eng.wait_ge(w_done, n + 1)
            r = slice(HEAD * hd, HEAD * hd + HEAD)
            mm(ps[r, 6 + o % 2, c0:], vn[g % 2][:, key, r], u[:, n % 2, c0:], start=first, stop=True,
               skip_group_check=True).then_inc(av_done, 1)

        for kt in range(KT):
            eng.wait_ge(split_done, UNIT[("x", kt)] + 1)
            c = slice(kt * P, (kt + 1) * P)
            for kind, name, h, p in PROLOGUE[:4]:
                s_ = slice(h * HALF, (h + 1) * HALF)
                i = IN_TILES.index(name)
                last = three(bank_of(p), wh[:, i, c], wl[:, i, c], xh[:, kt, s_], xl[:, kt, s_],
                             kt == 0, kt == KT - 1)
                if kt == KT - 1:
                    last.then_inc(p_full, 1)
        for it in PROLOGUE[4:]:
            if it[0] == "turn":
                eng.wait_ge(const_in, 48)
                eng.wait_ge(const_r, 1)
            piece(it, 0, 1)
        for n in range(-2, NSTEP):
            if n >= 0:
                suffix(n)
            if n + 2 < NSTEP:
                z_scores(n + 2)
            for pc in (BY_STEP[0] if n == -1 else BY_STEP[n] if n > 0 else []):
                piece(*pc)
            if n >= 0:
                rest_and_values(n)
        meet(eng, 1)

        def bank_pair(name):
            pair, before = task_place(name)
            if before and name[:2] == "sp":
                eng.wait_ge(var_done, 1)
            elif before:
                eng.wait_ge(d_free[pair], before)
            return two(pair)

        def turn(dst, src):
            return nc.tensor.transpose(dst, src, table("ident"))

        def evacuated(name):
            pair, before = task_place(name)
            eng.wait_ge(d_free[pair], before + 1)

        def out_rows(m, kts):
            if kts[0] == OUT_ORDER[0] and m < 2:
                pairs = [task_place(name) for name in TASKS]
                eng.wait_ge(d_free[m], max(b + 1 for q, b in pairs if q == m))
                eng.wait_ge(sb_split, 3)
            t = slice(m * P, (m + 1) * P)
            for kt in kts:
                eng.wait_ge(split_done, UNIT[("out", kt)] + 1)
                if kt < 2:
                    evacuated("po%d" % kt)
                elif kt < 5:
                    eng.wait_ge(ssd_split, (3, 2, 4).index(kt) + 1)
                for h in range(2):
                    c = slice(h * HALF, (h + 1) * HALF)
                    last = three(two(m % 2)[:, c], mh[:, kt, t], ml[:, kt, t], oh[kt][:, c], ol[kt][:, c],
                                 kt == OUT_ORDER[0], kt == OUT_ORDER[-1])
            return last

        for name in TASKS:
            kind, i = name[:2], int(name[2])
            if kind == "cu":
                eng.wait_ge(dt_v, 2)
            elif kind == "bt":
                eng.wait_ge(silu_done, 3 + i + 1)
            elif kind == "cb":
                eng.wait_ge(silu_done, 5 + i + 1)
            elif kind == "xt":
                eng.wait_ge(silu_done, 3)
            elif kind == "st":
                eng.wait_ge(xw_done, 2 * (i + 1))
                evacuated("bt1")
            elif kind == "yy":
                eng.wait_ge(wt_done, 2 * (i + 1))
                evacuated("st3")
            elif kind == "po":
                eng.wait_ge(pooled, 2)
            elif kind == "rm":
                eng.wait_ge(sq_done, 2)
            elif kind == "sp":
                if i == 0:
                    out_rows(1, (5, 6, 7))
                    for kt in (0, 1):
                        for m in range(2):
                            out_rows(m, (kt,))
            dst = bank_pair(name)
            if kind == "cu":
                for c in range(MT):
                    col = sm[:, 5, c * SSD_HEADS + i:c * SSD_HEADS + i + 1]
                    last = mm(dst[:, c * P:(c + 1) * P], col.broadcast_to([P, P]), table("tri_le"),
                              start=True, stop=True)
            elif kind == "bt":
                for c in range(MT):
                    last = turn(dst[:, c * P:(c + 1) * P], cv[:, 3 + i, c * P:(c + 1) * P])
            elif kind == "cb":
                for c in range(MT):
                    t = slice(c * P, (c + 1) * P)
                    last = mm(dst[:, t], cv[:, 3 + i, t], cv[:, 5 + i, t], start=True, stop=True)
            elif kind == "xt":
                for c in range(2):
                    for j in range(3):
                        last = turn(dst[:, c * HALF + j * P:c * HALF + (j + 1) * P],
                                    cv[:, j, (2 * i + c) * P:(2 * i + c + 1) * P])
            elif kind == "st":
                for c in range(2 if i < 3 else 1):
                    for g in range(2):
                        w = SSD_W // 2
                        last = mm(dst[:, c * HALF + g * w:c * HALF + (g + 1) * w], bn[:, g, 2 * i + c, :],
                                  xw[:, 2 * i + c, g * w:(g + 1) * w], start=True, stop=True)
            elif kind == "yy":
                for c in range(MT):
                    t = slice(c * P, (c + 1) * P)
                    for hd in range(2):
                        r = slice(HEAD * hd, HEAD * hd + HEAD)
                        f = slice((2 * i + hd) * HEAD, (2 * i + hd + 1) * HEAD)
                        mm(dst[r, t], xdt[:, c, f], wt[i % 2][:, hd, t], start=True, stop=False)
                        last = mm(dst[r, t], hs[:, c, f], ce[i % 2][:, hd, t], start=False, stop=True)
            elif kind == "po":
                for h in range(2):
                    s_ = slice(h * HALF, (h + 1) * HALF)
                    last = mm(dst[:, s_], pool_w[:, i, :], ht[:, 10 + i, s_], start=True, stop=True)
            elif kind == "rm":
                for j in range(3):
                    if j == 2:
                        out_rows(0, (5, 6, 7))
                        eng.wait_ge(sq_done, 3)
                    for h in range(2):
                        s_ = slice(h * HALF, (h + 1) * HALF)
                        last = mm(dst[:, s_], table("rms_%d" % j), cv[:, 3 + j, s_], start=j == 0, stop=j == 2)
            elif kind == "sp":
                for h in range(2):
                    s_ = slice(h * HALF, (h + 1) * HALF)
                    if i == 0:
                        eng.wait_ge(rms_done, h + 1)
                    last = mm(dst[:, s_], table("from_last" if i else "from_first"), tmp[:, s_],
                              start=True, stop=True)
            last.then_inc(d_full, 1)
        for kt in OUT_ORDER[5:]:
            for m in range(2):
                last = out_rows(m, (kt,))
                if kt == OUT_ORDER[-1]:
                    last.then_inc(y_full, 1)

        def back(m):
            eng.wait_ge(y_norm, m + 1)
            if m >= 2:
                eng.wait_ge(x1_done, m - 1)
            dst = two(2 + m % 2)
            for kt in range(KT):
                last = turn(dst[:, kt * P:(kt + 1) * P], yn[:, m % 2, kt * P:(kt + 1) * P])
            last.then_inc(t_full, 1)

        for m in range(2, MT):
            eng.wait_ge(y_read, m - 1)
            out_rows(m, OUT_ORDER).then_inc(y_full, 1)
            back(m - 2)
        back(MT - 2)

        def column_tile(item, slot, n, it=0, halves=(0, 1)):
            eng.wait_ge(split_done, n + 1 + 6 * it)
            for h in halves:
                s_ = slice(h * HALF, (h + 1) * HALF)
                for kt in range(KT):
                    c = slice(kt * P, (kt + 1) * P)
                    last = three(two(item % 2)[:, s_], wh[:, slot, c], wl[:, slot, c], mh[:, kt, s_], ml[:, kt, s_],
                                 kt == 0, kt == KT - 1)
                if h == 0 and item == LAST_UP:
                    last.then_inc(half_full, 1)
            if 1 in halves:
                last.then_inc(u_full, 1)

        def gate_item(j, halves=(0, 1)):
            n = UNIT[("gate", j)]
            column_tile(ple_item("gate", j), RING_OF[n] % RINGS, n, 0, halves)

        def proj_item(j):
            dst = two(ple_item("proj", j) % 2)
            c = slice(j * P, (j + 1) * P)
            for h in range(2):
                s_ = slice(h * HALF, (h + 1) * HALF)
                for i in range(PLE_TILES):
                    last = three(dst[:, s_], pwh[:, i, c], pwl[:, i, c], ph[:, i, s_], pl[:, i, s_],
                                 i == 0, i == PLE_TILES - 1)
            last.then_inc(u_full, 1)

        eng.wait_ge(x1_split, MT // 2)
        gate_item(0, (0,))
        back(MT - 1)
        eng.wait_ge(y_read, MT)
        gate_item(1, (0,))
        eng.wait_ge(x1_split, MT)
        gate_item(0, (1,))
        gate_item(1, (1,))
        eng.wait_ge(split_done, UNIT[("proj", 1)] + 1)
        for j in range(2):
            eng.wait_ge(sig_done, j + 1)
            proj_item(j)
        for j in range(2, KT):
            if j == 2:
                eng.wait_ge(u_free, 1)
            else:
                eng.wait_ge(sig_done, j)
            gate_item(j)
            eng.wait_ge(u_free, 2 * j - 1)
            proj_item(j)

        def up(t, n, it=0):
            if t == 0:
                eng.wait_ge(sig_done, KT)
            else:
                eng.wait_ge(u_free, 2 * KT + t - 1 + 4 * it)
            column_tile(2 * KT + t, RING_OF[n] % RINGS, n, it)

        def turn_back(m):
            if m in (0, MT // 2):
                eng.wait_ge(dn_added, 16 * (CHUNKS - 2) + 8 + 8 * (m // 4))
            if m == 0:
                eng.wait_ge(u_free, 2 * KT + 4 * CHUNKS - 1)
            elif m == 1:
                eng.wait_ge(half_conv, 2)
            elif m >= 2:
                eng.wait_ge(o_nrm, m - 1)
            for kt in range(KT):
                last = turn(two(m % 2)[:, kt * P:(kt + 1) * P], acc[:, kt, m * P:(m + 1) * P])
            last.then_inc(o_full, 1)

        def down(n, d, it=0):
            eng.wait_ge(split_done, n + 2 + 6 * it)
            eng.wait_ge(h_done, d // 8 + 2 + 2 * it)
            for k in range(16):
                j, h = k // 2, k % 2
                if d + k >= 4:
                    eng.wait_ge(dn_added, d + k - 3 + 16 * it)
                s_, c = slice(h * HALF, (h + 1) * HALF), slice(j * P, (j + 1) * P)
                for i in range(2):
                    slot = (RING_OF[n] + i) % RINGS
                    last = three(ps[:, 4 + k % 4, :], wh[:, slot, c], wl[:, slot, c], hh[:, i, s_], hl[:, i, s_],
                                 i == 0, i == 1)
                last.then_inc(dn_full, 1)

        def last_down(n, d):
            def part(k, i):
                s_, c = slice(k // 8 * HALF, (k // 8 + 1) * HALF), slice(k % 8 * P, (k % 8 + 1) * P)
                h_, l_ = (hh, hl) if i < 2 else (h2h, h2l)
                w_h, w_l = unit_place(n + i, False), unit_place(n + i, True)
                return three(ps[:, 4 + k % 4, :], w_h[:, c], w_l[:, c], h_[:, i % 2, s_], l_[:, i % 2, s_],
                             i == 0, i == 3)

            eng.wait_ge(split_done, n + 2)
            eng.wait_ge(h_done, 2 * (CHUNKS - 1))
            for k in range(4):
                eng.wait_ge(dn_added, d + k - 3)
                part(k, 0)
                part(k, 1)
            eng.wait_ge(split_done, n + 4)
            eng.wait_ge(half_done, 1)
            for k in range(16):
                if k == 8:
                    eng.wait_ge(half_done, 2)
                if k in (9, 10, 12, 13):
                    turn_back((9, 10, 12, 13).index(k))
                if k >= 4:
                    eng.wait_ge(dn_added, d + k - 3)
                    part(k, 0)
                    part(k, 1)
                part(k, 2)
                part(k, 3).then_inc(dn_full, 1)

        for t in range(4):
            up(t, FFN0 + t)
        n1 = FFN0 + 4

        def chunk(c, n, it=0):
            up(4 * c, n, it)
            down(n + 1, 16 * (c - 1), it)
            for t in (1, 2, 3):
                up(4 * c + t, n + 2 + t, it)

        chunk(1, n1)
        with eng.Fori(0, CHUNKS - 3) as it:
            chunk(2, n1 + 6, it)
        n = len(UNITS) - 8
        for t in range(4):
            up(4 * (CHUNKS - 1) + t, n + t)
        last_down(n + 4, 16 * (CHUNKS - 2))
        for m in range(MT // 2, MT):
            turn_back(m)

    @block.scalar
    def _(eng):
        act = nc.scalar.activation

        def evacuate(it):
            kind, name, h, p = it
            if kind == "sums" or (kind == "turn" and name == 3):
                return
            eng.wait_ge(p_full, p + 1)
            bank = bank_of(p)
            s_ = slice(h * HALF, (h + 1) * HALF)
            if kind == "turn":
                act(vn[name % 2][:, 4 * h:4 * h + 4, :].rearrange("p m n -> p (m n)"), bank,
                    ACT.Copy).then_inc(p_free[p % 2], 1)
            elif name in H_TILES:
                if name == "p1":
                    for hh_ in range(2):
                        wait_evacuated(eng, PLACE[("turn3", hh_)])
                act(ht[:, H_TILES.index(name), s_], bank, ACT.Copy).then_inc(p_free[p % 2], 1)
            elif name in TURNED:
                g = TURNED.index(name)
                if g:
                    for hh_ in range(2):
                        wait_evacuated(eng, PLACE[("turn%d" % (g - 1), hh_)])
                act(vt[:, s_], bank, ACT.Copy).then_inc(p_free[p % 2], 1)
            else:
                g = int(name[1])
                act((qh if name[0] == "q" else kh)[g % 2][:, s_], bank, ACT.Copy).then_inc(qk_hi, 1)

        for n in range(UNIT[("in", 2)]):
            hi(n)
        eng.wait_ge(const_in, 48)
        act(neg_ge[:, :], table("neg_ge"), ACT.Copy)
        act(neg_lt[:, :], table("neg_lt"), ACT.Copy).then_inc(const_r, 1)
        nc.scalar.preload_act_table_set("natural_log_exp_and_others")
        hi(UNIT[("in", 2)])
        for it in PROLOGUE[:4]:
            evacuate(it)
        hi(UNIT[("in", 3)])
        hi(UNIT[("in", 4)])
        for it in PROLOGUE[4:]:
            evacuate(it)
        for n in range(-2, NSTEP + 1):
            if 0 <= n + 1 < NSTEP:
                k, c0 = n + 1, first_col(n + 1)
                eng.wait_ge(zs_done, k + 1)
                act(na[:, k % 2, c0:], na[:, k % 2, c0:], ACT.Exp, scale=-1.0).then_inc(e_done, 1)
                eng.wait_ge(e_done, k + 1)
                act(na[:, k % 2, c0:], na[:, k % 2, c0:], ACT.Ln, bias=1.0).then_inc(l_done, 1)
            if 0 <= n < NSTEP:
                c0 = first_col(n)
                eng.wait_ge(u_done, n + 1)
                act(u[:, n % 2, c0:], u[:, n % 2, c0:], ACT.Exp).then_inc(w_done, 1)
            if 0 <= n + 2 < NSTEP:
                k, c0 = n + 2, first_col(n + 2)
                eng.wait_ge(z_full, k + 1)
                if k >= 3:
                    eng.wait_ge(u_done, k - 2)
                act(zs[:, k % 3, c0:], ps[:, 2 + k % 2, c0:], ACT.Copy, scale=SCALE)
                act(na[:, k % 2, c0:], ps[:, 2 + k % 2, c0:], ACT.Abs, scale=SCALE).then_inc(zs_done, 1)
            for it in (DONE_AT[n - 1] if 1 <= n <= NSTEP else []):
                evacuate(it)
            for r in SPLIT_AT.get(n, []):
                hi(UNIT[("in", r)])
            if n in CONV_AT:
                j = CONV_AT.index(n)
                for hh_ in range(2):
                    wait_evacuated(eng, PLACE[(H_TILES[j], hh_)])
                if j:
                    eng.wait_ge(conv_done, j)
                act(cv[:, j, :], ht[:, j, :], ACT.Identity, scale=param("conv_w", 4 * j + 3),
                    bias=param("conv_b", j)).then_inc(tap_done, 1)
            if n == DT_AT + 1:
                eng.wait_ge(dt_v, 1)
                act(sm[:, 2, :], sm[:, 1, :], ACT.Exp).then_inc(dt_a, 1)
                eng.wait_ge(dt_a, 1)
                act(sm[:, 2, :], sm[:, 2, :], ACT.Ln, bias=1.0)
                act(sm[:, 4, :], param("a_log", 0, DTN), ACT.Exp).then_inc(dt_a, 1)
            if n == SUMS_AT:
                eng.wait_ge(decay_done, 1)
                act(sm[:, 8, :], sm[:, 8, :], ACT.Exp).then_inc(dt_a, 1)
                act(sm[:, 9, :], sm[:, 7, :], ACT.Exp).then_inc(dt_a, 1)
            if n >= 1 and STEPS[n - 1][2] == 0 and STEPS[n - 1][3] == 1:
                g, q_half = STEPS[n - 1][:2]
                eng.wait_ge(av_done, n)
                act(sb[:, g, q_half * HALF:(q_half + 1) * HALF], ps[:, 6 + q_half, :],
                    ACT.Copy).then_inc(o_out, 1)
            if n == NSTEP - 1:
                eng.wait_ge(conv_done, 7)
                for j in range(3):
                    act(cv[:, j, :], cv[:, j, :], ACT.Silu).then_inc(silu_done, 1)
        meet(eng, 1)

        def task(name):
            eng.wait_ge(d_full, TASKS.index(name) + 1)
            pair = task_place(name)[0]
            return two(pair), d_free[pair]

        for j in (3, 4):
            act(cv[:, j, :], cv[:, j, :], ACT.Silu).then_inc(silu_done, 1)
        for g in range(2):
            src, free = task("bt%d" % g)
            act(bn[:, g, :, :].rearrange("p m n -> p (m n)"), src, ACT.Copy).then_inc(free, 1)
        for j in (5, 6):
            act(cv[:, j, :], cv[:, j, :], ACT.Silu).then_inc(silu_done, 1)
        for j in range(3):
            act(ht[:, 7 + j, :], ht[:, 7 + j, :], ACT.Silu).then_inc(silu_done, 1)
        for g in range(2):
            src, free = task("cb%d" % g)
            act(cb[:, g, :], src, ACT.Copy).then_inc(free, 1)
        def exponents(h):
            eng.wait_ge(arg_done, h + 1)
            if h >= 4:
                eng.wait_ge(d_full, TASKS.index("yy0") + 1)
            elif h >= 2:
                eng.wait_ge(sb_split, 3)
                eng.wait_ge(d_full, TASKS.index("st3") + 1)
            act(wt[h // 2 % 2][:, h % 2, :], tmp[:, :], ACT.Exp).then_inc(wexp_done, 1)
            src, free = task("cu%d" % h)
            act(ce[h // 2 % 2][:, h % 2, :], src, ACT.Exp).then_inc(free, 1)

        def squared(i):
            eng.wait_ge(hg_done, i + 1)
            act(cv[:, 3 + i, :], cv[:, i, :], ACT.Square).then_inc(sq_done, 1)

        nc.scalar.preload_act_table_set("natural_log_exp_and_others")
        def pool_mean(i):
            eng.wait_ge(pool_sum, i + 1)
            for src, rows in ((pa, slice(0, HEAD)), (pb, slice(HEAD, P))):
                inv = par[rows, PARAMS["pool_inv"] + i:PARAMS["pool_inv"] + i + 1]
                last = act(pb[rows, :], src[rows, :], ACT.Copy, scale=inv)
            last.then_inc(pool_scaled, 1)

        pool_mean(0)
        for h in range(SSD_HEADS):
            exponents(h)
            if h == 2:
                pool_mean(1)
        squared(0)
        eng.wait_ge(d_full, TASKS.index("yy1") + 1)
        hi(UNIT[("out", 5)])
        hi(UNIT[("out", 6)])
        for k in range(2):
            src, free = task("po%d" % k)
            act(mh[:, k, :], src, ACT.Copy, scale=param("pool_scale", k)).then_inc(mixh, 1)
        squared(1)
        hi(UNIT[("out", 7)])
        squared(2)
        nc.scalar.preload_act_table(ACT.Sqrt)
        for k in (0, 1):
            hi(UNIT[("out", k)])
        eng.wait_ge(var_done, 1)
        act(tmp[:, :], tmp[:, :], ACT.Sqrt).then_inc(sqrt_done, 1)
        for k, unit in enumerate(OUT_ORDER[5:]):
            hi(UNIT[("out", unit)])
            i = (1, 0, 2)[k]
            eng.wait_ge(nrm_done, k + 1)
            act(mh[:, 2 + i, :], cv[:, i, :], ACT.Copy).then_inc(mixh, 1)

        def gain_bias(m):
            eng.wait_ge(t_full, m + 1)
            for kt in range(KT):
                last = act(acc[:, kt, m * P:(m + 1) * P], two(2 + m % 2)[:, kt * P:(kt + 1) * P], ACT.Identity,
                           scale=param("ln1_g", kt), bias=param("ln1_b", kt))
            last.then_inc(x1_done, 1)

        hi(UNIT[("gate", 0)])
        for m in range(MT):
            if m == 1:
                hi(UNIT[("gate", 1)])
            eng.wait_ge(v_eps, m + 1)
            act(st[:, m, 15:16], st[:, m, 14:15], ACT.Sqrt).then_inc(v_sqrt, 1)
            if m >= 2:
                gain_bias(m - 2)
        gain_bias(MT - 2)
        for i in range(PLE_TILES):
            hi(UNIT[("p", i)])
        gain_bias(MT - 1)

        for i in range(PLE_TILES):
            hi(UNIT[("proj", i)])
        hi(UNIT[("gate", 2)])
        for j in range(KT):
            item = ple_item("gate", j)
            eng.wait_ge(u_full, item + 1)
            if j >= 2:
                eng.wait_ge(u_free, 2 * j - 2)
            act(sig[:, j % 2, :], two(item % 2), ACT.Sigmoid).then_inc(sig_done, 1)
            hi(UNIT[("gate", j + 3)] if j + 3 < KT else FFN0 + j + 3 - KT)

        def tap(c, t, it=0):
            item = 2 * KT + 4 * c + t
            eng.wait_ge(u_full, item + 1 + 4 * it)
            if c or t >= 2:
                eng.wait_ge(h_done, 2 * c + t // 2 + 2 * it)
            w, b = PARAMS["ff_w"] + 3 * (4 * c + t) + 2, PARAMS["ff_b"] + 4 * c + t
            act(cf[:, t % 2, :], two(item % 2), ACT.Identity, scale=column(w, 12, it),
                bias=column(b, 4, it)).then_inc(tap_ff, 1)

        def column(c, step, it):
            return par[:, c:c + 1] if isinstance(it, int) else par[:, bass.ds(c + step * it, 1)]

        def gate(c, i, it=0):
            eng.wait_ge(u_free, 2 * KT + 4 * c + 2 * i + 1 + 4 * it)
            act(cf[:, 0, :], cf[:, 0, :], ACT.Silu).then_inc(silu_ff, 1)

        hi(FFN0 + 3)
        tap(0, 0)
        gate(0, 0)
        tap(0, 1)
        hi(FFN0 + 4)
        tap(0, 2)
        gate(0, 1)
        hi(FFN0 + 5)
        tap(0, 3)
        hi(FFN0 + 6)

        def chunk(c, n, it=0):
            tap(c, 0, it)
            hi(n + 3, it)
            gate(c, 0, it)
            hi(n + 4, it)
            hi(n + 5, it)
            tap(c, 1, it)
            hi(n + 6, it)
            tap(c, 2, it)
            gate(c, 1, it)
            hi(n + 7, it)
            tap(c, 3, it)
            hi(n + 8, it)

        n1 = FFN0 + 4
        chunk(1, n1)
        with eng.Fori(0, CHUNKS - 3) as it:
            chunk(2, n1 + 6, it)
        c, n = CHUNKS - 1, len(UNITS) - 8
        tap(c, 0)
        hi(n + 3)
        gate(c, 0)
        tap(c, 1)
        hi(n + 4)
        tap(c, 2)
        gate(c, 1)
        hi(n + 5)
        hi(n + 6)
        hi(n + 7)
        eng.wait_ge(h_done, 2 * c + 1)
        for h in range(2):
            eng.wait_ge(*((half_full, 1) if h == 0 else (u_full, LAST_UP + 1)))
            s_ = slice(h * HALF, (h + 1) * HALF)
            act(cf[:, 1, s_], two(LAST_UP % 2)[:, s_], ACT.Identity, scale=param("ff_w", 3 * (4 * c + 3) + 2),
                bias=param("ff_b", 4 * c + 3)).then_inc(half_tap, 1)

        for m in range(MT):
            eng.wait_ge(o_eps, m + 1)
            act(st[:, m, 15:16], st[:, m, 14:15], ACT.Sqrt).then_inc(o_sqrt, 1)
            eng.wait_ge(o_aff, m + 1)
            if m >= 4:
                eng.wait_ge(stored[m % 4], 16 * (m // 4))
            act(on[:, m % 4, :], two(m % 2), ACT.Identity, scale=st[:, m, 13:14],
                bias=st[:, m, 12:13]).then_inc(o_nrm, 1)

    @block.vector
    def _(eng):
        v = nc.vector
        chained = [0]

        def link(ins):
            chained[0] += 1
            ins.then_inc(dve_chain, 1)
            eng.wait_ge(dve_chain, chained[0])

        def evacuate(it):
            kind, name, h, p = it
            if kind == "sums":
                eng.wait_ge(p_full, p + 1)
                v.tensor_copy(sm[:, 6:8, :], ps[:, p % 2, 0:128].rearrange("p (k n) -> p k n", k=2)[:, :, 0:DTN]
                              ).then_inc(p_free[p % 2], 1)
                wait_evacuated(eng, p)
                v.tensor_tensor(sm[:, 8, :], sm[:, 7, :], sm[:, 6, :], ALU.subtract).then_inc(decay_done, 1)
            elif kind == "turn" and name == 3:
                eng.wait_ge(p_full, p + 1)
                f = slice(4 * h * SSD_HEADS, 4 * (h + 1) * SSD_HEADS)
                by_tile = lambda ap: ap.rearrange("p (m n) -> p m n", m=4)
                src = by_tile(ps[:, p % 2, :])
                link(v.tensor_tensor(by_tile(sm[:, 0, f]), src[:, :, 0:SSD_HEADS],
                                     by_tile(param("dt_bias", 4 * h * SSD_HEADS, 4 * SSD_HEADS)), ALU.add))
                v.tensor_tensor(by_tile(sm[:, 0, f]), by_tile(sm[:, 0, f]), src[:, :, HEAD:HEAD + SSD_HEADS],
                                ALU.add).then_inc(p_free[p % 2], 1)
            elif kind == "tile" and name[0] in "qk":
                g, s_ = int(name[1]), slice(h * HALF, (h + 1) * HALF)
                eng.wait_ge(qk_hi, QK_ORDER.index((name, h)) + 1)
                hi_, lo_ = (qh, ql) if name[0] == "q" else (kh, kl)
                v.tensor_tensor(lo_[g % 2][:, s_], bank_of(p), hi_[g % 2][:, s_].bitcast(F32),
                                ALU.subtract).then_inc(p_free[p % 2], 1)

        def split_dt(n):
            eng.wait_ge(hi_done, n + 1)
            second = lambda ap: ap.rearrange("p (k c) -> p k c", k=KT)[:, :, HEAD:HEAD + SSD_HEADS]
            h_, l_ = unit_place(n, False), unit_place(n, True)
            link(v.tensor_tensor(l_, unit_raw(n), h_.bitcast(F32), ALU.subtract))
            v.tensor_copy(second(h_), second(l_).bitcast(F32)).then_inc(split_done, 1)

        for n in range(UNIT[("in", 2)] + 1):
            lo(n)
        eng.wait_ge(const_in, 48)
        for it in PROLOGUE[:4]:
            evacuate(it)
        lo(UNIT[("in", 3)])
        lo(UNIT[("in", 4)])
        for it in PROLOGUE[4:]:
            evacuate(it)
        for n in range(-2, NSTEP + 1):
            if 0 <= n < NSTEP:
                c0, hd = first_col(n), STEPS[n][3]
                eng.wait_ge(tri_full, n + 1)
                if n >= 2:
                    eng.wait_ge(av_done, n - 1)
                ins = v.tensor_tensor(u[:, n % 2, c0:], zs[:, n % 3, c0:], ps[:, 4 + hd, c0:], ALU.add)
                if on_diagonal(n):
                    link(ins)
                    d = u[:, n % 2, c0:c0 + P]
                    ins = v.tensor_tensor(d, d, table("cap_lt"), ALU.min)
                ins.then_inc(u_done, 1)
            if 0 <= n + 1 < NSTEP:
                k, c0 = n + 1, first_col(n + 1)
                eng.wait_ge(l_done, k + 1)
                if k:
                    eng.wait_ge(lo_done, k)
                link(v.scalar_tensor_tensor(out=sp[:, c0:], in0=zs[:, k % 3, c0:], scalar=0.0,
                                            in1=na[:, k % 2, c0:], op0=ALU.max, op1=ALU.add))
                if on_diagonal(k):
                    d = sp[:, c0:c0 + P]
                    link(v.tensor_tensor(d, d, table("mask_lt"), ALU.mult))
                if k >= 3:
                    eng.wait_ge(av_done, k - 2)
                link(v.tensor_copy(sph[:, k % 3, c0:], sp[:, c0:]))
                v.tensor_tensor(spl[:, k % 3, c0:], sp[:, c0:], sph[:, k % 3, c0:].bitcast(F32),
                                ALU.subtract).then_inc(lo_done, 1)
            for it in (DONE_AT[n - 1] if 1 <= n <= NSTEP else []):
                evacuate(it)
            for r in SPLIT_AT.get(n, []):
                if IN_TILES[r] == "dt":
                    split_dt(UNIT[("in", r)])
                else:
                    lo(UNIT[("in", r)])
            for j, at in enumerate(TAPS_AT):
                if n in at:
                    b = at.index(n) + 1
                    if b == 1:
                        eng.wait_ge(tap_done, j + 1)
                    ins = v.scalar_tensor_tensor(out=cv[:, j, b:], in0=ht[:, j, :S - b],
                                                 scalar=param("conv_w", 4 * j + 3 - b), in1=cv[:, j, b:],
                                                 op0=ALU.mult, op1=ALU.add)
                    if b < CONV - 1:
                        link(ins)
                    else:
                        ins.then_inc(conv_done, 1)
            if n == DT_AT:
                wait_evacuated(eng, PLACE[("turn3", 1)])
                v.tensor_scalar(sm[:, 1, :].bitcast(I32), sm[:, 0, :].bitcast(I32), SIGN, None,
                                ALU.bitwise_or).then_inc(dt_v, 1)
            if n == DT_AT + 2:
                eng.wait_ge(dt_a, 2)
                link(v.scalar_tensor_tensor(out=sm[:, 3, :], in0=sm[:, 0, :], scalar=0.0, in1=sm[:, 2, :],
                                            op0=ALU.max, op1=ALU.add))
                v.scalar_tensor_tensor(out=sm[:, 5, :], in0=sm[:, 3, :], scalar=-1.0, in1=sm[:, 4, :],
                                       op0=ALU.mult, op1=ALU.mult).then_inc(dt_v, 1)
        meet(eng, 1)

        def task(name):
            eng.wait_ge(d_full, TASKS.index(name) + 1)
            pair = task_place(name)[0]
            return two(pair), d_free[pair]

        def evacuated(name):
            pair, before = task_place(name)
            eng.wait_ge(d_free[pair], before + 1)

        eng.wait_ge(dt_a, 4)
        for k in range(4):
            src, free = task("xt%d" % k)
            for c in range(2):
                ch = 2 * k + c
                ins = v.tensor_tensor(heads(xdt[:, ch, :]), heads(src[:, c * HALF:c * HALF + SSD_W]),
                                      per_head(3, ch), ALU.mult)
                (ins.then_inc(free, 1) if c else ins.then_inc(xdt_done, 1))

        def argument(h):
            src, _ = task("cu%d" % h)
            if h:
                eng.wait_ge(wexp_done, h)
            for c in range(MT):
                t = slice(c * P, (c + 1) * P)
                ins = v.scalar_tensor_tensor(out=tmp[:, t], in0=src[:, t],
                                             scalar=sm[:, 6, c * SSD_HEADS + h:c * SSD_HEADS + h + 1],
                                             in1=table("cap_le"), op0=ALU.subtract, op1=ALU.min)
            ins.then_inc(arg_done, 1)

        def decayed(h):
            g = h // 3
            w, c_ = wt[h // 2 % 2][:, h % 2, :], ce[h // 2 % 2][:, h % 2, :]
            eng.wait_ge(wexp_done, h + 1)
            v.tensor_tensor(w, w, cb[:, g, :], ALU.mult)
            evacuated("cu%d" % h)
            v.tensor_tensor(c_, c_, cv[:, 5 + g, :], ALU.mult).then_inc(wt_done, 1)

        def gated(i):
            src, free = task("yy%d" % i)
            eng.wait_ge(silu_done, 10)
            v.scalar_tensor_tensor(out=cv[:, i, :], in0=cv[:, i, :], scalar=param("ssd_d", i), in1=src,
                                   op0=ALU.mult, op1=ALU.add).then_inc(free, 1)
            evacuated("yy%d" % i)
            v.tensor_tensor(cv[:, i, :], cv[:, i, :], ht[:, 7 + i, :], ALU.mult).then_inc(hg_done, 1)

        for g in range(PAIRS):
            v.tensor_copy(mh[:, 5 + g, :], sb[:, g, :]).then_inc(mixh, 1)
        for k in range(4):
            src, free = task("st%d" % k)
            for c in range(2 if k < 3 else 1):
                ch = 2 * k + c
                if ch == 0:
                    eng.wait_ge(pool_chain, 1)
                link(v.tensor_tensor(heads(hs[:, ch + 1, :]), heads(hs[:, ch, :]), per_head(9, ch), ALU.mult))
                ins = v.tensor_tensor(hs[:, ch + 1, :], hs[:, ch + 1, :], src[:, c * HALF:c * HALF + SSD_W], ALU.add)
                if c or k == 3:
                    ins.then_inc(free, 1)
                    evacuated("st%d" % k)
                else:
                    link(ins)
        argument(0)
        argument(1)
        decayed(0)
        argument(2)
        decayed(1)
        argument(3)
        decayed(2)
        gated(0)
        argument(4)
        decayed(3)
        argument(5)
        decayed(4)
        gated(1)
        decayed(5)
        for k in range(2):
            src, free = task("po%d" % k)
            eng.wait_ge(mixh, 4 + k)
            v.scalar_tensor_tensor(out=ml[:, k, :], in0=src, scalar=param("pool_scale", k),
                                   in1=mh[:, k, :].bitcast(F32), op0=ALU.mult, op1=ALU.subtract).then_inc(free, 1)
        gated(2)
        eng.wait_ge(split_done, UNIT[("out", 7)])
        lo(UNIT[("out", 7)])

        def normalised(k):
            i = (1, 0, 2)[k]
            src = task("sp%d" % i)[0] if k else tmp[:, :]
            v.scalar_tensor_tensor(out=cv[:, i, :], in0=cv[:, i, :], scalar=param("norm_w", i), in1=src,
                                   op0=ALU.mult, op1=ALU.mult).then_inc(nrm_done, 1)

        def mix_lo(k):
            i = (1, 0, 2)[k]
            eng.wait_ge(mixh, 6 + k)
            v.tensor_tensor(ml[:, 2 + i, :], cv[:, i, :], mh[:, 2 + i, :].bitcast(F32),
                            ALU.subtract).then_inc(ssd_split, 1)

        lo(UNIT[("out", 0)])
        src, free = task("rm0")
        v.tensor_scalar(tmp[:, :], src, 1.0 / (SSD_W // 2), RMS_EPS, ALU.mult, ALU.add).then_inc(var_done, 1)
        lo(UNIT[("out", 1)])
        eng.wait_ge(sqrt_done, 1)
        for h in range(2):
            s_ = slice(h * HALF, (h + 1) * HALF)
            v.reciprocal(tmp[:, s_], tmp[:, s_]).then_inc(rms_done, 1)
        eng.wait_ge(rms_done, 2)
        normalised(0)
        lo(UNIT[("out", OUT_ORDER[5])])
        mix_lo(0)
        normalised(1)
        lo(UNIT[("out", OUT_ORDER[6])])
        mix_lo(1)
        normalised(2)
        lo(UNIT[("out", OUT_ORDER[7])])
        mix_lo(2)

        lo(UNIT[("gate", 0)])

        def statistics(m, rows):
            v.bn_stats(st[:, m, 0:6], rows[:, 0:HALF])
            link(v.bn_stats(st[:, m, 6:12], rows[:, HALF:D]))
            link(v.bn_aggr(st[:, m, 12:14], st[:, m, 0:12]))
            return v.tensor_scalar(st[:, m, 14:15], st[:, m, 13:14], LN_EPS, None, ALU.add)

        def split_x1(m):
            eng.wait_ge(x1_done, m + 1)
            t = slice(m * P, (m + 1) * P)
            link(v.tensor_copy(mh[:, :, t], acc[:, :, t]))
            v.tensor_tensor(ml[:, :, t], acc[:, :, t], mh[:, :, t].bitcast(F32), ALU.subtract).then_inc(x1_split, 1)

        for m in range(MT):
            if m == 1:
                lo(UNIT[("gate", 1)])
            eng.wait_ge(y_full, m + 1)
            eng.wait_ge(x_in, 16 * (m + 1))
            if m >= 2:
                eng.wait_ge(t_full, m - 1)
            v.scalar_tensor_tensor(out=yn[:, m % 2, :], in0=xn[:, :], scalar=ALPHA, in1=two(m % 2),
                                   op0=ALU.mult, op1=ALU.add).then_inc(y_read, 1)
            eng.wait_ge(y_read, m + 1)
            statistics(m, yn[:, m % 2, :]).then_inc(v_eps, 1)
            if 2 <= m < MT - 1:
                split_x1(m - 2)
            eng.wait_ge(v_sqrt, m + 1)
            link(v.reciprocal(st[:, m, 15:16], st[:, m, 15:16]))
            v.tensor_scalar(yn[:, m % 2, :], yn[:, m % 2, :], st[:, m, 12:13], st[:, m, 15:16], ALU.subtract,
                            ALU.mult).then_inc(y_norm, 1)
        split_x1(MT - 3)
        split_x1(MT - 2)
        for i in range(PLE_TILES):
            lo(UNIT[("p", i)])
        split_x1(MT - 1)

        for i in range(PLE_TILES):
            lo(UNIT[("proj", i)])
        lo(UNIT[("gate", 2)])
        for j in range(KT):
            item = ple_item("proj", j)
            eng.wait_ge(sig_done, j + 1)
            eng.wait_ge(u_full, item + 1)
            v.tensor_tensor(sig[:, j % 2, :], sig[:, j % 2, :], two(item % 2), ALU.mult).then_inc(u_free, 1)
            eng.wait_ge(u_free, 2 * j + 1)
            v.scalar_tensor_tensor(out=acc[:, j, :], in0=acc[:, j, :], scalar=ALPHA, in1=sig[:, j % 2, :],
                                   op0=ALU.mult, op1=ALU.add).then_inc(u_free, 1)
            lo(UNIT[("gate", j + 3)] if j + 3 < KT else FFN0 + j + 3 - KT)

        def column(c, step, it):
            return par[:, c:c + 1] if isinstance(it, int) else par[:, bass.ds(c + step * it, 1)]

        def conv(c, t, it=0):
            item = 2 * KT + 4 * c + t
            src = two(item % 2)
            w = PARAMS["ff_w"] + 3 * (4 * c + t)
            eng.wait_ge(tap_ff, 4 * c + t + 1 + 4 * it)
            v.scalar_tensor_tensor(out=cf[:, t % 2, 1:], in0=src[:, :S - 1], scalar=column(w + 1, 12, it),
                                   in1=cf[:, t % 2, 1:], op0=ALU.mult, op1=ALU.add).then_inc(tap_mid, 1)
            eng.wait_ge(tap_mid, 4 * c + t + 1 + 4 * it)
            v.scalar_tensor_tensor(out=cf[:, t % 2, 2:], in0=src[:, :S - 2], scalar=column(w, 12, it),
                                   in1=cf[:, t % 2, 2:], op0=ALU.mult, op1=ALU.add).then_inc(u_free, 1)

        def product(c, i, it=0):
            eng.wait_ge(silu_ff, 2 * c + i + 1 + 2 * it)
            eng.wait_ge(u_free, 2 * KT + 4 * c + 2 * i + 2 + 4 * it)
            v.tensor_tensor(hf[:, :], cf[:, 0, :], cf[:, 1, :], ALU.mult).then_inc(prod_mid, 1)
            eng.wait_ge(prod_mid, 2 * (2 * c + i) + 1 + 4 * it)
            last = c == CHUNKS - 1
            hi_, lo_ = (h2h, h2l) if last else (hh, hl)
            if c and not last:
                eng.wait_ge(dn_full, 16 * c + 16 * it)
            v.tensor_copy(hi_[:, i, :], hf[:, :]).then_inc(prod_mid, 1)
            eng.wait_ge(prod_mid, 2 * (2 * c + i) + 2 + 4 * it)
            v.tensor_tensor(lo_[:, i, :], hf[:, :], hi_[:, i, :].bitcast(F32), ALU.subtract).then_inc(h_done, 1)

        def add_down(c, it=0, by_half=False, ks=range(16)):
            for k in ks:
                eng.wait_ge(dn_full, 16 * c + k + 1 + 16 * it)
                j, h = (k % 8, k // 8) if by_half else (k // 2, k % 2)
                dst = acc[:, j, h * HALF:(h + 1) * HALF]
                if k == 0:
                    eng.wait_ge(u_free, 2 * KT)
                    if c:
                        eng.wait_ge(dn_added, 16 * c + 16 * it)
                v.tensor_tensor(dst, dst, ps[:, 4 + k % 4, :], ALU.add).then_inc(dn_added, 1)

        lo(FFN0 + 3)
        conv(0, 0)
        conv(0, 1)
        lo(FFN0 + 4)
        product(0, 0)
        conv(0, 2)
        lo(FFN0 + 5)
        conv(0, 3)
        product(0, 1)
        lo(FFN0 + 6)

        def chunk(c, n, it=0):
            conv(c, 0, it)
            add_down(c - 1, it, ks=range(6))
            lo(n + 3, it)
            add_down(c - 1, it, ks=range(6, 16))
            lo(n + 4, it)
            lo(n + 5, it)
            conv(c, 1, it)
            product(c, 0, it)
            lo(n + 6, it)
            conv(c, 2, it)
            lo(n + 7, it)
            conv(c, 3, it)
            product(c, 1, it)
            lo(n + 8, it)

        n1 = FFN0 + 4
        chunk(1, n1)
        with eng.Fori(0, CHUNKS - 3) as it:
            chunk(2, n1 + 6, it)
        c, n = CHUNKS - 1, len(UNITS) - 8
        conv(c, 0)
        lo(n + 3)
        conv(c, 1)
        product(c, 0)
        lo(n + 4)
        conv(c, 2)
        lo(n + 5)
        lo(n + 6)
        lo(n + 7)

        def last_half(h):
            src, w = two(LAST_UP % 2), 3 * (4 * c + 3)
            s_ = slice(h * HALF, (h + 1) * HALF)
            eng.wait_ge(half_tap, h + 1)
            for b, done in ((1, half_mid), (2, half_conv)):
                t = slice(max(h * HALF, b), (h + 1) * HALF)
                v.scalar_tensor_tensor(out=cf[:, 1, t], in0=src[:, t.start - b:t.stop - b],
                                       scalar=param("ff_w", w + 2 - b), in1=cf[:, 1, t],
                                       op0=ALU.mult, op1=ALU.add).then_inc(done, 1)
                eng.wait_ge(done, h + 1)
            eng.wait_ge(silu_ff, 2 * CHUNKS)
            link(v.tensor_tensor(hf[:, s_], cf[:, 0, s_], cf[:, 1, s_], ALU.mult))
            link(v.tensor_copy(h2h[:, 1, s_], hf[:, s_]))
            v.tensor_tensor(h2l[:, 1, s_], hf[:, s_], h2h[:, 1, s_].bitcast(F32), ALU.subtract).then_inc(half_done, 1)

        last_half(0)
        last_half(1)
        add_down(c - 1, 0, True, range(9))

        eng.wait_ge(ln_in, 32)

        def gain(m):
            eng.wait_ge(o_nrm, m + 1)
            v.tensor_tensor(on[:, m % 4, :], on[:, m % 4, :], lng[:, :], ALU.mult).then_inc(o_gain, 1)

        for m in range(MT):
            eng.wait_ge(o_full, m + 1)
            statistics(m, two(m % 2)).then_inc(o_eps, 1)
            if m < 4:
                add_down(c - 1, 0, True, ((9,), (10, 11), (12, 13), (14, 15))[m])
            if m - 1 in GAIN_ON_VECTOR:
                gain(m - 1)
            eng.wait_ge(o_sqrt, m + 1)
            link(v.reciprocal(st[:, m, 13:14], st[:, m, 15:16]))
            v.scalar_tensor_tensor(out=st[:, m, 12:13], in0=st[:, m, 12:13], scalar=-1.0, in1=st[:, m, 13:14],
                                   op0=ALU.mult, op1=ALU.mult).then_inc(o_aff, 1)
        m = MT - 1
        gain(m)
        eng.wait_ge(o_gain, len(GAIN_ON_VECTOR))
        v.tensor_tensor(on[:, m % 4, :], on[:, m % 4, :], lnb[:, :], ALU.add).then_inc(o_last, 1)

    @block.gpsimd
    def _(eng):
        g = nc.gpsimd
        chained = [0]

        def link(ins):
            chained[0] += 1
            ins.then_inc(pool_chain, 1)
            eng.wait_ge(pool_chain, chained[0])

        def doubled(dst, src, k, rows, done=None):
            link(g.tensor_copy(dst[rows, :k], src[rows, :k]))
            ins = g.tensor_tensor(dst[rows, k:], src[rows, k:], src[rows, :S - k], ALU.add)
            if done is None:
                link(ins)
            else:
                ins.then_inc(done, 1)

        meet(eng, 1)
        g.memset(hs[:, 0, :], 0.0).then_inc(pool_chain, 1)
        chained[0] += 1
        eng.wait_ge(dt_a, 4)
        for ch in range(MT):
            if ch % 2:
                pair, before = task_place("xt%d" % (ch // 2))
                eng.wait_ge(d_free[pair], before + 1)
            else:
                eng.wait_ge(xdt_done, ch // 2 + 1)
            g.tensor_tensor(heads(xw[:, ch, :]), heads(xdt[:, ch, :]), per_head(8, ch),
                            ALU.mult).then_inc(xw_done, 1)
        every, upper = slice(0, P), slice(HEAD, P)

        def mean_and_rest(i):
            eng.wait_ge(pool_scaled, i + 1)
            link(g.tensor_tensor(pb[:, 0:16], pb[:, 0:16], table("pool_cnt")[:, 16 * i:16 * i + 16], ALU.mult))
            g.tensor_tensor(ht[:, 10 + i, :], pb[:, :], ht[:, 10 + i, :], ALU.subtract).then_inc(pooled, 1)
            eng.wait_ge(pooled, i + 1)

        doubled(pa, ht[:, 10, :], 1, every)
        doubled(pb, pa, 2, upper, pool_sum)
        eng.wait_ge(pool_sum, 1)
        for k in range(PAIRS):
            eng.wait_ge(mixh, k + 1)
            g.tensor_tensor(ml[:, 5 + k, :], sb[:, k, :], mh[:, 5 + k, :].bitcast(F32),
                            ALU.subtract).then_inc(sb_split, 1)
        mean_and_rest(0)
        doubled(pa, ht[:, 11, :], 1, every)
        doubled(pb, pa, 2, every)
        doubled(pa, pb, 4, every)
        doubled(pb, pa, 8, upper, pool_sum)
        mean_and_rest(1)
        for k in OUT_ORDER[:2]:
            lo(UNIT[("out", k)], eng=g)
        eng.wait_ge(ln_in, 32)
        for m in range(MT - 1):
            if m in GAIN_ON_VECTOR:
                eng.wait_ge(o_gain, GAIN_ON_VECTOR.index(m) + 1)
            else:
                eng.wait_ge(o_nrm, m + 1)
                link(g.tensor_tensor(on[:, m % 4, :], on[:, m % 4, :], lng[:, :], ALU.mult))
            g.tensor_tensor(on[:, m % 4, :], on[:, m % 4, :], lnb[:, :], ALU.add).then_inc(o_bias, 1)


def _tiles(w):
    n = w.shape[1] // P
    return w.reshape(KT, P, n, P).transpose(2, 1, 0, 3).reshape(n, P, D)


def _tables():
    i, j = np.arange(P)[:, None], np.arange(P)[None, :]
    one = lambda c: np.broadcast_to(c, (P, P)).astype(np.float32)
    cnt = np.ones((P, P), np.float32)
    for tile in range(2):
        for half in range(2):
            w = (2, 4, 8, 16)[2 * tile + half]
            cnt[HEAD * half:HEAD * half + HEAD, 16 * tile:16 * tile + 16] = w / np.minimum(np.arange(16) + 1, w)
    t = {"ident": one(i == j), "ones": one(i >= 0), "tri_le": one(i <= j), "mask_lt": one(i < j),
         "cap_lt": np.where(i < j, BIG, NEG), "cap_le": np.where(i <= j, BIG, NEG),
         "neg_ge": -one(i >= j), "neg_lt": -one(i < j),
         "rms_0": one(j < HEAD), "rms_1": one((i < HEAD) == (j < HEAD)), "rms_2": one(j >= HEAD),
         "from_first": one(i == 0), "from_last": one(i == P - 1), "pool_cnt": cnt}
    return np.concatenate([t[k].astype(np.float32) for k in TABLES], axis=1)


def _columns(v):
    return v.reshape(-1, P).T


def kernel(**inputs):
    import concourse.bacc as bacc
    from concourse.bass_utils import run_bass_kernel_spmd

    g = {k: np.asarray(v) for k, v in inputs.items()}
    w_in = g["w_in"][0]
    dt_half = np.pad(w_in[:, COL_DT:COL_Q], ((0, 0), (0, HEAD - SSD_HEADS)))
    dt_cols = np.concatenate([dt_half, dt_half], axis=1)
    cols = np.concatenate([dt_cols if t == "dt" else
                           w_in[:, IN_COLS[t[0]] + P * int(t[1]):IN_COLS[t[0]] + P * int(t[1]) + P]
                           for t in IN_TILES], axis=1)
    x = g["x"][0]
    order = [k for c in range(CHUNKS) for t in range(PER_CHUNK) for k in (PER_CHUNK * c + t,
                                                                        FF_TILES + PER_CHUNK * c + t)]
    up = _tiles(g["ffn_w_up"][0])[order]
    pool = np.zeros((P, 2, P), np.float32)
    for k in range(4):
        r = slice(HEAD * (k % 2), HEAD * (k % 2) + HEAD)
        pool[r, k // 2, r] = g["pool_w"][0, k]
    pool_inv = np.repeat(np.array([[1 / 2, 1 / 8], [1 / 4, 1 / 16]], np.float32), HEAD, axis=0)
    lanes = lambda v, n: np.broadcast_to(np.tile(v, n), (P, n * len(v)))
    cw = g["ssd_conv_w"][0].reshape(CONV, 7, P).transpose(2, 1, 0).reshape(P, 28)
    fw = g["ffn_conv_w"][0].reshape(FF_CONV, 2 * FF_TILES, P).transpose(2, 1, 0)[:, order].reshape(P, -1)
    fb = _columns(g["ffn_conv_b"][0])[:, order]
    params = {"conv_w": cw, "conv_b": _columns(g["ssd_conv_b"][0]), "pool_scale": _columns(g["pool_scale"][0]),
              "pool_inv": pool_inv, "ssd_d": _columns(np.repeat(g["ssd_d"][0], HEAD)),
              "norm_w": _columns(g["ssd_norm_w"][0]), "dt_bias": lanes(g["ssd_dt_bias"][0], MT),
              "a_log": lanes(g["ssd_a_log"][0], MT), "ln1_g": _columns(g["ln1_g"][0]),
              "ln1_b": _columns(g["ln1_b"][0]), "ff_w": fw, "ff_b": fb}
    arrays = {
        "u_x": x.T.reshape(KT, P, S), "u_in": _tiles(cols), "u_out": g["w_out"][0].reshape(KT, P, D),
        "u_p": g["p"][0, 0].T.reshape(PLE_TILES, P, S), "u_proj": g["ple_w_proj"][0].reshape(PLE_TILES, P, D),
        "u_gate": _tiles(g["ple_w_gate"][0]), "u_up": up, "u_down": g["ffn_w_down"][0].reshape(FF_TILES, P, D),
        "x_nat": x.reshape(MT, P, D), "tables": _tables(), "pool_w": pool.reshape(P, 2 * P),
        "params": np.concatenate([params[k] for k in PARAM_SIZES], axis=1),
        "ln2_g": g["ln2_g"][0], "ln2_b": g["ln2_b"][0],
    }
    arrays = {k: np.ascontiguousarray(v) for k, v in arrays.items()}
    nc = bacc.Bacc("TRN2", target_bir_lowering=False, num_devices=1, dynamic_dma_scratch_size=1024)
    aps = {k: nc.dram_tensor(k, v.shape, mybir.dt.from_np(v.dtype), kind="ExternalInput").ap()
           for k, v in arrays.items()}
    out = nc.dram_tensor("out", (S, D), F32, kind="ExternalOutput").ap()
    with ExitStack() as ctx:
        build(nc, ctx, aps, out)
    r = run_bass_kernel_spmd(nc, [arrays], core_ids=[0])
    return r.results[0]["out"].reshape(1, S, D)
```
